# Optimizing a Trainium2 kernel written in Bass

```python
import math
import jax, jax.numpy as jnp
from jax import lax
import numpy as np

D_MODEL = 1024
BATCH = 1
SEQ = 256
DEPTH = 2

DA_HEADS = 4
DA_HEAD_DIM = 64
DA_WIDTH = DA_HEADS * 2 * DA_HEAD_DIM
CONV_CH = 512
CONV_WIDTH = 31
SB_HEADS = 8
SB_HEAD_DIM = 64
SB_WIDTH = SB_HEADS * SB_HEAD_DIM
N_BRANCH = 3
Q_BLOCK = 128
ROPE_THETA = 10000.0
MAX_POS_OFFSET = 1024
EPS = 1e-6
NEG_INF = -1e30
IN_SIZES = (DA_WIDTH, DA_WIDTH, DA_WIDTH, 2 * CONV_CH, SB_WIDTH, SB_WIDTH, SB_WIDTH, N_BRANCH * D_MODEL)
IN_COLS = sum(IN_SIZES)
IN_SPLITS = tuple(int(v) for v in np.cumsum(IN_SIZES)[:-1])
N_EXPERTS = 64
TOP_K = 8
N_GROUPS = 8
TOPK_GROUPS = 4
EXPERT_FF = 256
SHARED_FF = 256
ROUTED_SCALE = 2.5
EXPERT_BLOCK = 128


def rms_norm(x, g):
    xf = x.astype(jnp.float32)
    y = xf * lax.rsqrt(jnp.mean(xf * xf, axis=-1, keepdims=True) + EPS)
    return (y * g.astype(jnp.float32)).astype(x.dtype)

def layer_norm(x, g, b):
    xf = x.astype(jnp.float32)
    mu = jnp.mean(xf, axis=-1, keepdims=True)
    var = jnp.mean(jnp.square(xf - mu), axis=-1, keepdims=True)
    y = (xf - mu) * lax.rsqrt(var + EPS) * g.astype(jnp.float32) + b.astype(jnp.float32)
    return y.astype(x.dtype)

def rope_tables(positions, dim):
    inv = ROPE_THETA ** (-jnp.arange(0, dim, 2, dtype=jnp.float32) / dim)
    ang = positions.astype(jnp.float32)[..., None] * inv
    return jnp.cos(ang)[:, :, None, :], jnp.sin(ang)[:, :, None, :]

def apply_rope(x, cos, sin):
    x1, x2 = jnp.split(x, 2, axis=-1)
    c = cos.astype(x.dtype)
    s = sin.astype(x.dtype)
    return jnp.concatenate([x1 * c - x2 * s, x2 * c + x1 * s], axis=-1)

def to_blocks(x):
    b, s = x.shape[:2]
    x = x.reshape((b, s // Q_BLOCK, Q_BLOCK) + x.shape[2:])
    return jnp.moveaxis(x, 1, 0)

def from_blocks(y):
    y = jnp.moveaxis(y, 0, 1)
    return y.reshape((y.shape[0], y.shape[1] * y.shape[2]) + y.shape[3:])

def diff_attention(q, k, v, lam, lambda_init, subln_g):
    S = k.shape[1]
    n_blocks = S // Q_BLOCK
    scale = DA_HEAD_DIM ** -0.5
    kpos = jnp.arange(S)

    def block(args):
        qb, start = args
        s = jnp.einsum('bqhmd,bkhmd->bhmqk', qb, k).astype(jnp.float32) * scale
        qpos = start + jnp.arange(Q_BLOCK)
        causal = kpos[None, :] <= qpos[:, None]
        p = jax.nn.softmax(jnp.where(causal, s, NEG_INF), axis=-1)
        a = p[:, :, 0] - lam * p[:, :, 1]
        return jnp.einsum('bhqk,bkhe->bqhe', a.astype(v.dtype), v)

    starts = jnp.arange(n_blocks, dtype=jnp.int32) * Q_BLOCK
    o = from_blocks(lax.map(block, (to_blocks(q), starts)))
    o = rms_norm(o, subln_g) * (1.0 - lambda_init)
    return o.reshape(o.shape[0], S, DA_WIDTH)

def stick_breaking(q, k, v):
    S = k.shape[1]
    n_blocks = S // Q_BLOCK
    scale = SB_HEAD_DIM ** -0.5
    kpos = jnp.arange(S)

    def block(args):
        qb, start = args
        z = jnp.einsum('bqhd,bkhd->bhqk', qb, k).astype(jnp.float32) * scale
        qpos = start + jnp.arange(Q_BLOCK)
        before = kpos[None, :] < qpos[:, None]
        log_beta = jax.nn.log_sigmoid(z)
        log_one_minus = jnp.where(before, jax.nn.log_sigmoid(-z), 0.0)
        key_axis = log_one_minus.ndim - 1
        suffix = lax.cumsum(log_one_minus, axis=key_axis, reverse=True) - log_one_minus
        a = jnp.where(before, jnp.exp(log_beta + suffix), 0.0)
        return jnp.einsum('bhqk,bkhd->bqhd', a.astype(v.dtype), v)

    starts = jnp.arange(n_blocks, dtype=jnp.int32) * Q_BLOCK
    o = from_blocks(lax.map(block, (to_blocks(q), starts)))
    return o.reshape(o.shape[0], S, SB_WIDTH)

def conformer_conv(u, w_dw, b_dw, ln_g, ln_b):
    a, g = jnp.split(u, 2, axis=-1)
    h = a * jax.nn.sigmoid(g)
    h = lax.conv_general_dilated(
        h, w_dw[:, None, :].astype(h.dtype), window_strides=(1,),
        padding=[(CONV_WIDTH - 1, 0)], dimension_numbers=('NWC', 'WIO', 'NWC'),
        feature_group_count=CONV_CH) + b_dw
    return jax.nn.silu(layer_norm(h, ln_g, ln_b))

def mixer(h, cos, sin, lambda_init, w_in, qn_g, kn_g, lam_q1, lam_k1, lam_q2, lam_k2, subln_g,
          w_proj_a, w_dw, b_dw, conv_ln_g, conv_ln_b, w_proj_b, b_proj_b, w_proj_c, w_out):
    B, S, _ = h.shape
    proj = h @ w_in
    qa, ka, va, ub, qc, kc, vc, gates = jnp.split(proj, IN_SPLITS, axis=-1)

    qa = apply_rope(rms_norm(qa.reshape(B, S, 2 * DA_HEADS, DA_HEAD_DIM), qn_g), cos, sin)
    ka = apply_rope(rms_norm(ka.reshape(B, S, 2 * DA_HEADS, DA_HEAD_DIM), kn_g), cos, sin)
    qa = qa.reshape(B, S, DA_HEADS, 2, DA_HEAD_DIM)
    ka = ka.reshape(B, S, DA_HEADS, 2, DA_HEAD_DIM)
    va = va.reshape(B, S, DA_HEADS, 2 * DA_HEAD_DIM)
    lam = (jnp.exp(jnp.sum(lam_q1.astype(jnp.float32) * lam_k1.astype(jnp.float32)))
           - jnp.exp(jnp.sum(lam_q2.astype(jnp.float32) * lam_k2.astype(jnp.float32)))
           + lambda_init)
    y_a = diff_attention(qa, ka, va, lam, lambda_init, subln_g) @ w_proj_a

    y_b = conformer_conv(ub, w_dw, b_dw, conv_ln_g, conv_ln_b) @ w_proj_b + b_proj_b

    y_c = stick_breaking(qc.reshape(B, S, SB_HEADS, SB_HEAD_DIM),
                         kc.reshape(B, S, SB_HEADS, SB_HEAD_DIM),
                         vc.reshape(B, S, SB_HEADS, SB_HEAD_DIM)) @ w_proj_c

    g = jax.nn.sigmoid(gates.reshape(B, S, N_BRANCH, D_MODEL))
    merged = g[:, :, 0] * y_a + g[:, :, 1] * y_b + g[:, :, 2] * y_c
    return merged @ w_out

def swiglu(x, w1, w3, w2):
    return (jax.nn.silu(x @ w1) * (x @ w3)) @ w2

def moe_ffn(u, w_router, b_router, w1, w3, w2, ws1, ws3, ws2):
    B, S, D = u.shape
    T = B * S
    xf = u.reshape(T, D)
    scores = jax.nn.sigmoid((xf @ w_router).astype(jnp.float32))
    biased = scores + b_router.astype(jnp.float32)
    grouped = biased.reshape(T, N_GROUPS, N_EXPERTS // N_GROUPS)
    group_score = jnp.sum(lax.top_k(grouped, 2)[0], axis=-1)
    _, top_groups = lax.top_k(group_score, TOPK_GROUPS)
    group_mask = jnp.any(top_groups[..., None] == jnp.arange(N_GROUPS), axis=-2)
    expert_mask = jnp.repeat(group_mask, N_EXPERTS // N_GROUPS, axis=-1)
    _, idx = lax.top_k(jnp.where(expert_mask, biased, NEG_INF), TOP_K)
    w = jnp.take_along_axis(scores, idx, axis=-1)
    w = w / (jnp.sum(w, axis=-1, keepdims=True) + 1e-20) * ROUTED_SCALE

    TK = T * TOP_K
    flat_e = idx.reshape(TK).astype(jnp.int32)
    flat_tok = jnp.arange(TK, dtype=jnp.int32) // TOP_K
    flat_w = w.reshape(TK)
    order = jnp.argsort(flat_e)
    se, st, sw = flat_e[order], flat_tok[order], flat_w[order]
    counts = jnp.bincount(flat_e, length=N_EXPERTS).astype(jnp.int32)
    starts = jnp.cumsum(counts) - counts
    padded = (counts + EXPERT_BLOCK - 1) // EXPERT_BLOCK * EXPERT_BLOCK
    pad_ends = jnp.cumsum(padded)
    pad_starts = pad_ends - padded
    dest = pad_starts[se] + (jnp.arange(TK, dtype=jnp.int32) - starts[se])
    n_blocks = (TK + N_EXPERTS * (EXPERT_BLOCK - 1) + EXPERT_BLOCK - 1) // EXPERT_BLOCK
    n_slots = n_blocks * EXPERT_BLOCK
    slot_tok = jnp.full((n_slots,), T, jnp.int32).at[dest].set(st)
    slot_w = jnp.zeros((n_slots,), jnp.float32).at[dest].set(sw)
    block_e = jnp.minimum(jnp.searchsorted(pad_ends, jnp.arange(n_blocks, dtype=jnp.int32) * EXPERT_BLOCK,
                                           side='right'), N_EXPERTS - 1).astype(jnp.int32)
    xpad = jnp.concatenate([xf, jnp.zeros((1, D), xf.dtype)], axis=0)

    def expert_block(args):
        toks, e, wts = args
        out = swiglu(xpad[toks], w1[e], w3[e], w2[e])
        return out * wts[:, None].astype(out.dtype)

    y = lax.map(expert_block, (slot_tok.reshape(n_blocks, EXPERT_BLOCK), block_e,
                               slot_w.reshape(n_blocks, EXPERT_BLOCK)))
    routed = jax.ops.segment_sum(y.reshape(n_slots, D), slot_tok, num_segments=T + 1)[:T]
    shared = swiglu(xf, ws1, ws3, ws2)
    return (routed + shared).reshape(B, S, D)

def first_inputs(seed: int = 0) -> dict:
    key = jax.random.key(seed)
    ks = iter(jax.random.split(key, 40))
    L = DEPTH

    def nrm(shape, s):
        return jax.random.normal(next(ks), shape, jnp.float32) * s

    def gain(shape):
        return 1.0 + nrm(shape, 0.02)

    D = D_MODEL
    x = nrm((BATCH, SEQ, D), 1.0)
    c = nrm((BATCH, D), 1.0)
    positions = (jnp.arange(SEQ, dtype=jnp.int32)[None, :]
                 + jax.random.randint(next(ks), (BATCH, 1), 0, MAX_POS_OFFSET, dtype=jnp.int32))
    return {
        "x": x, "c": c, "positions": positions,
        "w_mod": nrm((L, D, 6 * D), 0.3 * D ** -0.5),
        "b_mod": nrm((L, 6 * D), 0.02),
        "norm_mix_g": gain((L, D)),
        "norm_ffn_g": gain((L, D)),
        "w_in": nrm((L, D, IN_COLS), D ** -0.5),
        "qn_g": gain((L, DA_HEAD_DIM)),
        "kn_g": gain((L, DA_HEAD_DIM)),
        "lam_q1": nrm((L, DA_HEAD_DIM), 0.1),
        "lam_k1": nrm((L, DA_HEAD_DIM), 0.1),
        "lam_q2": nrm((L, DA_HEAD_DIM), 0.1),
        "lam_k2": nrm((L, DA_HEAD_DIM), 0.1),
        "subln_g": gain((L, 2 * DA_HEAD_DIM)),
        "w_proj_a": nrm((L, DA_WIDTH, D), DA_WIDTH ** -0.5),
        "w_dw": nrm((L, CONV_WIDTH, CONV_CH), CONV_WIDTH ** -0.5),
        "b_dw": nrm((L, CONV_CH), 0.02),
        "conv_ln_g": gain((L, CONV_CH)),
        "conv_ln_b": nrm((L, CONV_CH), 0.02),
        "w_proj_b": nrm((L, CONV_CH, D), CONV_CH ** -0.5),
        "b_proj_b": nrm((L, D), 0.02),
        "w_proj_c": nrm((L, SB_WIDTH, D), SB_WIDTH ** -0.5),
        "w_out": nrm((L, D, D), D ** -0.5),
        "w_router": nrm((L, D, N_EXPERTS), D ** -0.5),
        "b_router": nrm((L, N_EXPERTS), 0.01),
        "w1": nrm((L, N_EXPERTS, D, EXPERT_FF), D ** -0.5),
        "w3": nrm((L, N_EXPERTS, D, EXPERT_FF), D ** -0.5),
        "w2": nrm((L, N_EXPERTS, EXPERT_FF, D), EXPERT_FF ** -0.5),
        "ws1": nrm((L, D, SHARED_FF), D ** -0.5),
        "ws3": nrm((L, D, SHARED_FF), D ** -0.5),
        "ws2": nrm((L, SHARED_FF, D), SHARED_FF ** -0.5),
    }

def first_block(x, c, positions, w_mod, b_mod, norm_mix_g, norm_ffn_g, w_in, qn_g, kn_g,
              lam_q1, lam_k1, lam_q2, lam_k2, subln_g, w_proj_a, w_dw, b_dw, conv_ln_g, conv_ln_b,
              w_proj_b, b_proj_b, w_proj_c, w_out, w_router, b_router, w1, w3, w2, ws1, ws3, ws2):
    cos, sin = rope_tables(positions, DA_HEAD_DIM)
    c_act = jax.nn.silu(c)
    for l in range(DEPTH):
        lambda_init = 0.8 - 0.6 * math.exp(-0.3 * l)
        mod = c_act @ w_mod[l] + b_mod[l]
        sh_m, sc_m, g_m, sh_f, sc_f, g_f = [m[:, None, :] for m in jnp.split(mod, 6, axis=-1)]
        h = rms_norm(x, norm_mix_g[l]) * (1.0 + sc_m) + sh_m
        x = x + g_m * mixer(h, cos, sin, lambda_init, w_in[l], qn_g[l], kn_g[l], lam_q1[l], lam_k1[l],
                            lam_q2[l], lam_k2[l], subln_g[l], w_proj_a[l], w_dw[l], b_dw[l],
                            conv_ln_g[l], conv_ln_b[l], w_proj_b[l], b_proj_b[l], w_proj_c[l], w_out[l])
        h = rms_norm(x, norm_ffn_g[l]) * (1.0 + sc_f) + sh_f
        x = x + g_f * moe_ffn(h, w_router[l], b_router[l], w1[l], w3[l], w2[l], ws1[l], ws3[l], ws2[l])
    return x


CTX_LEN = 256
GRID_W = 64
N_EVEN = (DEPTH + 1) // 2
N_ODD = DEPTH // 2

M_HEADS = 4
M_HEAD_DIM = D_MODEL // M_HEADS
M_WIDTH = M_HEADS * M_HEAD_DIM
M_CHUNK = 128
M_CONV = 3
P_WINDOWS = (2, 4, 8, 16)
P_GROUPS = len(P_WINDOWS)
P_GROUP_DIM = D_MODEL // P_GROUPS
P_WIDTH = P_GROUPS * P_GROUP_DIM
AB_WIDTH = M_WIDTH + P_WIDTH
N_GATE = 4 * M_HEADS
GATE_OFF = 5 * M_WIDTH + 2 * P_WIDTH
AB_IN = GATE_OFF + N_GATE

A_HEADS = 16
A_KV_HEADS = 4
A_GROUP = A_HEADS // A_KV_HEADS
A_HEAD_DIM = D_MODEL // A_HEADS
A_WIDTH = A_HEADS * A_HEAD_DIM
A_KV_WIDTH = A_KV_HEADS * A_HEAD_DIM
A_WINDOW = 128
A_BLOCK = 128
A_BAND = A_BLOCK + 2 * A_WINDOW
ROPE_BASE = 10000.0
C_IN = 2 * A_WIDTH + 2 * A_KV_WIDTH


f32 = jnp.float32

def rmsnorm(x, g):
    xf = x.astype(f32)
    return (xf * lax.rsqrt(jnp.mean(xf * xf, -1, keepdims=True) + EPS) * g).astype(x.dtype)

def short_conv(u, w):
    pad = w.shape[0] // 2
    return lax.conv_general_dilated(u, w[:, None, :].astype(u.dtype), (1,), [(pad, pad)],
                                    dimension_numbers=('NWC', 'WIO', 'NWC'),
                                    feature_group_count=u.shape[-1])

def to_heads(a):
    bsz, n, _ = a.shape
    return a.reshape(bsz, n, M_HEADS, M_HEAD_DIM).transpose(0, 2, 1, 3).astype(f32)

def mlstm_chunkwise(q, k, v, log_i, log_f, state):
    bsz, nh, n, dh = q.shape
    nc = n // M_CHUNK

    def chunks(a):
        return jnp.moveaxis(a.reshape(a.shape[:2] + (nc, M_CHUNK) + a.shape[3:]), 2, 0)

    lower = jnp.tril(jnp.ones((M_CHUNK, M_CHUNK), bool))

    def step(carry, inp):
        c_mem, n_mem, m_prev = carry
        qc, kc, vc, lic, lfc = inp
        b = jnp.cumsum(lfc, axis=-1)
        dmat = b[..., :, None] - b[..., None, :] + lic[..., None, :]
        dmat = jnp.where(lower, dmat, -jnp.inf)
        inter = b + m_prev[..., None]
        m_t = jnp.maximum(inter, dmat.max(-1))
        w_inter = jnp.exp(inter - m_t)
        s = jnp.einsum('bhtd,bhsd->bhts', qc, kc) * jnp.exp(dmat - m_t[..., None])
        num = w_inter[..., None] * jnp.einsum('bhtd,bhde->bhte', qc, c_mem) + jnp.einsum('bhts,bhse->bhte', s, vc)
        den = w_inter * jnp.einsum('bhtd,bhd->bht', qc, n_mem) + s.sum(-1)
        h = num / jnp.maximum(jnp.abs(den), jnp.exp(-m_t))[..., None]
        b_last = b[..., -1]
        d_last = b_last[..., None] - b + lic
        m_new = jnp.maximum(b_last + m_prev, d_last.max(-1))
        w_s = jnp.exp(d_last - m_new[..., None])[..., None] * kc
        decay = jnp.exp(b_last + m_prev - m_new)
        c_new = decay[..., None, None] * c_mem + jnp.einsum('bhsd,bhse->bhde', w_s, vc)
        n_new = decay[..., None] * n_mem + w_s.sum(2)
        return (c_new, n_new, m_new), h

    state, hs = lax.scan(step, state, (chunks(q), chunks(k), chunks(v), chunks(log_i), chunks(log_f)))
    return jnp.moveaxis(hs, 0, 2).reshape(bsz, nh, n, dh), state

def mlstm_inputs(u, conv_w, b_gate):
    bsz, n, _ = u.shape
    qk = short_conv(u[..., :2 * M_WIDTH], conv_w)
    q = to_heads(qk[..., :M_WIDTH])
    k = to_heads(qk[..., M_WIDTH:]) * (M_HEAD_DIM ** -0.5)
    v = to_heads(u[..., 2 * M_WIDTH:3 * M_WIDTH])
    g = (u[..., GATE_OFF:] + b_gate).astype(f32).reshape(bsz, n, 4, M_HEADS)
    g = jnp.transpose(g, (2, 0, 3, 1))
    return q, k, v, (g[0], jax.nn.log_sigmoid(g[1]), g[2], jax.nn.log_sigmoid(g[3]))

def multiscale_pool(u, pool_w, pool_scale):
    bsz, n, _ = u.shape
    ug = u.astype(f32).reshape(bsz, n, P_GROUPS, P_GROUP_DIM)
    csum = jnp.concatenate([jnp.zeros_like(ug[:, :1]), jnp.cumsum(ug, axis=1)], axis=1)
    t = jnp.arange(n)[:, None]
    half = jnp.array(P_WINDOWS, jnp.int32)[None, :] // 2
    lo = jnp.clip(t - half, 0, n)
    hi = jnp.clip(t + half, 0, n)
    gi = jnp.arange(P_GROUPS)[None, :]
    win_sum = csum[:, hi, gi] - csum[:, lo, gi]
    mean = win_sum / (hi - lo).astype(f32)[None, :, :, None]
    mixed = jnp.einsum('bngc,gcd->bngd', mean - ug, pool_w.astype(f32))
    return mixed.reshape(bsz, n, P_WIDTH) * pool_scale

def head_rmsnorm(h, w):
    bsz, n, _ = h.shape
    hh = h.reshape(bsz, n, M_HEADS, M_HEAD_DIM)
    hh = hh * lax.rsqrt(jnp.mean(hh * hh, -1, keepdims=True) + EPS)
    return hh.reshape(bsz, n, M_WIDTH) * w

def mlstm_pool_output(u, h, mnorm_w, pool_w, pool_scale, w_out):
    bsz, n, _ = u.shape
    o_gate = jax.nn.sigmoid(u[..., 3 * M_WIDTH:4 * M_WIDTH].astype(f32))
    h = jnp.transpose(h, (0, 2, 1, 3)).reshape(bsz, n, M_WIDTH) * o_gate
    y_m = head_rmsnorm(h, mnorm_w) * jax.nn.silu(u[..., 4 * M_WIDTH:5 * M_WIDTH].astype(f32))
    p0 = 5 * M_WIDTH
    y_p = multiscale_pool(u[..., p0:p0 + P_WIDTH], pool_w, pool_scale) * jax.nn.silu(
        u[..., p0 + P_WIDTH:p0 + 2 * P_WIDTH].astype(f32))
    return jnp.concatenate([y_m, y_p], -1).astype(u.dtype) @ w_out

def mlstm_pool_mixer(hx, hc, w_in, b_gate, conv_w, mnorm_w, pool_w, pool_scale, w_out, need_ctx):
    ux, uc = hx @ w_in, hc @ w_in
    qx, kx, vx, (lif_x, lff_x, lib_x, lfb_x) = mlstm_inputs(ux, conv_w, b_gate)
    qc, kc, vc, (lif_c, lff_c, lib_c, lfb_c) = mlstm_inputs(uc, conv_w, b_gate)
    bsz = hx.shape[0]
    zero = (jnp.zeros((bsz, M_HEADS, M_HEAD_DIM, M_HEAD_DIM), f32),
            jnp.zeros((bsz, M_HEADS, M_HEAD_DIM), f32),
            jnp.zeros((bsz, M_HEADS), f32))
    rev = lambda a: jnp.flip(a, axis=2)
    hc_f, st_f = mlstm_chunkwise(qc, kc, vc, lif_c, lff_c, zero)
    hx_f, _ = mlstm_chunkwise(qx, kx, vx, lif_x, lff_x, st_f)
    hc_b, st_b = mlstm_chunkwise(rev(qc), rev(kc), rev(vc), rev(lib_c), rev(lfb_c), zero)
    hx_b, _ = mlstm_chunkwise(rev(qx), rev(kx), rev(vx), rev(lib_x), rev(lfb_x), st_b)
    yx = mlstm_pool_output(ux, hx_f + rev(hx_b), mnorm_w, pool_w, pool_scale, w_out)
    yc = mlstm_pool_output(uc, hc_f + rev(hc_b), mnorm_w, pool_w, pool_scale, w_out) if need_ctx else None
    return yx, yc

def axial_rope(n):
    rows = n // GRID_W
    row = jnp.repeat(jnp.arange(rows), GRID_W).astype(f32)
    col = jnp.tile(jnp.arange(GRID_W), rows).astype(f32)
    n_freq = A_HEAD_DIM // 4
    inv = ROPE_BASE ** (-jnp.arange(n_freq, dtype=f32) / n_freq)
    ang = jnp.concatenate([row[:, None] * inv, col[:, None] * inv], -1)
    return jnp.cos(ang), jnp.sin(ang)

def apply_rope_2(x, cos, sin):
    xf = x.astype(f32)
    x1, x2 = xf[..., 0::2], xf[..., 1::2]
    c, s = cos[None, :, None, :], sin[None, :, None, :]
    return jnp.stack([x1 * c - x2 * s, x1 * s + x2 * c], -1).reshape(x.shape).astype(x.dtype)

def gqa_scores(q, k):
    return jnp.einsum('bqkgd,bskd->bkgqs', q, k).astype(f32) * (A_HEAD_DIM ** -0.5)

def window_attention(q, k, v, k_ctx, v_ctx, sink):
    bsz, n = q.shape[:2]
    n_ctx = k_ctx.shape[1]
    pad = ((0, 0), (A_WINDOW, A_WINDOW), (0, 0), (0, 0))
    kp, vp = jnp.pad(k, pad), jnp.pad(v, pad)
    qg = q.reshape(bsz, n, A_KV_HEADS, A_GROUP, A_HEAD_DIM)
    sink_l = sink.reshape(1, A_KV_HEADS, A_GROUP, 1, 1).astype(f32)

    def block(bi):
        start = bi * A_BLOCK
        qb = lax.dynamic_slice_in_dim(qg, start, A_BLOCK, axis=1)
        kb = lax.dynamic_slice_in_dim(kp, start, A_BAND, axis=1)
        vb = lax.dynamic_slice_in_dim(vp, start, A_BAND, axis=1)
        qi = start + jnp.arange(A_BLOCK)
        kj = start - A_WINDOW + jnp.arange(A_BAND)
        ok = (jnp.abs(qi[:, None] - kj[None, :]) <= A_WINDOW) & (kj >= 0) & (kj < n)
        s_lat = jnp.where(ok, gqa_scores(qb, kb), -jnp.inf)
        s_ctx = gqa_scores(qb, k_ctx)
        sk = jnp.broadcast_to(sink_l, s_ctx.shape[:-1] + (1,))
        p = jax.nn.softmax(jnp.concatenate([s_lat, s_ctx, sk], -1), axis=-1)
        o = (jnp.einsum('bkgqs,bskd->bqkgd', p[..., :A_BAND].astype(v.dtype), vb)
             + jnp.einsum('bkgqs,bskd->bqkgd', p[..., A_BAND:A_BAND + n_ctx].astype(v.dtype), v_ctx))
        return o.reshape(bsz, A_BLOCK, A_WIDTH)

    out = lax.map(block, jnp.arange(n // A_BLOCK))
    return jnp.moveaxis(out, 0, 1).reshape(bsz, n, A_WIDTH)

def context_attention(q, k, v, sink):
    bsz, n = q.shape[:2]
    s = gqa_scores(q.reshape(bsz, n, A_KV_HEADS, A_GROUP, A_HEAD_DIM), k)
    sk = jnp.broadcast_to(sink.reshape(1, A_KV_HEADS, A_GROUP, 1, 1).astype(f32), s.shape[:-1] + (1,))
    p = jax.nn.softmax(jnp.concatenate([s, sk], -1), axis=-1)
    o = jnp.einsum('bkgqs,bskd->bqkgd', p[..., :n].astype(v.dtype), v)
    return o.reshape(bsz, n, A_WIDTH)

def split_attn(u):
    bsz, n, _ = u.shape
    q = u[..., :A_WIDTH].reshape(bsz, n, A_HEADS, A_HEAD_DIM)
    k = u[..., A_WIDTH:A_WIDTH + A_KV_WIDTH].reshape(bsz, n, A_KV_HEADS, A_HEAD_DIM)
    v = u[..., A_WIDTH + A_KV_WIDTH:A_WIDTH + 2 * A_KV_WIDTH].reshape(bsz, n, A_KV_HEADS, A_HEAD_DIM)
    z = u[..., A_WIDTH + 2 * A_KV_WIDTH:]
    return q, k, v, z

def window_attention_mixer(hx, hc, w_in, sink, w_out, need_ctx):
    qx, kx, vx, zx = split_attn(hx @ w_in)
    qc, kc, vc, zc = split_attn(hc @ w_in)
    cos, sin = axial_rope(hx.shape[1])
    qx, kx = apply_rope_2(qx, cos, sin), apply_rope_2(kx, cos, sin)
    ox = window_attention(qx, kx, vx, kc, vc, sink)
    yx = (ox * jax.nn.silu(zx)) @ w_out
    yc = (context_attention(qc, kc, vc, sink) * jax.nn.silu(zc)) @ w_out if need_ctx else None
    return yx, yc

def second_inputs(seed: int = 0) -> dict:
    key = jax.random.key(seed)
    ks = jax.random.split(key, 20)
    nrm = lambda k, shape, s: jax.random.normal(k, shape, f32) * s
    kg = jax.random.split(ks[9], 2)
    i_bias = nrm(kg[0], (N_EVEN, 2, M_HEADS), 0.1)
    f_bias = jnp.linspace(3.0, 6.0, M_HEADS, dtype=f32) + nrm(kg[1], (N_EVEN, 2, M_HEADS), 0.1)
    return {
        'x': nrm(ks[0], (BATCH, SEQ, D_MODEL), 1.0),
        'c': nrm(ks[1], (BATCH, D_MODEL), 1.0),
        'ctx': nrm(ks[2], (BATCH, CTX_LEN, D_MODEL), 1.0),
        'c_ctx': nrm(ks[3], (D_MODEL,), 1.0),
        'w_mod': nrm(ks[4], (DEPTH, D_MODEL, 3 * D_MODEL), 0.5 * D_MODEL ** -0.5),
        'b_mod': nrm(ks[5], (DEPTH, 3 * D_MODEL), 0.01),
        'g_pre': 1.0 + nrm(ks[6], (DEPTH, D_MODEL), 0.02),
        'g_post': 1.0 + nrm(ks[7], (DEPTH, D_MODEL), 0.02),
        'ab_w_in': nrm(ks[8], (N_EVEN, D_MODEL, AB_IN), D_MODEL ** -0.5),
        'ab_b_gate': jnp.stack([i_bias, f_bias], axis=2).reshape(N_EVEN, N_GATE),
        'ab_conv': nrm(ks[10], (N_EVEN, M_CONV, 2 * M_WIDTH), M_CONV ** -0.5),
        'ab_mnorm': 1.0 + nrm(ks[11], (N_EVEN, M_WIDTH), 0.02),
        'ab_pool_w': nrm(ks[12], (N_EVEN, P_GROUPS, P_GROUP_DIM, P_GROUP_DIM), P_GROUP_DIM ** -0.5),
        'ab_pool_scale': 1.0 + nrm(ks[13], (N_EVEN, P_WIDTH), 0.02),
        'ab_w_out': nrm(ks[14], (N_EVEN, AB_WIDTH, D_MODEL), AB_WIDTH ** -0.5),
        'c_w_in': nrm(ks[15], (N_ODD, D_MODEL, C_IN), D_MODEL ** -0.5),
        'c_sink': nrm(ks[16], (N_ODD, A_HEADS), 1.0),
        'c_w_out': nrm(ks[17], (N_ODD, A_WIDTH, D_MODEL), A_WIDTH ** -0.5),
    }

def second_block(x, c, ctx, c_ctx, w_mod, b_mod, g_pre, g_post, ab_w_in, ab_b_gate, ab_conv, ab_mnorm,
              ab_pool_w, ab_pool_scale, ab_w_out, c_w_in, c_sink, c_w_out):
    for l in range(DEPTH):
        j = l // 2
        last = l == DEPTH - 1
        shift, scale, gate = jnp.split(jax.nn.silu(c) @ w_mod[l] + b_mod[l], 3, axis=-1)
        shift_c, scale_c, gate_c = jnp.split(jax.nn.silu(c_ctx) @ w_mod[l] + b_mod[l], 3, axis=-1)
        hx = rmsnorm(x, g_pre[l]) * (1 + scale[:, None]) + shift[:, None]
        hc = rmsnorm(ctx, g_pre[l]) * (1 + scale_c) + shift_c
        if l % 2 == 0:
            yx, yc = mlstm_pool_mixer(hx, hc, ab_w_in[j], ab_b_gate[j], ab_conv[j], ab_mnorm[j],
                                      ab_pool_w[j], ab_pool_scale[j], ab_w_out[j], not last)
        else:
            yx, yc = window_attention_mixer(hx, hc, c_w_in[j], c_sink[j], c_w_out[j], not last)
        x = x + gate[:, None] * rmsnorm(yx, g_post[l])
        if not last:
            ctx = ctx + gate_c * rmsnorm(yc, g_post[l])
    return x


def setup_inputs(seed=0):
    out = dict(first_inputs(seed))
    for name, value in second_inputs(seed + 1).items():
        if name != "x":
            out[name + "_2"] = value
    return out


def reference(
    x, c, positions, w_mod, b_mod, norm_mix_g, norm_ffn_g, w_in, qn_g, kn_g, lam_q1, lam_k1,
    lam_q2, lam_k2, subln_g, w_proj_a, w_dw, b_dw, conv_ln_g, conv_ln_b, w_proj_b, b_proj_b,
    w_proj_c, w_out, w_router, b_router, w1, w3, w2, ws1, ws3, ws2, c_2, ctx_2, c_ctx_2,
    w_mod_2, b_mod_2, g_pre_2, g_post_2, ab_w_in_2, ab_b_gate_2, ab_conv_2, ab_mnorm_2,
    ab_pool_w_2, ab_pool_scale_2, ab_w_out_2, c_w_in_2, c_sink_2, c_w_out_2,
):
    x = first_block(
        x, c, positions, w_mod, b_mod, norm_mix_g, norm_ffn_g, w_in, qn_g, kn_g, lam_q1, lam_k1,
        lam_q2, lam_k2, subln_g, w_proj_a, w_dw, b_dw, conv_ln_g, conv_ln_b, w_proj_b, b_proj_b,
        w_proj_c, w_out, w_router, b_router, w1, w3, w2, ws1, ws3, ws2,
    )
    return second_block(
        x, c_2, ctx_2, c_ctx_2, w_mod_2, b_mod_2, g_pre_2, g_post_2, ab_w_in_2, ab_b_gate_2,
        ab_conv_2, ab_mnorm_2, ab_pool_w_2, ab_pool_scale_2, ab_w_out_2, c_w_in_2, c_sink_2,
        c_w_out_2,
    )


_drawn_inputs = setup_inputs


def setup_inputs(seed=0):
    import zlib

    import numpy as np

    out = dict(_drawn_inputs(seed))
    spreads = {}
    factors = {'norm_mix_g': 4.078,
     'qn_g': 5.141,
     'kn_g': 6.735,
     'lam_q1': 4.167,
     'lam_k1': 6.063,
     'subln_g': 4.576,
     'b_dw': 5.315,
     'conv_ln_g': 6.273,
     'conv_ln_b': 8.0,
     'b_proj_b': 5.381,
     'g_pre_2': 3.778,
     'g_post_2': 7.163,
     'ab_mnorm_2': 22.421,
     'ab_pool_scale_2': 8.0,
     'c_sink_2': 64.0,
     'lam_q2': 2.858}
    for name, (base, spread) in spreads.items():
        noise = np.random.default_rng([zlib.crc32(name.encode()), seed]).standard_normal(out[name].shape)
        drawn = base * np.exp(spread * noise) if base else spread * noise
        out[name] = __import__('jax').numpy.asarray(drawn.astype(out[name].dtype))
    for name, factor in factors.items():
        out[name] = (out[name] * factor).astype(out[name].dtype)
    return out
```

```python
import math
from contextlib import ExitStack

import numpy as np
import concourse.bass as bass
from concourse import mybir

F32 = mybir.dt.float32
I32 = mybir.dt.int32
ALU = mybir.AluOpType
ACT = mybir.ActivationFunctionType
AX = mybir.AxisListType.X

P = 128
D = 1024
NEG = -1.0e30
EPS = 1e-6
UNIT = 2048
UNITS = 11
LAYERS = 2
EXPERTS = 64

CONST_COLS = {}


def make_consts():
    p = np.arange(P)
    cols = []
    at = [0]

    def add(name, a):
        a = np.asarray(a, np.float32).reshape(P, -1)
        CONST_COLS[name] = (at[0], a.shape[1])
        at[0] += a.shape[1]
        cols.append(a)

    add("ident", np.eye(P))
    add("ones", np.ones((P, P)))
    add("blk64", (p[:, None] // 64) == (p[None, :] // 64))
    half = np.zeros((P, P))
    pair = np.zeros((P, P))
    for m in range(P):
        if m % 64 < 32:
            half[m + 32, m] = -1.0
        else:
            half[m - 32, m] = 1.0
        if m % 2 == 0:
            pair[m + 1, m] = -1.0
        else:
            pair[m - 1, m] = 1.0
    add("swap_half", half)
    add("swap_pair", pair)
    add("from_s", p[:, None] >= p[None, :])
    causal = np.where(p[None, :] <= p[:, None], 0.0, NEG)
    add("causal", np.concatenate([np.zeros((P, P)), causal], 1))
    before = np.where(p[:, None] < p[None, :], 0.0, NEG)
    add("before", np.concatenate([before, np.zeros((P, P)), before], 1))
    add("tri_f", np.where(p[:, None] <= p[None, :], 0.0, NEG))
    add("tri_b", np.where(p[:, None] >= p[None, :], 0.0, NEG))
    inv = (np.float32(10000.0) ** (-np.arange(0, 64, 2, dtype=np.float32) / np.float32(64))).astype(np.float32)
    add("inv", inv[p % 32][:, None])
    a8 = np.arange(8)
    add("tri8", np.broadcast_to((a8[None, :] < a8[:, None]).astype(np.float32).reshape(1, 64), (P, 64)))
    t = np.arange(256)
    band = []
    for i in range(2):
        q = i * P + p
        ok = np.abs(q[:, None] - t[None, :]) <= 128
        band.append(np.concatenate([np.zeros((P, 256)), np.where(ok, 0.0, NEG)], 1))
    add("band", np.concatenate(band, 1))
    rec = []
    for w in (2, 4, 8, 16):
        n = np.clip(t + w // 2, 0, 256) - np.clip(t - w // 2, 0, 256)
        rec.append((np.float32(1.0) / n.astype(np.float32)))
    add("recip", np.broadcast_to(np.concatenate(rec)[None, :], (P, 1024)))
    f = (np.float32(10000.0) ** (-np.arange(16, dtype=np.float32) / np.float32(16))).astype(np.float32)
    ang = np.concatenate([(t // 64).astype(np.float32)[:, None] * f, (t % 64).astype(np.float32)[:, None] * f], 1)
    i32 = (p % 64) // 2
    add("ax_cos", np.cos(ang.astype(np.float64))[:, i32].T)
    add("ax_sin", np.sin(ang.astype(np.float64))[:, i32].T)
    return np.ascontiguousarray(np.concatenate(cols, 1))


class Eng:

    def __init__(self, eng, sem, name):
        self.eng, self.sem, self.name, self.n, self.seen = eng, sem, name, 0, {}

    def wait(self, marks):
        for m in marks:
            if m is None:
                continue
            if isinstance(m, list):
                self.wait(m)
                continue
            sem, value, key = m
            if self.seen.get(key, 0) < value:
                self.eng.wait_ge(sem, value)
                self.seen[key] = value

    def __call__(self, fn, waits, *args, **kw):
        self.wait(waits)
        ins = fn(*args, **kw)
        return self.done(ins)

    def done(self, ins):
        self.n += 1
        ins.then_inc(self.sem, 1)
        return (self.sem, self.n, self.name)

    def last(self):
        return (self.sem, self.n, self.name)


class Buf:

    def __init__(self, t):
        self.t, self.w = t, []

    def free(self, *marks):
        self.w = list(marks)


class Rot:

    def __init__(self, tiles, bufs=None):
        self.bufs, self.i = bufs or [Buf(t) for t in tiles], 0

    def take(self):
        b = self.bufs[self.i % len(self.bufs)]
        self.i += 1
        return b


class Ring:

    def __init__(self, tile, sp, sems):
        self.tile, self.sp, self.sems = tile, sp, sems
        self.items, self.nxt, self.pos, self.live = [], 0, 0, []
        self.count = [0] * len(sems)
        self.where, self.gone = {}, {}

    def plan(self, key, units, parts):
        self.items.append((key, units, parts))

    def pump(self):
        while self.nxt < len(self.items):
            key, units, parts = self.items[self.nxt]
            pos = self.pos if self.pos + units <= UNITS else 0
            over = [x for x in self.live if x[0] < pos + units and pos < x[1]]
            if any(x[2] not in self.gone for x in over):
                return
            for x in over:
                self.sp.wait([self.gone[x[2]]])
            self.live = [x for x in self.live if x not in over]
            flat = self.tile[:, pos * UNIT:(pos + units) * UNIT]
            k = self.nxt % len(self.sems)
            for dst, src in parts:
                self.sp.eng.dma_start(dst(flat), src).then_inc(self.sems[k], 16)
                self.count[k] += 16
            self.where[key] = (flat, (self.sems[k], self.count[k], f"ring{k}"))
            self.live.append((pos, pos + units, key))
            self.pos = pos + units
            self.nxt += 1

    def get(self, key):
        return self.where[key]

    def release(self, key, *marks):
        self.gone[key] = list(marks)
        self.pump()


def build(nc, I, consts, out):
    ctx = ExitStack()
    with ctx:
        program(nc, ctx, I, consts, out)


def program(nc, ctx, I, consts, out):
    def sb(name, shape, dt=F32):
        return ctx.enter_context(nc.sbuf_tensor(name, shape, dt))

    def sem(name):
        return ctx.enter_context(nc.semaphore(name))

    T = Eng(nc.tensor, sem("s_pe"), "pe")
    A = Eng(nc.scalar, sem("s_act"), "act")
    V = Eng(nc.vector, sem("s_dve"), "dve")
    G = Eng(nc.gpsimd, sem("s_pool"), "pool")
    SP = Eng(nc.sync, sem("s_sp"), "sp")
    engines = [T, A, V, G]
    te, ac, ve, gp = nc.tensor, nc.scalar, nc.vector, nc.gpsimd

    def barrier():
        marks = [e.last() for e in engines if e.n]
        for e in engines:
            e.wait([m for m in marks if m[2] != e.name] + ([e.last()] if e.n and e is not T else []))

    NCOL = consts.shape[1]
    cst = sb("cst", [P, NCOL])
    ring_t = sb("ring", [P, UNITS * UNIT])
    xT = sb("xT", [P, 8, 512])
    hT = sb("hT", [P, 4096])
    par = sb("par", [P, 640])
    AR_COLS = 16330
    ar = sb("ar", [P, AR_COLS])
    banks = Rot([ctx.enter_context(nc.psum_tensor(f"ps{i}", [P, 512], F32)) for i in range(8)])
    ring = Ring(ring_t, SP, [sem(f"s_ring{i}") for i in range(UNITS + 1)])
    s_par = sem("s_par")
    s_x = sem("s_x")
    s_out = sem("s_out")

    top = [0]

    def reset():
        barrier()
        top[0] = 0

    def carve(*shape):
        n = int(np.prod(shape))
        a = ar[:, top[0]:top[0] + n]
        top[0] += n
        assert top[0] <= AR_COLS, top[0]
        if len(shape) == 2:
            a = a.rearrange("p (a b) -> p a b", a=shape[0])
        if len(shape) == 3:
            a = a.rearrange("p (a b c) -> p a b c", a=shape[0], b=shape[1])
        return a

    rows = carve(3, P)

    def C(name):
        o, n = CONST_COLS[name]
        return cst[:, o:o + n]

    ptop = [0]

    def pcol(n):
        a = par[:, ptop[0]:ptop[0] + n]
        ptop[0] += n
        assert ptop[0] <= 640
        return a

    def mm(o, pairs, waits, first=True, last=True, lax=False):
        T.wait(waits)
        n = len(pairs)
        for i, (l, r) in enumerate(pairs):
            ins = te.matmul(o, l, r, start=(first and i == 0), stop=(last and i == n - 1), skip_group_check=lax)
        return T.done(ins)

    def tr(o, i, ident, waits):
        T.wait(waits)
        return T.done(te.transpose(o, i, ident))

    ident, ones = C("ident"), C("ones")

    def plan_cols(key, w, c0, n, units):
        src = w.rearrange("(p k) n -> p k n", k=8)[:, :, c0:c0 + n]
        ring.plan(key, units, [(lambda f: f[:, 0:8 * n].rearrange("p (k n) -> p k n", k=8), src)])

    def plan_rows(key, w, k, units):
        src = w.rearrange("(c p) n -> p c n", c=k)
        ring.plan(key, units, [(lambda f: f[:, 0:k * src.shape[2]].rearrange("p (c n) -> p c n", c=k), src)])

    def plan_expert(key, w1, w3, w2):
        ring.plan(key, 3, [
            (lambda f: f[:, 0:UNIT], w1.rearrange("(p k) f -> p (k f)", k=8)),
            (lambda f: f[:, UNIT:2 * UNIT], w3.rearrange("(p k) f -> p (k f)", k=8)),
            (lambda f: f[:, 2 * UNIT:3 * UNIT], w2.rearrange("(p j) n -> p (j n)", j=2))])

    for l in range(LAYERS):
        for j in range(6):
            plan_cols(("mod", l, j), I["w_mod"][l], j * D, D, 4)
        for b in range(4):
            plan_cols(("in", l, b), I["w_in"][l], b * D, D, 4)
        for b, n in enumerate(("w_proj_a", "w_proj_b", "w_proj_c")):
            plan_cols(("in", l, 4 + b), I["w_in"][l], (4 + b) * D, D, 4)
            plan_rows(("proj", l, b), I[n][l], 4, 2)
        plan_cols(("out", l), I["w_out"][l], 0, D, 4)
        plan_cols(("router", l), I["w_router"][l], 0, EXPERTS, 1)
        for e in range(EXPERTS):
            plan_expert(("exp", l, e), I["w1"][l, e], I["w3"][l, e], I["w2"][l, e])
        plan_expert(("exp", l, EXPERTS), I["ws1"][l], I["ws3"][l], I["ws2"][l])
    abw = I["ab_w_in_2"][0]
    for j in range(3):
        plan_cols(("mod2", 0, j), I["w_mod_2"][0], j * D, D, 4)
    plan_rows(("poolw",), I["ab_pool_w_2"][0].rearrange("g c d -> (g c) d"), 8, 1)
    for g in range(4):
        plan_cols(("pin", g), abw, 5 * D + g * 256, 256, 1)
        plan_cols(("pgate", g), abw, 6 * D + g * 256, 256, 1)
    plan_cols(("gates",), abw, 7 * D, 16, 1)
    for h in range(4):
        for n, b in (("q", 0), ("k", 1), ("v", 2), ("o", 3), ("z", 4)):
            plan_cols((n, h), abw, b * D + h * 256, 256, 1)
    for j in range(2):
        plan_rows(("about", j), I["ab_w_out_2"][0, j * D:(j + 1) * D, :], 8, 4)
    for j in range(3):
        plan_cols(("mod2", 1, j), I["w_mod_2"][1], j * D, D, 4)
    cw = I["c_w_in_2"][0]
    plan_cols(("cq",), cw, 0, D, 4)
    plan_cols(("ckv",), cw, D, 512, 2)
    plan_cols(("cz",), cw, D + 512, D, 4)
    plan_rows(("cout",), I["c_w_out_2"][0], 8, 4)

    npar = [0]

    def pdma(dst, src, slow=False):
        nc.scalar.dma_start(dst, src, allow_slow_non_contiguous=slow).then_inc(s_par, 16)
        npar[0] += 16

    def dcols(v):
        return v.rearrange("(p k) -> p k", k=8)

    pdma(cst[:, :], consts)
    xin = hT[:, 0:2048].rearrange("p (i d) -> p i d", i=2)
    cin = hT[:, 2048:4096].rearrange("p (i d) -> p i d", i=2)
    nc.scalar.dma_start(xin, I["x"][0].rearrange("(i p) d -> p i d", p=P)).then_inc(s_x, 16)
    nc.scalar.dma_start(cin, I["ctx_2"][0].rearrange("(i p) d -> p i d", p=P)).then_inc(s_x, 16)
    craw = pcol(24).rearrange("p (c k) -> p c k", c=3)
    pdma(craw[:, 0, :], dcols(I["c"][0]))
    pdma(craw[:, 1, :], dcols(I["c_ctx_2"]))
    pdma(craw[:, 2, :], dcols(I["c_2"][0]))
    bmod = [pcol(48).rearrange("p (j k) -> p j k", j=6) for _ in range(LAYERS)]
    gmix, gffn, bprb = [], [], []
    lamrow = carve(8, 64)
    brow = [pcol(64) for _ in range(LAYERS)]
    for l in range(LAYERS):
        pdma(bmod[l], I["b_mod"][l].rearrange("(j p k) -> p j k", j=6, k=8))
        for lst, n in ((gmix, "norm_mix_g"), (gffn, "norm_ffn_g"), (bprb, "b_proj_b")):
            lst.append(pcol(8))
            pdma(lst[l], dcols(I[n][l]))
        for q, n in enumerate(("lam_q1", "lam_k1", "lam_q2", "lam_k2")):
            pdma(lamrow[:, 4 * l + q, :], I[n][l].partition_broadcast(P))
        pdma(brow[l], I["b_router"][l].partition_broadcast(P))
    bmod2, gpre, gpost = [], [], []
    for l in range(2):
        bmod2.append(pcol(24).rearrange("p (j k) -> p j k", j=3))
        pdma(bmod2[l], I["b_mod_2"][l].rearrange("(j p k) -> p j k", j=3, k=8))
        for lst, n in ((gpre, "g_pre_2"), (gpost, "g_post_2")):
            lst.append(pcol(8))
            pdma(lst[l], dcols(I[n][l]))
    bgate = pcol(4)
    pdma(bgate[0:4, :], I["ab_b_gate_2"][0].rearrange("(t h) -> h t", t=4), True)
    sink = pcol(16)
    pdma(sink, I["c_sink_2"][0].partition_broadcast(P))
    posi = carve(256)
    pdma(posi.bitcast(I32), I["positions"][0].partition_broadcast(P))
    for l in range(LAYERS):
        pdma(rows[0:124, l, :], I["w_dw"][l].rearrange("k (c q) -> (k c) q", q=P))
    misc = []
    at = [0]

    def prow(key, src):
        n = src.shape[0]
        pdma(rows[at[0]:at[0] + n, 2, 0:src.shape[1]], src)
        misc.append((key, at[0], n))
        at[0] += n

    prow("conv", I["ab_conv_2"][0].rearrange("j (c q) -> (j c) q", q=P))
    for l in range(LAYERS):
        for n in ("b_dw", "conv_ln_g", "conv_ln_b"):
            prow((n, l), I[n][l].rearrange("(c q) -> c q", q=P))
        prow(("subln_g", l), I["subln_g"][l].rearrange("(c q) -> c q", q=P))
    prow("mnorm", I["ab_mnorm_2"][0].rearrange("(c q) -> c q", q=P))
    prow("pscale", I["ab_pool_scale_2"][0].rearrange("(c q) -> c q", q=P))
    for l in range(LAYERS):
        for n in ("qn_g", "kn_g"):
            r0 = at[0]
            pdma(rows[r0:r0 + 1, 2, 64:128], I[n][l].rearrange("(c q) -> c q", c=1))
            prow((n, l), I[n][l].rearrange("(c q) -> c q", c=1))
    NR = at[0]
    m_par = (s_par, npar[0], "par")
    m_x = (s_x, 32, "x")
    ring.pump()

    wdw = [sb(f"wdw{l}", [P, 124]) for l in range(LAYERS)]
    pmisc = sb("pmisc", [P, P])
    m_prm = []
    for l in range(LAYERS):
        b = banks.take()
        m = tr(b.t[:, 0:124], rows[0:124, l, :], ident[0:124, 0:124], [m_par] + b.w)
        m = V(ve.tensor_copy, [m], wdw[l][:, :], b.t[:, 0:124])
        b.free(m)
        m_prm.append(m)
    b = banks.take()
    m = tr(b.t[:, 0:NR], rows[0:NR, 2, :], ident[0:NR, 0:NR], [m_par] + b.w)
    m = V(ve.tensor_copy, [m], pmisc[:, 0:NR], b.t[:, 0:NR])
    b.free(m)
    m_prm.append(m)
    PM = {k: pmisc[:, o:o + n] for k, o, n in misc}
    for e in (A, V, G, T):
        e.wait([m_par] + m_prm)

    for src, c0 in ((cin, 0), (xin, 256)):
        for i in range(2):
            for k0 in (0, 4):
                b = banks.take()
                T.wait([m_x] + b.w)
                for k in range(k0, k0 + 4):
                    ins = te.transpose(b.t[:, (k - k0) * P:(k - k0 + 1) * P], src[:, i, k::8], ident)
                m = T.done(ins)
                m = A(ac.activation, [m], xT[:, k0:k0 + 4, c0 + i * P:c0 + (i + 1) * P],
                      b.t[:, :].rearrange("p (k t) -> p k t", k=4), ACT.Copy)
                b.free(m)
    cosT = sb("cosT", [P, 256])
    sinT = sb("sinT", [P, 256])
    posf, ang, rn, t0 = carve(256), carve(256), carve(256), carve(256)
    TWO_PI = 2.0 * math.pi
    C1 = 6.28125
    C2 = 0.00193500518798828125
    C3 = TWO_PI - C1 - C2
    MAGIC = 1.5 * 2.0 ** 23
    HALF = 3.1415925
    m = V(ve.tensor_copy, [], posf, posi.bitcast(I32))
    m = V(ve.tensor_scalar, [m], ang, posf, C("inv"), None, ALU.mult)
    m = V(ve.tensor_scalar, [m], rn, ang, 1.0 / TWO_PI, MAGIC, ALU.mult, ALU.add)
    m = V(ve.tensor_scalar, [m], rn, rn, MAGIC, None, ALU.subtract)
    for cc in (C1, C2, C3):
        m = V(ve.scalar_tensor_tensor, [m], ang, rn, -cc, ang, ALU.mult, ALU.add)
    m = V(ve.tensor_scalar, [m], ang, ang, HALF, -HALF, ALU.min, ALU.max)
    ms = A(ac.activation, [m], sinT[:, :], ang, ACT.Sin)
    m = V(ve.tensor_scalar, [m], rn, ang, math.pi / 2, None, ALU.add)
    m = V(ve.tensor_scalar, [m], t0, rn, math.pi, -TWO_PI, ALU.is_gt, ALU.mult)
    m = V(ve.tensor_tensor, [m], rn, rn, t0, ALU.add)
    m = V(ve.tensor_scalar, [m], rn, rn, HALF, -HALF, ALU.min, ALU.max)
    A(ac.activation, [m], cosT[:, :], rn, ACT.Sin)
    neglam = [pcol(1) for _ in range(LAYERS)]
    lams = pcol(4)
    for l in range(LAYERS):
        for q in range(2):
            m = V(ve.tensor_tensor, [], lamrow[:, 4 * l + 2 * q, :], lamrow[:, 4 * l + 2 * q, :],
                  lamrow[:, 4 * l + 2 * q + 1, :], ALU.mult)
            m = V(ve.tensor_reduce, [m], lams[:, 2 * l + q:2 * l + q + 1], lamrow[:, 4 * l + 2 * q, :], AX, ALU.add)
    lexp = pcol(4)
    m = A(ac.activation, [m], lexp, lams, ACT.Exp)
    lam_init = [0.8 - 0.6 * math.exp(-0.3 * l) for l in range(LAYERS)]
    sublnS = [pcol(1) for _ in range(LAYERS)]
    for l in range(LAYERS):
        m2 = V(ve.tensor_tensor, [m], neglam[l], lexp[:, 2 * l + 1:2 * l + 2], lexp[:, 2 * l:2 * l + 1], ALU.subtract)
        V(ve.tensor_scalar, [m2], neglam[l], neglam[l], -lam_init[l], None, ALU.add)
        V(ve.tensor_scalar, [], sublnS[l], PM[("subln_g", l)], 1.0 - lam_init[l], None, ALU.mult)
    cact = pcol(24).rearrange("p (c k) -> p c k", c=3)
    A(ac.activation, [], cact, craw, ACT.Silu)

    def rstd(src_ps, dst, n, waits):
        m = V(ve.tensor_scalar, waits, dst, src_ps, 1.0 / n, EPS, ALU.mult, ALU.add)
        m = V(ve.reciprocal, [m], dst, dst)
        return A(ac.activation, [m], dst, dst, ACT.Sqrt)

    def modulation(key, bias, ncol, cvec, dst):
        for j in range(bias.shape[1]):
            flat, ml = ring.get(key + (j,))
            w = flat.rearrange("p (k n) -> p k n", k=8)
            b = banks.take()
            for k in range(8):
                m = mm(b.t[:, k * ncol:(k + 1) * ncol], [(w[:, kk, k::8], cvec[kk]) for kk in range(8)],
                       [ml] + b.w)
            ring.release(key + (j,), m)
            for c in range(ncol):
                o = dst[:, c, j, :]
                src = b.t[:, 0:8 * ncol].rearrange("p (k c) -> p k c", c=ncol)[:, :, c]
                m2 = V(ve.tensor_tensor, [m], o, src, bias[:, j, :], ALU.add)
            b.free(m2)
        return m2

    def norm_modulate(cols, h, scale, shift, sq_t, r_t):
        c0, c1 = cols
        n = c1 - c0
        ms = A(ac.activation, [], sq_t, xT[:, :, c0:c1], ACT.Square)
        b = banks.take()
        m = mm(b.t[:, 0:n], [(ones, sq_t[:, k, :]) for k in range(8)], [ms] + b.w)
        mr = rstd(b.t[:, 0:n], r_t, D, [m])
        b.free(mr)
        for k in range(8):
            for s in range(n // 256):
                seg = slice(s * 256, (s + 1) * 256)
                m = V(ve.scalar_tensor_tensor, [mr], h[:, k, seg], xT[:, k, c0 + s * 256:c0 + (s + 1) * 256],
                      scale[s][:, k:k + 1], r_t[:, seg], ALU.mult, ALU.mult)
                mh = A(ac.activation, [m], h[:, k, seg], h[:, k, seg], ACT.Identity, bias=shift[s][:, k:k + 1])
        return mh

    XC = (256, 512)
    for l in range(LAYERS):
        first_layer(nc, locals(), l)
    second_block(nc, locals())


def first_layer(nc, S, l):
    V, A, T, G = S["V"], S["A"], S["T"], S["G"]
    te, ac, ve, gp = nc.tensor, nc.scalar, nc.vector, nc.gpsimd
    mm, tr, C, carve, reset, banks, ring, rstd = (S["mm"], S["tr"], S["C"], S["carve"], S["reset"], S["banks"],
                                                  S["ring"], S["rstd"])
    I, PM, hT, xT, ident, ones = S["I"], S["PM"], S["hT"], S["xT"], S["ident"], S["ones"]
    reset()
    h = hT[:, 0:2048].rearrange("p (k t) -> p k t", k=8)
    merged = hT[:, 2048:4096].rearrange("p (k t) -> p k t", k=8)
    mod = carve(1, 6, 8)
    m_mod = S["modulation"](("mod", l), S["bmod"][l], 1, [S["cact"][:, 0, kk:kk + 1] for kk in range(8)], mod)
    amix, affn = carve(8), carve(8)
    m1 = V(ve.scalar_tensor_tensor, [m_mod], amix, mod[:, 0, 1, :], 1.0, S["gmix"][l], ALU.add, ALU.mult)
    m2 = V(ve.scalar_tensor_tensor, [m_mod], affn, mod[:, 0, 4, :], 1.0, S["gffn"][l], ALU.add, ALU.mult)
    A.wait([m1, m2])
    V.wait([m1, m2])
    keep = S["top"][0]
    sq_t, r_t = carve(8, 256), carve(256)
    m_h = S["norm_modulate"](S["XC"], h, [amix], [mod[:, 0, 0, :]], sq_t, r_t)
    S["barrier"]()
    S["top"][0] = keep

    qR, kR = carve(4, 256), carve(4, 256)
    va, vc = carve(2, 512), carve(2, 512)
    hpad = carve(4, 286)
    acc = carve(4, 256)
    qc, kc = merged[:, 0:4, :], merged[:, 4:8, :]
    keep = S["top"][0]
    r_a, r_sq, r_t1, r_r = [Rot([carve(2, 256) for _ in range(2)]) for _ in range(4)]
    cosB = S["cosT"][:, :].unsqueeze(1).to_broadcast([P, 2, 256])
    sinB = S["sinT"][:, :].unsqueeze(1).to_broadcast([P, 2, 256])
    m_zero = G(gp.memset, [], hpad[:, :, 0:30], 0.0)

    flat, ml = ring.get(("in", l, 0))
    w = flat.rearrange("p (k n) -> p k n", k=8)
    m_rope = None
    for half, (dst, gname) in enumerate(((qR, "qn_g"), (kR, "kn_g"))):
        g = PM[(gname, l)]
        for pr in range(2):
            b = banks.take()
            for c in range(2):
                c0 = half * 512 + (2 * pr + c) * P
                m = mm(b.t[:, c * 256:(c + 1) * 256], [(w[:, kk, c0:c0 + P], h[:, kk, :]) for kk in range(8)],
                       [ml, m_h] + b.w)
            if half == 1 and pr == 1:
                ring.release(("in", l, 0), m)
            ps = b.t[:, :].rearrange("p (c t) -> p c t", c=2)
            qa, sq, t1, rr = r_a.take(), r_sq.take(), r_t1.take(), r_r.take()
            ma = A(ac.activation, [m] + qa.w, qa.t, ps, ACT.Copy, scale=g)
            mq = A(ac.activation, [m] + sq.w, sq.t, ps, ACT.Square)
            b.free(ma, mq)
            bs, bw = banks.take(), banks.take()
            m_ss = mm(bs.t[:, :], [(C("blk64"), sq.t)], [mq] + bs.w)
            sq.free(m_ss)
            m_sw = mm(bw.t[:, :], [(C("swap_half"), qa.t)], [ma] + bw.w)
            pss = bs.t[:, :].rearrange("p (c t) -> p c t", c=2)
            psw = bw.t[:, :].rearrange("p (c t) -> p c t", c=2)
            V.wait(rr.w)
            mr = rstd(pss, rr.t, 64, [m_ss])
            bs.free(mr)
            mt = V(ve.tensor_tensor, [m_sw] + t1.w, t1.t, psw, sinB, ALU.mult)
            bw.free(mt)
            mb = G(gp.tensor_tensor, [ma, m_sw], qa.t, qa.t, cosB, ALU.mult)
            mt = V(ve.tensor_tensor, [mt, mb], t1.t, t1.t, qa.t, ALU.add)
            qa.free(mt)
            m_rope = V(ve.tensor_tensor, [mt, mr], dst[:, 2 * pr:2 * pr + 2, :], t1.t, rr.t, ALU.mult)
            t1.free(m_rope)
            rr.free(m_rope)

    flat, ml = ring.get(("in", l, 1))
    w = flat.rearrange("p (k n) -> p k n", k=8)
    for i in range(2):
        b = banks.take()
        m = mm(b.t[:, :], [(h[:, kk, i * P:(i + 1) * P], w[:, kk, 0:512]) for kk in range(8)], [ml] + b.w)
        m_va = A(ac.activation, [m], va[:, i, :], b.t[:, :], ACT.Copy)
        b.free(m_va)
    for pr in range(2):
        b = banks.take()
        for c in range(2):
            c0 = 512 + (2 * pr + c) * P
            m = mm(b.t[:, c * 256:(c + 1) * 256], [(w[:, kk, c0:c0 + P], h[:, kk, :]) for kk in range(8)], b.w)
        m_ua = A(ac.activation, [m], hpad[:, 2 * pr:2 * pr + 2, 30:286],
                 b.t[:, :].rearrange("p (c t) -> p c t", c=2), ACT.Copy)
        b.free(m_ua)
    ring.release(("in", l, 1), m)
    flat, ml = ring.get(("in", l, 2))
    w = flat.rearrange("p (k n) -> p k n", k=8)
    m_glu = []
    for pr in range(2):
        b = banks.take()
        for c in range(2):
            c0 = (2 * pr + c) * P
            m = mm(b.t[:, c * 256:(c + 1) * 256], [(w[:, kk, c0:c0 + P], h[:, kk, :]) for kk in range(8)],
                   [ml] + b.w)
        sg = r_sq.take()
        ms = A(ac.activation, [m] + sg.w, sg.t, b.t[:, :].rearrange("p (c t) -> p c t", c=2), ACT.Sigmoid)
        b.free(ms)
        hp = hpad[:, 2 * pr:2 * pr + 2, 30:286]
        mg = V(ve.tensor_tensor, [ms, m_ua], hp, hp, sg.t, ALU.mult)
        sg.free(mg)
        m_glu.append(mg)
    for dst, blk, off in ((qc, 2, 512), (kc, 3, 0)):
        if blk == 3:
            ring.release(("in", l, 2), m)
            flat, ml = ring.get(("in", l, 3))
            w = flat.rearrange("p (k n) -> p k n", k=8)
        for pr in range(2):
            b = banks.take()
            for c in range(2):
                c0 = off + (2 * pr + c) * P
                m = mm(b.t[:, c * 256:(c + 1) * 256], [(w[:, kk, c0:c0 + P], h[:, kk, :]) for kk in range(8)],
                       [ml] + b.w)
            m_qk = A(ac.activation, [m], dst[:, 2 * pr:2 * pr + 2, :],
                     b.t[:, :].rearrange("p (c t) -> p c t", c=2), ACT.Copy)
            b.free(m_qk)
    for i in range(2):
        b = banks.take()
        m = mm(b.t[:, :], [(h[:, kk, i * P:(i + 1) * P], w[:, kk, 512:1024]) for kk in range(8)], [ml] + b.w)
        m_vc = A(ac.activation, [m], vc[:, i, :], b.t[:, :], ACT.Copy)
        b.free(m_vc)
    ring.release(("in", l, 3), m)

    wd = S["wdw"][l]
    mc = [None] * 4
    V.wait([m_zero] + m_glu)
    conv_steps = []
    for k in range(31):
        for c in range(4):
            conv_steps.append((k, c))

    def conv(n):
        for _ in range(min(n, len(conv_steps))):
            k, c = conv_steps.pop(0)
            tap = wd[:, k * 4 + c:k * 4 + c + 1]
            if k == 0:
                mc[c] = V(ve.tensor_scalar, [], acc[:, c, :], hpad[:, c, 0:256], tap, PM[("b_dw", l)][:, c:c + 1],
                          ALU.mult, ALU.add)
            else:
                mc[c] = V(ve.scalar_tensor_tensor, [mc[c]], acc[:, c, :], hpad[:, c, k:k + 256], tap, acc[:, c, :],
                          ALU.mult, ALU.add)

    S["barrier"]()
    S["top"][0] = keep
    oa, oc = carve(4, 256), carve(4, 256)
    f_s = Rot([carve(2, 256) for _ in range(2)])
    f_a = Rot([carve(1, 256) for _ in range(2)])
    f_st = Rot([carve(8) for _ in range(4)])
    f_at = Rot([carve(3, P) for _ in range(2)])
    f_o = Rot([carve(256) for _ in range(2)])
    f_r = Rot([carve(256) for _ in range(2)])
    mask = C("causal")

    def diff_head(hd):
        at = f_at.take()
        for i in range(2):
            K = (i + 1) * P
            s, st = f_s.take(), f_st.take()
            for mp in range(2):
                b = banks.take()
                m = mm(b.t[:, 0:K],
                       [(qR[mp * 64:mp * 64 + 64, hd, i * P:(i + 1) * P], kR[mp * 64:mp * 64 + 64, hd, 0:K])], b.w)
                m = V(ve.scalar_tensor_tensor, [m] + s.w, s.t[:, mp, 0:K], b.t[:, 0:K], 0.125, mask[:, 256 - K:256],
                      ALU.mult, ALU.add)
                b.free(m)
            m = V(ve.tensor_reduce, [m] + st.w, st.t[:, 0:2], s.t[:, :, 0:K], AX, ALU.max)
            m = V(ve.tensor_scalar, [m], st.t[:, 2:4], st.t[:, 0:2], -1.0, None, ALU.mult)
            for mp in range(2):
                me = A(ac.activation, [m], s.t[:, mp, 0:K], s.t[:, mp, 0:K], ACT.Exp, bias=st.t[:, 2 + mp:3 + mp],
                       accum_out=st.t[:, 4 + mp:5 + mp])
            m = V(ve.reciprocal, [me], st.t[:, 6:8], st.t[:, 4:6])
            a = f_a.take()
            m2 = V(ve.tensor_scalar, [m] + a.w, a.t[:, 0, 0:K], s.t[:, 0, 0:K], st.t[:, 6:7], None, ALU.mult)
            m1 = V(ve.tensor_tensor, [m], st.t[:, 7:8], st.t[:, 7:8], S["neglam"][l], ALU.mult)
            m = V(ve.scalar_tensor_tensor, [m1, m2], a.t[:, 0, 0:K], s.t[:, 1, 0:K], st.t[:, 7:8], a.t[:, 0, 0:K],
                  ALU.mult, ALU.add)
            s.free(m)
            st.free(m)
            b = banks.take()
            for kb in range(i + 1):
                mt = tr(b.t[:, kb * P:(kb + 1) * P], a.t[:, 0, kb * P:(kb + 1) * P], ident, [m] + b.w)
            a.free(mt)
            m_at = A(ac.activation, [mt] + at.w, at.t[:, i:2 * i + 1, :],
                     b.t[:, 0:K].rearrange("p (k t) -> p k t", k=i + 1), ACT.Copy)
            b.free(m_at)
        b = banks.take()
        vv = [va[:, kb, hd * P:(hd + 1) * P] for kb in range(2)]
        mm(b.t[:, 0:P], [(vv[0], at.t[:, 0, :])], [m_at] + b.w)
        m = mm(b.t[:, P:256], [(vv[0], at.t[:, 1, :]), (vv[1], at.t[:, 2, :])], [])
        at.free(m)
        o, r = f_o.take(), f_r.take()
        msq = A(ac.activation, [m] + o.w, o.t, b.t[:, 0:256], ACT.Square)
        b2 = banks.take()
        m2 = mm(b2.t[:, 0:256], [(ones, o.t)], [msq] + b2.w)
        o.free(m2)
        V.wait(r.w)
        mr = rstd(b2.t[:, 0:256], r.t, P, [m2])
        b2.free(mr)
        m = V(ve.scalar_tensor_tensor, [mr, m], oa[:, hd, :], b.t[:, 0:256], S["sublnS"][l], r.t, ALU.mult, ALU.mult)
        r.free(m)
        b.free(m, msq)
        return m

    f_z = Rot([carve(384) for _ in range(2)])
    f_e = Rot([carve(384) for _ in range(2)])
    bef = C("before")

    def stick_pair(c):
        bo = banks.take()
        wo = list(bo.w)
        for u in range(2):
            hd, base = 2 * c + u, u * 64
            b = banks.take()
            kk, qq = kc[base:base + 64, c, :], qc[base:base + 64, c, :]
            mm(b.t[:, 0:256], [(kk[:, 0:P], qq)], b.w)
            m = mm(b.t[:, 256:384], [(kk[:, P:256], qq[:, P:256])], [])
            z, e = f_z.take(), f_e.take()
            mz = V(ve.scalar_tensor_tensor, [m] + z.w, z.t, b.t[:, 0:384], 0.125, bef, ALU.mult, ALU.add)
            b.free(mz)
            m = A(ac.activation, [mz] + e.w, e.t, z.t, ACT.Abs)
            m = A(ac.activation, [m], e.t, e.t, ACT.Exp, scale=-1.0)
            m = A(ac.activation, [m], e.t, e.t, ACT.Ln, bias=ones[:, 0:1])
            m = V(ve.scalar_tensor_tensor, [m], e.t, z.t, 0.0, e.t, ALU.max, ALU.add)
            b = banks.take()
            mm(b.t[:, 256:384], [(C("from_s"), e.t[:, 256:384])], [m] + b.w)
            mm(b.t[:, 0:P], [(C("from_s"), e.t[:, 0:P])], [])
            ms = mm(b.t[:, P:256], [(C("from_s"), e.t[:, P:256]), (ones, e.t[:, 256:384])], [])
            m = V(ve.tensor_tensor, [ms], z.t, z.t, b.t[:, 0:384], ALU.subtract)
            b.free(m)
            m = A(ac.activation, [m], e.t, z.t, ACT.Exp)
            z.free(m)
            o = bo.t[base:base + 64, :]
            vv = [vc[:, j, hd * 64:(hd + 1) * 64] for j in range(2)]
            mm(o[:, 0:P], [(vv[0], e.t[:, 0:P])], [m] + wo)
            m = mm(o[:, P:256], [(vv[0], e.t[:, P:256]), (vv[1], e.t[:, 256:384])], [])
            e.free(m)
        m = A(ac.activation, [m], oc[:, c, :], bo.t[:, 0:256], ACT.Copy)
        bo.free(m)
        return m

    for c in range(4):
        m_oa = diff_head(c)
        conv(16)
        m_oc = stick_pair(c)
        conv(15)
    conv(999)
    lnm, lnr = f_o.take(), f_r.take()
    b = banks.take()
    m = mm(b.t[:, 0:256], [(ones, acc[:, c, :]) for c in range(4)], mc + b.w)
    m = A(ac.activation, [m] + lnm.w, lnm.t, b.t[:, 0:256], ACT.Copy, scale=1.0 / 512)
    b.free(m)
    m = V(ve.tensor_tensor, [m], acc, acc, lnm.t.unsqueeze(1).to_broadcast([P, 4, 256]), ALU.subtract)
    lnm.free(m)
    ob = hpad[:, :, 0:256]
    msq = A(ac.activation, [m], ob, acc, ACT.Square)
    b = banks.take()
    m2 = mm(b.t[:, 0:256], [(ones, ob[:, c, :]) for c in range(4)], [msq] + b.w)
    V.wait(lnr.w)
    mr = rstd(b.t[:, 0:256], lnr.t, 512, [m2])
    b.free(mr)
    m = V(ve.tensor_tensor, [mr], acc, acc, lnr.t.unsqueeze(1).to_broadcast([P, 4, 256]), ALU.mult)
    lnr.free(m)
    A.wait([m2])
    for c in range(4):
        m_ob = A(ac.activation, [m], ob[:, c, :], acc[:, c, :], ACT.Silu, bias=PM[("conv_ln_b", l)][:, c:c + 1],
                 scale=PM[("conv_ln_g", l)][:, c:c + 1])

    S["barrier"]()
    S["top"][0] = 64
    f_g = Rot([carve(256) for _ in range(3)])
    f_y = Rot([carve(256) for _ in range(3)])
    m_mrg = [None] * 8
    for br, (o, mo) in enumerate(((oa, m_oa), (ob, m_ob), (oc, m_oc))):
        flat, ml = ring.get(("in", l, 4 + br))
        w = flat.rearrange("p (k n) -> p k n", k=8)
        pflat, mp = ring.get(("proj", l, br))
        pw = pflat.rearrange("p (c n) -> p c n", c=4)
        for k in range(8):
            b = banks.take()
            mm(b.t[:, 0:256], [(w[:, kk, k::8], h[:, kk, :]) for kk in range(8)], [ml] + b.w)
            my = mm(b.t[:, 256:512], [(pw[:, c, k::8], o[:, c, :]) for c in range(4)], [mp, mo])
            sg = f_g.take()
            ms = A(ac.activation, [my] + sg.w, sg.t, b.t[:, 0:256], ACT.Sigmoid)
            if br == 0:
                m = V(ve.tensor_tensor, [ms, my], merged[:, k, :], sg.t, b.t[:, 256:512], ALU.mult)
                m_mrg[k] = m
            else:
                y = f_y.take()
                if br == 1:
                    m = V(ve.scalar_tensor_tensor, [ms, my] + y.w, y.t, b.t[:, 256:512], S["bprb"][l][:, k:k + 1],
                          sg.t, ALU.add, ALU.mult)
                else:
                    m = V(ve.tensor_tensor, [ms, my] + y.w, y.t, sg.t, b.t[:, 256:512], ALU.mult)
                m_mrg[k] = G(gp.tensor_tensor, [m, m_mrg[k]], merged[:, k, :], merged[:, k, :], y.t, ALU.add)
                y.free(m_mrg[k])
            sg.free(m)
            b.free(m, ms)
        ring.release(("in", l, 4 + br), my)
        ring.release(("proj", l, br), my)
    flat, ml = ring.get(("out", l))
    w = flat.rearrange("p (k n) -> p k n", k=8)
    for k in range(8):
        b = banks.take()
        m = mm(b.t[:, 0:256], [(w[:, kk, k::8], merged[:, kk, :]) for kk in range(8)], [ml] + m_mrg + b.w)
        mv = V(ve.scalar_tensor_tensor, [m], xT[:, k, 256:512], b.t[:, 0:256], mod[:, 0, 2, k:k + 1],
               xT[:, k, 256:512], ALU.mult, ALU.add)
        b.free(mv)
    ring.release(("out", l), m)

    S["barrier"]()
    S["top"][0] = 64
    sq_t, r_t = carve(8, 256), carve(256)
    m_h = S["norm_modulate"](S["XC"], h, [affn], [mod[:, 0, 3, :]], sq_t, r_t)
    WT = route(nc, S, l, h, m_h)
    moe(nc, S, l, h, WT, mod)


def route(nc, S, l, h, m_h):
    V, A, T, G = S["V"], S["A"], S["T"], S["G"]
    ac, ve = nc.scalar, nc.vector
    mm, tr, C, carve, banks, ring = S["mm"], S["tr"], S["C"], S["carve"], S["banks"], S["ring"]
    flat, ml = ring.get(("router", l))
    w = flat[:, 0:512].rearrange("p (k e) -> p k e", k=8)
    b = banks.take()
    for i in range(2):
        m = mm(b.t[:, i * 64:(i + 1) * 64], [(h[:, kk, i * P:(i + 1) * P], w[:, kk, :]) for kk in range(8)],
               [ml, m_h] + b.w)
    ring.release(("router", l), m)
    sc, bi, mk, rep = carve(2, 64), carve(2, 64), carve(2, 64), carve(2, 64)
    s8, gs, rank = carve(16, 8), carve(2, 8), carve(2, 8)
    cmp1, cmp2 = carve(8, 8), carve(8, 8)
    top8, den = carve(2, 8), carve(2)
    WT = carve(256)
    ms = A(ac.activation, [m], sc, b.t[:, 0:128].rearrange("p (i e) -> p i e", i=2), ACT.Sigmoid)
    b.free(ms)
    m = V(ve.tensor_tensor, [ms], bi, sc, S["brow"][l].unsqueeze(1).to_broadcast([P, 2, 64]), ALU.add)
    for q in range(16):
        m2 = V(ve.max, [m], s8[:, q, :], bi[:, q // 8, (q % 8) * 8:(q % 8) * 8 + 8])
    m = V(ve.tensor_tensor, [m2], gs.rearrange("p i g -> p (i g)"), s8[:, :, 0], s8[:, :, 1], ALU.add)
    tri8 = C("tri8").rearrange("p (a b) -> p a b", a=8)
    for i in range(2):
        ga = gs[:, i, :].unsqueeze(2).to_broadcast([P, 8, 8])
        gb = gs[:, i, :].unsqueeze(1).to_broadcast([P, 8, 8])
        m1 = V(ve.tensor_tensor, [m], cmp1, gb, ga, ALU.is_gt)
        m = V(ve.tensor_tensor, [m], cmp2, gb, ga, ALU.is_equal)
        m = V(ve.tensor_tensor, [m], cmp2, cmp2, tri8, ALU.mult)
        m = V(ve.tensor_tensor, [m, m1], cmp1, cmp1, cmp2, ALU.add)
        m = V(ve.tensor_reduce, [m], rank[:, i, :], cmp1, AX, ALU.add)
        m = V(ve.tensor_scalar, [m], gs[:, i, :], rank[:, i, :], 3.5, None, ALU.is_lt)
        gm = gs[:, i, :].unsqueeze(2).to_broadcast([P, 8, 8])
        bv = bi[:, i, :].rearrange("p (g e) -> p g e", g=8)
        mv = mk[:, i, :].rearrange("p (g e) -> p g e", g=8)
        rv = rep[:, i, :].rearrange("p (g e) -> p g e", g=8)
        m1 = V(ve.tensor_tensor, [m], mv, bv, gm, ALU.mult)
        m = V(ve.tensor_scalar, [m], rank[:, i, :], gs[:, i, :], 1.0, 1.0e30, ALU.subtract, ALU.mult)
        m = V(ve.tensor_tensor, [m, m1], mv, mv, rank[:, i, :].unsqueeze(2).to_broadcast([P, 8, 8]), ALU.add)
        m1 = V(ve.max, [m], top8[:, i, :], mk[:, i, :])
        m = V(ve.match_replace, [m1], rep[:, i, :], top8[:, i, :], mk[:, i, :], -3.0e38)
        m = V(ve.tensor_tensor, [m], mk[:, i, :], mk[:, i, :], rep[:, i, :], ALU.not_equal)
        m = V(ve.tensor_tensor, [m], mk[:, i, :], mk[:, i, :], sc[:, i, :], ALU.mult)
        m = V(ve.tensor_reduce, [m], den[:, i:i + 1], mk[:, i, :], AX, ALU.add)
        m = V(ve.tensor_scalar, [m], den[:, i:i + 1], den[:, i:i + 1], 1e-20, None, ALU.add)
        m = V(ve.reciprocal, [m], den[:, i:i + 1], den[:, i:i + 1])
        m = V(ve.tensor_scalar, [m], mk[:, i, :], mk[:, i, :], den[:, i:i + 1], 2.5, ALU.mult, ALU.mult)
        b = banks.take()
        mt = tr(b.t[0:64, 0:P], mk[:, i, :], S["ident"], [m] + b.w)
        m_w = V(ve.tensor_copy, [mt], WT[0:64, i * P:(i + 1) * P], b.t[0:64, 0:P])
        b.free(m_w)
        m = m_w
    return WT, m_w


def moe(nc, S, l, h, route_out, mod):
    V, A, T, G = S["V"], S["A"], S["T"], S["G"]
    te, ac, ve, gp = nc.tensor, nc.scalar, nc.vector, nc.gpsimd
    mm, carve, banks, ring, xT, ident = S["mm"], S["carve"], S["banks"], S["ring"], S["xT"], S["ident"]
    WT, m_w = route_out
    S["barrier"]()
    ps = [b.t for b in banks.bufs]
    yb, up, wbb = ps[0:4], Rot(ps[4:7]), ps[7]
    m_wb, f_w = None, Rot([carve(2, 256) for _ in range(2)])
    f_s = Rot([carve(256) for _ in range(3)])
    f_g = Rot([carve(2, 256) for _ in range(2)])
    n = EXPERTS + 1

    def down(e, g, mg):
        flat, _ = ring.get(("exp", l, e))
        w2 = flat[:, 2 * UNIT:3 * UNIT].rearrange("p (j n) -> p j n", j=2)
        T.wait(mg)
        for k in range(8):
            o = yb[k // 2][:, (k % 2) * 256:(k % 2) * 256 + 256]
            for j in range(2):
                ins = te.matmul(o, w2[:, j, k::8], g.t[:, j, :], start=(e == 0 and j == 0 and k % 2 == 0),
                                stop=(e == n - 1 and j == 1), skip_group_check=True)
        m = T.done(ins)
        g.free(m)
        ring.release(("exp", l, e), m)
        return m

    prev = None
    for e in range(n):
        flat, ml = ring.get(("exp", l, e))
        w1 = flat[:, 0:UNIT].rearrange("p (k f) -> p k f", k=8)
        w3 = flat[:, UNIT:2 * UNIT].rearrange("p (k f) -> p k f", k=8)
        g = f_g.take()
        mg = []
        if e < EXPERTS and e % 2 == 0:
            wt = f_w.take()
            for u in range(2):
                m = mm(wbb[:, u * 256:u * 256 + 256],
                       [(ident[0:64, e + u:e + u + 1].to_broadcast([64, P]), WT[0:64, :])], [m_w, m_wb])
            m_wb = A(ac.activation, [m] + wt.w, wt.t, wbb[:, :].rearrange("p (u t) -> p u t", u=2), ACT.Copy)
        for j in range(2):
            b = up.take()
            mm(b.t[:, 0:256], [(w1[:, kk, j::2], h[:, kk, :]) for kk in range(8)], [ml] + b.w)
            m3 = mm(b.t[:, 256:512], [(w3[:, kk, j::2], h[:, kk, :]) for kk in range(8)], [])
            s = f_s.take()
            ms = A(ac.activation, [m3] + s.w, s.t, b.t[:, 0:256], ACT.Silu)
            if e < EXPERTS:
                m = V(ve.tensor_tensor, [ms, m3], s.t, s.t, b.t[:, 256:512], ALU.mult)
                b.free(ms, m)
                m = V(ve.tensor_tensor, [m, m_wb] + g.w, g.t[:, j, :], s.t, wt.t[:, e % 2, :], ALU.mult)
                wt.free(m)
            else:
                m = V(ve.tensor_tensor, [ms, m3] + g.w, g.t[:, j, :], s.t, b.t[:, 256:512], ALU.mult)
                b.free(ms, m)
            s.free(m)
            mg.append(m)
        if prev is not None:
            down(*prev)
        prev = (e, g, mg)
    m = down(*prev)
    for k in range(8):
        o = yb[k // 2][:, (k % 2) * 256:(k % 2) * 256 + 256]
        V(ve.scalar_tensor_tensor, [m], xT[:, k, 256:512], o, mod[:, 0, 5, k:k + 1], xT[:, k, 256:512],
          ALU.mult, ALU.add)
    S["barrier"]()
    for b in banks.bufs:
        b.free()


def modulate2(nc, S, l):
    V, ve, carve = S["V"], nc.vector, S["carve"]
    cact = S["cact"]
    mod = carve(2, 3, 8)
    m = S["modulation"](("mod2", l), S["bmod2"][l], 2, [cact[:, 1:3, kk] for kk in range(8)], mod)
    sc, gt = carve(2, 8), carve(2, 8)
    for s in range(2):
        m1 = V(ve.scalar_tensor_tensor, [m], sc[:, s, :], mod[:, s, 1, :], 1.0, S["gpre"][l], ALU.add, ALU.mult)
        m2 = V(ve.tensor_tensor, [m], gt[:, s, :], mod[:, s, 2, :], S["gpost"][l], ALU.mult)
    for e in (S["V"], S["A"], S["G"]):
        e.wait([m, m1, m2])
    return mod, sc, gt


def second_block(nc, S):
    V, A, T, G = S["V"], S["A"], S["T"], S["G"]
    te, ac, ve, gp = nc.tensor, nc.scalar, nc.vector, nc.gpsimd
    mm, tr, C, carve, reset, banks, ring, rstd = (S["mm"], S["tr"], S["C"], S["carve"], S["reset"], S["banks"],
                                                  S["ring"], S["rstd"])
    I, PM, xT, ident, ones = S["I"], S["PM"], S["xT"], S["ident"], S["ones"]
    top, barrier = S["top"], S["barrier"]
    h = S["hT"][:, :].rearrange("p (k t) -> p k t", k=8)
    seg2 = lambda a: a.rearrange("p (s t) -> p s t", s=2)

    reset()
    mod, sc, gt = modulate2(nc, S, 0)
    keep = top[0]
    sq_t, r_t = carve(8, 512), carve(512)
    m_h = S["norm_modulate"]((0, 512), h, [sc[:, 0, :], sc[:, 1, :]], [mod[:, 0, 0, :], mod[:, 1, 0, :]], sq_t, r_t)
    barrier()
    top[0] = keep
    yp, ym = carve(8, 512), carve(8, 512)
    keep = top[0]
    pad = Rot([carve(2, 272) for _ in range(2)])
    lev = [Rot([carve(2, 272) for _ in range(1)]) for _ in range(2)]
    dif = Rot([carve(2, 512) for _ in range(2)])
    sgr = Rot([carve(512) for _ in range(2)])
    mz = None
    for b_ in pad.bufs:
        mz = G(gp.memset, [], b_.t, 0.0)
        b_.free(mz)
    pflat, mpw = ring.get(("poolw",))
    pw = pflat.rearrange("p (c n) -> p c n", c=8)
    for g in range(4):
        flat, ml = ring.get(("pin", g))
        w = flat.rearrange("p (k n) -> p k n", k=8)
        df = dif.take()
        for c in range(2):
            b = banks.take()
            m = mm(b.t[:, :], [(w[:, kk, c * P:(c + 1) * P], h[:, kk, :]) for kk in range(8)], [ml, m_h] + b.w)
            p = pad.take()
            m = A(ac.activation, [m] + p.w, p.t[:, :, 8:264], seg2(b.t[:, :]), ACT.Copy)
            b.free(m)
            src = p.t
            lo, hi = 1, 272
            for lv in range(g + 1):
                o = lev[lv % 2].bufs[0].t
                if lv == 0:
                    m = V(ve.tensor_tensor, [m, V.last()], o[:, :, 1:272], src[:, :, 0:271], src[:, :, 1:272], ALU.add)
                else:
                    d = 1 << (lv - 1)
                    lo, hi = lo + d, hi - d
                    m = V(ve.tensor_tensor, [m], o[:, :, lo:hi], src[:, :, lo - d:hi - d], src[:, :, lo + d:hi + d],
                          ALU.add)
                src = o
            rec = C("recip")[:, g * 256:(g + 1) * 256].unsqueeze(1).to_broadcast([P, 2, 256])
            o = lev[(g + 1) % 2].bufs[0].t
            m = V(ve.tensor_tensor, [m], o[:, :, 8:264], src[:, :, 8:264], rec, ALU.mult)
            m_d = V(ve.tensor_tensor, [m] + df.w, seg2(df.t[:, c, :]), o[:, :, 8:264], p.t[:, :, 8:264],
                    ALU.subtract)
            p.free(m_d)
        ring.release(("pin", g), T.last())
        flat, ml = ring.get(("pgate", g))
        w = flat.rearrange("p (k n) -> p k n", k=8)
        for c in range(2):
            b = banks.take()
            m = mm(b.t[:, :], [(w[:, kk, c * P:(c + 1) * P], h[:, kk, :]) for kk in range(8)], [ml] + b.w)
            s = sgr.take()
            ms = A(ac.activation, [m] + s.w, s.t, b.t[:, :], ACT.Silu)
            b.free(ms)
            b = banks.take()
            m = mm(b.t[:, :], [(pw[:, 2 * g + cc, c * P:(c + 1) * P], df.t[:, cc, :]) for cc in range(2)],
                   [mpw, m_d] + b.w)
            mv = V(ve.scalar_tensor_tensor, [m, ms], yp[:, 2 * g + c, :], b.t[:, :],
                   PM["pscale"][:, 2 * g + c:2 * g + c + 1], s.t, ALU.mult, ALU.mult)
            b.free(mv)
            s.free(mv)
        df.free(m)
        ring.release(("pgate", g), m)
    ring.release(("poolw",), m)
    m_yp = mv
    barrier()
    top[0] = keep
    spare = ym.rearrange("p k t -> p (k t)")
    g16 = spare[:, 0:512]
    gates = spare[:, 512:2560].rearrange("p (j t) -> p j t", j=4)
    tmp = spare[:, 2560:3584].rearrange("p (j t) -> p j t", j=2)
    aR = spare[:, 3584:4096]
    nM = [carve(512) for _ in range(2)]
    flat, ml = ring.get(("gates",))
    w = flat[:, 0:128].rearrange("p (k n) -> p k n", k=8)
    b = banks.take()
    m = mm(b.t[0:16, :], [(w[:, kk, :], h[:, kk, :]) for kk in range(8)], [ml] + b.w)
    ring.release(("gates",), m)
    mg = A(ac.activation, [m], g16[0:16, :], b.t[0:16, :], ACT.Copy)
    b.free(mg)
    for t in range(4):
        b = banks.take()
        m = mm(b.t[0:4, :], [(ident[0:16, 4 * t:4 * t + 4], g16[0:16, :])], [mg] + b.w)
        m = A(ac.activation, [m], gates[0:4, t, :], b.t[0:4, :], ACT.Identity, bias=S["bgate"][0:4, t:t + 1])
        b.free(m)
    m_gt = m
    acol, ecol = carve(4, 2, 4), carve(4, 2, 4)
    for d in range(2):
        li, lf = gates[0:4, 2 * d, :], gates[0:4, 2 * d + 1, :]
        e, B = tmp[0:4, 0, :], tmp[0:4, 1, :]
        m = A(ac.activation, [m_gt, V.last(), T.last()], e, lf, ACT.Abs)
        m = A(ac.activation, [m], e, e, ACT.Exp, scale=-1.0)
        m = A(ac.activation, [m], e, e, ACT.Ln, bias=ones[0:4, 0:1])
        m = V(ve.scalar_tensor_tensor, [m], lf, lf, 0.0, e, ALU.min, ALU.subtract)

        def scans(dst, src, op, init, m):
            if d == 0:
                return V(ve.tensor_tensor_scan, [m], dst, src, src, init, op, ALU.bypass)
            m = V(ve.tensor_tensor_scan, [m], seg2(dst)[:, 0, ::-1],
                  seg2(src)[:, 0, ::-1], seg2(src)[:, 0, ::-1], init, op, ALU.bypass)
            return V(ve.tensor_tensor_scan, [m], seg2(dst)[:, 1, ::-1], seg2(src)[:, 1, ::-1],
                     seg2(src)[:, 1, ::-1], dst[:, 0:1], op, ALU.bypass)

        m = scans(B, lf, ALU.add, 0.0, m)
        m = V(ve.tensor_tensor, [m, T.last()], aR[0:4, :], li, B, ALU.subtract)
        m = scans(nM[d][0:4, :], aR[0:4, :], ALU.max, 0.0, m)
        m = V(ve.tensor_scalar, [m], nM[d][0:4, :], nM[d][0:4, :], -1.0, None, ALU.mult)
        nMB = e
        m = V(ve.tensor_tensor, [m], nMB, nM[d][0:4, :], B, ALU.subtract)
        b = banks.take()
        for j in range(4):
            tr(b.t[:, j * 4:j * 4 + 4], aR[0:4, j * P:(j + 1) * P], ident[0:4, 0:4], [m] + b.w)
            mt = tr(b.t[:, 16 + j * 4:20 + j * 4], nMB[:, j * P:(j + 1) * P], ident[0:4, 0:4], [])
        m1 = A(ac.activation, [mt], acol[:, :, d, :], b.t[:, 0:16].rearrange("p (j h) -> p j h", j=4), ACT.Copy)
        m2 = A(ac.activation, [mt], ecol[:, :, d, :], b.t[:, 16:32].rearrange("p (j h) -> p j h", j=4), ACT.Exp)
        b.free(m2)
    m_cols = m2
    A.wait([m_cols])
    V.wait([m_cols])
    T.wait([V.last()])
    vaug = carve(4, 257)
    qT, kT = carve(2, 512), carve(2, 512)
    oh = kT.rearrange("p a t -> p (a t)").rearrange("p (j e) -> p j e", j=4)
    zT = qT
    hs = carve(4, 256)
    upad = Rot([carve(2, 258)])
    Cd = carve(4, 512)
    dm = ym[:, 7, :].rearrange("p (j t) -> p j t", j=4)
    stt = carve(4, 4)
    ss = carve(8)
    for b_ in upad.bufs:
        b_.free(G(gp.memset, [], b_.t, 0.0))
    mone = G(gp.memset, [], vaug[:, :, 256:257], 1.0)
    cv = PM["conv"]
    m_hs = None
    for hd in range(4):
        barrier()
        for n, dst in (("q", qT), ("k", kT)):
            flat, ml = ring.get((n, hd))
            w = flat.rearrange("p (k n) -> p k n", k=8)
            for c in range(2):
                b = banks.take()
                m = mm(b.t[:, :], [(w[:, kk, c * P:(c + 1) * P], h[:, kk, :]) for kk in range(8)], [ml] + b.w)
                u = upad.take()
                m = A(ac.activation, [m] + u.w, u.t[:, :, 1:257], seg2(b.t[:, :]), ACT.Copy)
                b.free(m)
                ch = (0 if n == "q" else 8) + hd * 2 + c
                o = seg2(dst[:, c, :])
                m = V(ve.tensor_scalar, [m], o, u.t[:, :, 0:256], cv[:, ch:ch + 1], None, ALU.mult)
                for j in (1, 2):
                    m = V(ve.scalar_tensor_tensor, [m], o, u.t[:, :, j:j + 256], cv[:, 16 * j + ch:16 * j + ch + 1], o,
                          ALU.mult, ALU.add)
                u.free(m)
            ring.release((n, hd), T.last())
        m_qk = m
        flat, ml = ring.get(("v", hd))
        w = flat.rearrange("p (k n) -> p k n", k=8)
        for j in range(4):
            b = banks.take()
            m = mm(b.t[:, 0:256], [(h[:, kk, j * P:(j + 1) * P], w[:, kk, :]) for kk in range(8)], [ml] + b.w)
            m_v = A(ac.activation, [m], vaug[:, j, 0:256], b.t[:, 0:256], ACT.Copy)
            b.free(m_v)
        ring.release(("v", hd), m)
        for d in range(2):
            b = banks.take()
            m_nm = mm(b.t[:, :], [(ident[0:4, hd:hd + 1].to_broadcast([4, P]), nM[d][0:4, :])], b.w)
            tri = C("tri_f" if d == 0 else "tri_b").unsqueeze(1).to_broadcast([P, 4, P])
            m = V(ve.tensor_tensor, [m_nm, T.last(), A.last()], dm, b.t[:, :].rearrange("p (j t) -> p j t", j=4),
                  tri, ALU.add)
            spans = []
            for i in range(4):
                bias = acol[:, i, d, hd:hd + 1]
                lo, hi = i * P, (i + 1) * P
                if d == 0:
                    rest = [(hi, 512)]
                elif i < 2:
                    rest = [(0, lo), (256, 512)]
                else:
                    rest = [(256, lo)]
                A(ac.activation, [m], Cd[:, i, lo:hi], dm[:, i, :], ACT.Exp, bias=bias)
                me = A.last()
                for r0, r1 in rest:
                    if r1 > r0:
                        me = A(ac.activation, [m_nm], Cd[:, i, r0:r1], b.t[:, r0:r1], ACT.Exp, bias=bias)
                sp = [(lo, hi)] + [r for r in rest if r[1] > r[0]]
                sp.sort()
                out_ = [sp[0]]
                for r in sp[1:]:
                    if r[0] == out_[-1][1]:
                        out_[-1] = (out_[-1][0], r[1])
                    else:
                        out_.append(r)
                spans.append((out_, me))
            b.free(me, m)
            for i in range(4):
                b = banks.take()
                t0 = 0 if i < 2 else 256
                m_s = m = mm(b.t[:, t0:512], [(kT[:, c, i * P:(i + 1) * P], qT[:, c, t0:512]) for c in range(2)],
                       [m_qk] + b.w)
                for r0, r1 in spans[i][0]:
                    mc = V(ve.scalar_tensor_tensor, [m, spans[i][1]], Cd[:, i, r0:r1], b.t[:, r0:r1], 0.0625,
                           Cd[:, i, r0:r1], ALU.mult, ALU.mult)
                b.free(mc)
            for j in range(4):
                if d == 0:
                    src = list(range(j + 1))
                elif j < 2:
                    src = list(range(j, 2))
                else:
                    src = [0, 1] + list(range(j, 4))
                b = banks.take()
                m = mm(b.t[:, 0:257], [(Cd[:, i, j * P:(j + 1) * P], vaug[:, i, :]) for i in src],
                       [mc, m_v, mone] + b.w)
                st = stt[:, j, 2 * d:2 * d + 1]
                m = A(ac.activation, [m], st, b.t[:, 256:257], ACT.Abs)
                m = V(ve.tensor_tensor, [m], st, st, ecol[:, j, d, hd:hd + 1], ALU.max)
                m = V(ve.reciprocal, [m], st, st)
                if d == 0:
                    m_hs = V(ve.tensor_scalar, [m], hs[:, j, :], b.t[:, 0:256], st, None, ALU.mult)
                else:
                    m_hs = V(ve.scalar_tensor_tensor, [m], hs[:, j, :], b.t[:, 0:256], st, hs[:, j, :], ALU.mult,
                             ALU.add)
                b.free(m_hs)
        flat, ml = ring.get(("o", hd))
        w = flat.rearrange("p (k n) -> p k n", k=8)
        for j in range(4):
            b = banks.take()
            m = mm(b.t[:, 0:256], [(h[:, kk, j * P:(j + 1) * P], w[:, kk, :]) for kk in range(8)], [ml] + b.w)
            m_o = A(ac.activation, [m, m_s], oh[:, j, :], b.t[:, 0:256], ACT.Sigmoid)
            b.free(m_o)
        ring.release(("o", hd), m)
        flat, ml = ring.get(("z", hd))
        w = flat.rearrange("p (k n) -> p k n", k=8)
        for c in range(2):
            b = banks.take()
            m = mm(b.t[:, :], [(w[:, kk, c * P:(c + 1) * P], h[:, kk, :]) for kk in range(8)], [ml] + b.w)
            m_z = A(ac.activation, [m, m_s], zT[:, c, :], b.t[:, :], ACT.Silu)
            b.free(m_z)
        ring.release(("z", hd), m)
        m = V(ve.tensor_tensor, [m_hs, m_o], hs, hs, oh, ALU.mult)
        for j in range(4):
            mq = A(ac.activation, [m], oh[:, j, :], hs[:, j, :], ACT.Square, accum_out=ss[:, j:j + 1])
        mr = V(ve.tensor_scalar, [mq], ss[:, 4:8], ss[:, 0:4], 1.0 / 256, EPS, ALU.mult, ALU.add)
        mr = V(ve.reciprocal, [mr], ss[:, 4:8], ss[:, 4:8])
        mr = A(ac.activation, [mr], ss[:, 4:8], ss[:, 4:8], ACT.Sqrt)
        for j in range(4):
            m = V(ve.tensor_scalar, [mr], hs[:, j, :], hs[:, j, :], ss[:, 4 + j:5 + j], None, ALU.mult)
        for c in range(2):
            b = banks.take()
            for j in range(4):
                mt = tr(b.t[:, j * P:(j + 1) * P], hs[:, j, c * P:(c + 1) * P], ident, [m] + b.w)
            mv = V(ve.scalar_tensor_tensor, [mt, m_z], ym[:, 2 * hd + c, :], b.t[:, :],
                   PM["mnorm"][:, 2 * hd + c:2 * hd + c + 1], zT[:, c, :], ALU.mult, ALU.mult)
            b.free(mv)
    m_ym = mv
    barrier()
    fa, ma = ring.get(("about", 0))
    fb, mb = ring.get(("about", 1))
    wa, wb = fa.rearrange("p (c n) -> p c n", c=8), fb.rearrange("p (c n) -> p c n", c=8)
    for k in range(8):
        b = banks.take()
        m = mm(b.t[:, :], [(wa[:, c, k::8], ym[:, c, :]) for c in range(8)]
               + [(wb[:, c, k::8], yp[:, c, :]) for c in range(8)], [ma, mb, m_ym, m_yp] + b.w)
        m_y = A(ac.activation, [m], h[:, k, :], b.t[:, :], ACT.Copy)
        b.free(m_y)
    ring.release(("about", 0), m)
    ring.release(("about", 1), m)
    barrier()
    top[0] = keep
    post_norm(nc, S, h, 512, [(0, gt[:, 0, :]), (1, gt[:, 1, :])], ym, carve(512))

    reset()
    mod, sc, gt = modulate2(nc, S, 1)
    keep = top[0]
    sq_t, r_t = carve(8, 512), carve(512)
    m_h = S["norm_modulate"]((0, 512), h, [sc[:, 0, :], sc[:, 1, :]], [mod[:, 0, 0, :], mod[:, 1, 0, :]], sq_t, r_t)
    barrier()
    top[0] = keep
    qT, zT, oT = carve(8, 256), carve(8, 256), carve(8, 256)
    kT, vv, kd = carve(2, 512), carve(4, 256), carve(4, 512)
    axc, axs = C("ax_cos"), C("ax_sin")
    t1r = Rot([carve(256) for _ in range(2)])
    hx = h[:, :, 256:512]

    def rope(dst, m):
        b = banks.take()
        m = mm(b.t[:, 0:256], [(C("swap_pair"), dst)], [m] + b.w)
        t1 = t1r.take()
        mt = V(ve.tensor_tensor, [m] + t1.w, t1.t, b.t[:, 0:256], axs, ALU.mult)
        b.free(mt)
        mg = G(gp.tensor_tensor, [m], dst, dst, axc, ALU.mult)
        m = V(ve.tensor_tensor, [mt, mg], dst, dst, t1.t, ALU.add)
        t1.free(m)
        return m

    flat, ml = ring.get(("cq",))
    w = flat.rearrange("p (k n) -> p k n", k=8)
    for a in range(2):
        for g in range(4):
            b = banks.take()
            m = mm(b.t[:, 0:256], [(w[:, kk, (4 * a + g) * P:(4 * a + g + 1) * P], hx[:, kk, :]) for kk in range(8)], [ml, m_h] + b.w)
            ma = A(ac.activation, [m], qT[:, 4 * a + g, :], b.t[:, 0:256], ACT.Copy)
            b.free(ma)
            m_q = rope(qT[:, 4 * a + g, :], ma)
    ring.release(("cq",), m)
    flat, ml = ring.get(("ckv",))
    w = flat.rearrange("p (k n) -> p k n", k=8)
    for a in range(2):
        b = banks.take()
        m = mm(b.t[:, :], [(w[:, kk, a * P:(a + 1) * P], h[:, kk, :]) for kk in range(8)], [ml] + b.w)
        ma = A(ac.activation, [m], kT[:, a, :], b.t[:, :], ACT.Copy)
        b.free(ma)
        mr = rope(kT[:, a, 256:512], ma)
        for u in range(2):
            for half in (0, 64):
                m_k = A(ac.activation, [mr, ma], kd[half:half + 64, 2 * a + u, :], kT[u * 64:u * 64 + 64, a, :], ACT.Copy)
    for j in range(4):
        b = banks.take()
        m = mm(b.t[:, 0:256], [(h[:, kk, j * P:(j + 1) * P], w[:, kk, 256:512]) for kk in range(8)], [ml] + b.w)
        m_v = A(ac.activation, [m], vv[:, j, :], b.t[:, 0:256], ACT.Copy)
        b.free(m_v)
    ring.release(("ckv",), m)
    flat, ml = ring.get(("cz",))
    w = flat.rearrange("p (k n) -> p k n", k=8)
    for a in range(2):
        for g in range(4):
            b = banks.take()
            m = mm(b.t[:, 0:256], [(w[:, kk, (4 * a + g) * P:(4 * a + g + 1) * P], hx[:, kk, :]) for kk in range(8)], [ml] + b.w)
            m_z = A(ac.activation, [m], zT[:, 4 * a + g, :], b.t[:, 0:256], ACT.Silu)
            b.free(m_z)
    ring.release(("cz",), m)
    f_s = Rot([carve(512) for _ in range(3)])
    f_p = Rot([carve(4, P) for _ in range(2)])
    f_st = Rot([carve(8) for _ in range(4)])
    band = C("band").rearrange("p (i t) -> p i t", i=2)
    work, outs = Rot(None, banks.bufs[0:6]), Rot(None, banks.bufs[6:8])
    A.wait([m_z])
    V.wait([m_z])
    for a in range(2):
        for g in range(4):
            ch = 4 * a + g
            bo = outs.take()
            wo = list(bo.w)
            for u in range(2):
                hd, kv, base = 2 * ch + u, ch // 2, u * 64
                for i in range(2):
                    b = work.take()
                    m = mm(b.t[:, :], [(qT[base:base + 64, ch, i * P:(i + 1) * P], kd[base:base + 64, kv, :])],
                           [m_q, m_k] + b.w)
                    s, st = f_s.take(), f_st.take()
                    m = V(ve.scalar_tensor_tensor, [m] + s.w, s.t, b.t[:, :], 0.125, band[:, i, :], ALU.mult, ALU.add)
                    b.free(m)
                    m = V(ve.tensor_reduce, [m] + st.w, st.t[:, 0:1], s.t, AX, ALU.max)
                    m = V(ve.tensor_scalar, [m], st.t[:, 1:2], st.t[:, 0:1], S["sink"][:, hd:hd + 1], -1.0,
                          ALU.max, ALU.mult)
                    me = A(ac.activation, [m], s.t, s.t, ACT.Exp, bias=st.t[:, 1:2], accum_out=st.t[:, 2:3])
                    mk = A(ac.activation, [m], st.t[:, 3:4], S["sink"][:, hd:hd + 1], ACT.Exp, bias=st.t[:, 1:2])
                    m = V(ve.tensor_tensor, [mk, me], st.t[:, 4:5], st.t[:, 2:3], st.t[:, 3:4], ALU.add)
                    m = V(ve.reciprocal, [m], st.t[:, 5:6], st.t[:, 4:5])
                    m = V(ve.tensor_scalar, [m], s.t, s.t, st.t[:, 5:6], None, ALU.mult)
                    st.free(m)
                    b = work.take()
                    for kb in range(4):
                        mt = tr(b.t[:, kb * P:(kb + 1) * P], s.t[:, kb * P:(kb + 1) * P], ident, [m] + b.w)
                    s.free(mt)
                    p = f_p.take()
                    m = A(ac.activation, [mt] + p.w, p.t, b.t[:, :].rearrange("p (k t) -> p k t", k=4), ACT.Copy)
                    b.free(m)
                    m_o = mm(bo.t[base:base + 64, i * P:(i + 1) * P],
                             [(vv[:, kb, kv * 64:(kv + 1) * 64], p.t[:, kb, :]) for kb in range(4)], [m, m_v] + wo)
                    p.free(m_o)
            m_oT = V(ve.tensor_tensor, [m_o], oT[:, ch, :], zT[:, ch, :], bo.t[:, 0:256], ALU.mult)
            bo.free(m_oT)
    flat, ml = ring.get(("cout",))
    w = flat.rearrange("p (c n) -> p c n", c=8)
    y = S["hT"][:, 0:2048].rearrange("p (k t) -> p k t", k=8)
    for k in range(8):
        b = banks.take()
        m = mm(b.t[:, 0:256], [(w[:, c, k::8], oT[:, c, :]) for c in range(8)], [ml, m_oT] + b.w)
        m_y = A(ac.activation, [m], y[:, k, :], b.t[:, 0:256], ACT.Copy)
        b.free(m_y)
    ring.release(("cout",), m)
    barrier()
    post_norm(nc, S, y, 256, [(1, gt[:, 1, :])], qT, carve(256))
    barrier()
    xo = S["hT"][:, 2048:4096].rearrange("p (i d) -> p i d", i=2)
    for i in range(2):
        for k0 in (0, 4):
            b = banks.take()
            for k in range(k0, k0 + 4):
                m = tr(b.t[:, (k - k0) * P:(k - k0 + 1) * P], xT[:, k, 256 + i * P:256 + (i + 1) * P], ident, b.w)
            dst = xo[:, i, :].rearrange("p (d k) -> p k d", k=8)[:, k0:k0 + 4, :]
            m = V(ve.tensor_copy, [m], dst, b.t[:, :].rearrange("p (k t) -> p k t", k=4))
            b.free(m)
        S["SP"].wait([m])
        nc.sync.dma_start(S["out"][0, i * P:(i + 1) * P, :], xo[:, i, :]).then_inc(S["s_out"], 16)
    nc.sync.wait_ge(S["s_out"], 32)


def post_norm(nc, S, y, n, parts, sq_t, r_t):
    V, A, banks, mm, xT, ve, ac = S["V"], S["A"], S["banks"], S["mm"], S["xT"], nc.vector, nc.scalar
    ms = A(ac.activation, [], sq_t, y, ACT.Square)
    b = banks.take()
    m = mm(b.t[:, 0:n], [(S["ones"], sq_t[:, k, :]) for k in range(8)], [ms] + b.w)
    mr = S["rstd"](b.t[:, 0:n], r_t, D, [m])
    b.free(mr)
    for k in range(8):
        for q, (s, g) in enumerate(parts):
            seg = slice(q * 256, (q + 1) * 256)
            m = V(ve.scalar_tensor_tensor, [mr], y[:, k, seg], y[:, k, seg], g[:, k:k + 1], r_t[:, seg], ALU.mult,
                  ALU.mult)
            xs = xT[:, k, s * 256:(s + 1) * 256]
            V(ve.tensor_tensor, [m], xs, xs, y[:, k, seg], ALU.add)


_INS = """x c positions w_mod b_mod norm_mix_g norm_ffn_g w_in qn_g kn_g lam_q1 lam_k1 lam_q2 lam_k2 subln_g
w_proj_a w_dw b_dw conv_ln_g conv_ln_b w_proj_b b_proj_b w_proj_c w_out w_router b_router w1 w3 w2 ws1 ws3 ws2
c_2 ctx_2 c_ctx_2 w_mod_2 b_mod_2 g_pre_2 g_post_2 ab_w_in_2 ab_b_gate_2 ab_conv_2 ab_mnorm_2 ab_pool_w_2
ab_pool_scale_2 ab_w_out_2 c_w_in_2 c_sink_2 c_w_out_2""".split()


def kernel(**inputs):
    import concourse.bacc as _bacc
    from concourse.bass_utils import run_bass_kernel_spmd as _run

    nc = _bacc.Bacc("TRN2", target_bir_lowering=False, num_devices=1)
    arrays, aps = {}, {}
    for name in _INS:
        a = np.ascontiguousarray(inputs[name])
        arrays[f"in_{name}"] = a
        aps[name] = nc.dram_tensor(f"in_{name}", a.shape, mybir.dt.from_np(a.dtype), kind="ExternalInput").ap()
    table = make_consts()
    arrays["in_table"] = table
    consts = nc.dram_tensor("in_table", table.shape, F32, kind="ExternalInput").ap()
    out = nc.dram_tensor("out_0", (1, 256, D), F32, kind="ExternalOutput").ap()
    build(nc, aps, consts, out)
    r = _run(nc, [arrays], core_ids=[0])
    return r.results[0]["out_0"]
```

```python
import math
from contextlib import ExitStack

import numpy as np
import concourse.bass as bass
from concourse import mybir

F32 = mybir.dt.float32
I32 = mybir.dt.int32
ALU = mybir.AluOpType
ACT = mybir.ActivationFunctionType
AX = mybir.AxisListType.X

P = 128
D = 1024
NEG = -1.0e30
EPS = 1e-6
UNIT = 2048
UNITS = 11
LAYERS = 2
EXPERTS = 64
SLOTS = 64
MORE = 31
AR_COLS = 16264

CONST_COLS = {}


def make_consts():
    p = np.arange(P)
    cols = []
    at = [0]

    def add(name, a):
        a = np.asarray(a, np.float32).reshape(P, -1)
        CONST_COLS[name] = (at[0], a.shape[1])
        at[0] += a.shape[1]
        cols.append(a)

    add("ident", np.eye(P))
    add("ones", np.ones((P, P)))
    add("blk64", (p[:, None] // 64) == (p[None, :] // 64))
    half = np.zeros((P, P))
    pair = np.zeros((P, P))
    for m in range(P):
        if m % 64 < 32:
            half[m + 32, m] = -1.0
        else:
            half[m - 32, m] = 1.0
        if m % 2 == 0:
            pair[m + 1, m] = -1.0
        else:
            pair[m - 1, m] = 1.0
    add("swap_half", half)
    add("swap_pair", pair)
    add("from_s", p[:, None] >= p[None, :])
    causal = np.where(p[None, :] <= p[:, None], 0.0, NEG)
    add("causal", np.concatenate([np.zeros((P, P)), causal], 1))
    before = np.where(p[:, None] < p[None, :], 0.0, NEG)
    add("before", np.concatenate([before, np.zeros((P, P)), before], 1))
    add("tri_f", np.where(p[:, None] <= p[None, :], 0.0, NEG))
    add("tri_b", np.where(p[:, None] >= p[None, :], 0.0, NEG))
    inv = (np.float32(10000.0) ** (-np.arange(0, 64, 2, dtype=np.float32) / np.float32(64))).astype(np.float32)
    add("inv", inv[p % 32][:, None])
    add("iota", np.broadcast_to(np.arange(64)[None, :], (P, 64)))
    a8 = np.arange(8)
    add("tri8", np.broadcast_to((a8[None, :] < a8[:, None]).astype(np.float32).reshape(1, 64), (P, 64)))
    t = np.arange(256)
    band = []
    for i in range(2):
        q = i * P + p
        ok = np.abs(q[:, None] - t[None, :]) <= 128
        band.append(np.concatenate([np.zeros((P, 256)), np.where(ok, 0.0, NEG)], 1))
    add("band", np.concatenate(band, 1))
    rec = []
    for w in (2, 4, 8, 16):
        n = np.clip(t + w // 2, 0, 256) - np.clip(t - w // 2, 0, 256)
        rec.append((np.float32(1.0) / n.astype(np.float32)))
    add("recip", np.broadcast_to(np.concatenate(rec)[None, :], (P, 1024)))
    f = (np.float32(10000.0) ** (-np.arange(16, dtype=np.float32) / np.float32(16))).astype(np.float32)
    ang = np.concatenate([(t // 64).astype(np.float32)[:, None] * f, (t % 64).astype(np.float32)[:, None] * f], 1)
    i32 = (p % 64) // 2
    add("ax_cos", np.cos(ang.astype(np.float64))[:, i32].T)
    add("ax_sin", np.sin(ang.astype(np.float64))[:, i32].T)
    return np.ascontiguousarray(np.concatenate(cols, 1))


class Eng:

    def __init__(self, eng, sem, name):
        self.eng, self.sem, self.name, self.n, self.seen = eng, sem, name, 0, {}

    def wait(self, marks):
        for m in marks:
            if m is None:
                continue
            if isinstance(m, list):
                self.wait(m)
                continue
            sem, value, key = m
            if self.seen.get(key, 0) < value:
                self.eng.wait_ge(sem, value)
                self.seen[key] = value

    def __call__(self, fn, waits, *args, **kw):
        self.wait(waits)
        ins = fn(*args, **kw)
        return self.done(ins)

    def done(self, ins):
        self.n += 1
        ins.then_inc(self.sem, 1)
        return (self.sem, self.n, self.name)

    def last(self):
        return (self.sem, self.n, self.name)


class Buf:

    def __init__(self, t):
        self.t, self.w = t, []

    def free(self, *marks):
        self.w = list(marks)


class Rot:

    def __init__(self, tiles, bufs=None):
        self.bufs, self.i = bufs or [Buf(t) for t in tiles], 0

    def take(self):
        b = self.bufs[self.i % len(self.bufs)]
        self.i += 1
        return b


class Ring:

    def __init__(self, tile, sp, sems):
        self.tile, self.sp, self.sems = tile, sp, sems
        self.items, self.nxt, self.pos, self.live = [], 0, 0, []
        self.count = [0] * len(sems)
        self.where, self.gone = {}, {}

    def plan(self, key, units, parts):
        self.items.append((key, units, parts))

    def pump(self):
        while self.nxt < len(self.items):
            key, units, parts = self.items[self.nxt]
            pos = self.pos if self.pos + units <= UNITS else 0
            over = [x for x in self.live if x[0] < pos + units and pos < x[1]]
            if any(x[2] not in self.gone for x in over):
                return
            for x in over:
                self.sp.wait([self.gone[x[2]]])
            self.live = [x for x in self.live if x not in over]
            flat = self.tile[:, pos * UNIT:(pos + units) * UNIT]
            k = self.nxt % len(self.sems)
            for dst, src in parts:
                self.sp.eng.dma_start(dst(flat), src).then_inc(self.sems[k], 16)
                self.count[k] += 16
            self.where[key] = (flat, (self.sems[k], self.count[k], f"ring{k}"))
            self.live.append((pos, pos + units, key))
            self.pos = pos + units
            self.nxt += 1

    def get(self, key):
        return self.where[key]

    def release(self, key, *marks):
        self.gone[key] = list(marks)
        self.pump()


def build(nc, I, consts, out):
    ctx = ExitStack()
    with ctx:
        program(nc, ctx, I, consts, out)


def program(nc, ctx, I, consts, out):
    def sb(name, shape, dt=F32):
        return ctx.enter_context(nc.sbuf_tensor(name, shape, dt))

    def sem(name):
        return ctx.enter_context(nc.semaphore(name))

    T = Eng(nc.tensor, sem("s_pe"), "pe")
    A = Eng(nc.scalar, sem("s_act"), "act")
    V = Eng(nc.vector, sem("s_dve"), "dve")
    G = Eng(nc.gpsimd, sem("s_pool"), "pool")
    SP = Eng(nc.sync, sem("s_sp"), "sp")
    engines = [T, A, V, G]
    te, ac, ve, gp = nc.tensor, nc.scalar, nc.vector, nc.gpsimd

    def barrier():
        marks = [e.last() for e in engines if e.n]
        for e in engines:
            e.wait([m for m in marks if m[2] != e.name] + ([e.last()] if e.n and e is not T else []))

    NCOL = consts.shape[1]
    cst = sb("cst", [P, NCOL])
    ring_t = sb("ring", [P, UNITS * UNIT])
    xT = sb("xT", [P, 8, 512])
    hT = sb("hT", [P, 4096])
    par = sb("par", [P, 640])
    ar = sb("ar", [P, AR_COLS])
    banks = Rot([ctx.enter_context(nc.psum_tensor(f"ps{i}", [P, 512], F32)) for i in range(8)])
    ring = Ring(ring_t, SP, [sem(f"s_ring{i}") for i in range(UNITS + 1)])
    s_par = sem("s_par")
    s_x = sem("s_x")
    s_out = sem("s_out")
    more = []
    for l in range(LAYERS):
        more.append([Eng(e, sem(f"s_more_{n}{l}"), f"more_{n}{l}")
                     for e, n in ((nc.tensor, "pe"), (nc.scalar, "act"), (nc.vector, "dve"))]
                    + [[sem(f"s_more_w{l}{i}") for i in range(2)]])

    top = [0]

    def reset():
        barrier()
        top[0] = 0

    def carve(*shape):
        n = int(np.prod(shape))
        a = ar[:, top[0]:top[0] + n]
        top[0] += n
        assert top[0] <= AR_COLS, top[0]
        if len(shape) == 2:
            a = a.rearrange("p (a b) -> p a b", a=shape[0])
        if len(shape) == 3:
            a = a.rearrange("p (a b c) -> p a b c", a=shape[0], b=shape[1])
        return a

    rows = carve(3, P)

    def C(name):
        o, n = CONST_COLS[name]
        return cst[:, o:o + n]

    ptop = [0]

    def pcol(n):
        a = par[:, ptop[0]:ptop[0] + n]
        ptop[0] += n
        assert ptop[0] <= 640
        return a

    def mm(o, pairs, waits, first=True, last=True, lax=False):
        T.wait(waits)
        n = len(pairs)
        for i, (l, r) in enumerate(pairs):
            ins = te.matmul(o, l, r, start=(first and i == 0), stop=(last and i == n - 1), skip_group_check=lax)
        return T.done(ins)

    def tr(o, i, ident, waits):
        T.wait(waits)
        return T.done(te.transpose(o, i, ident))

    ident, ones = C("ident"), C("ones")

    def plan_cols(key, w, c0, n, units):
        src = w.rearrange("(p k) n -> p k n", k=8)[:, :, c0:c0 + n]
        ring.plan(key, units, [(lambda f: f[:, 0:8 * n].rearrange("p (k n) -> p k n", k=8), src)])

    def plan_rows(key, w, k, units):
        src = w.rearrange("(c p) n -> p c n", c=k)
        ring.plan(key, units, [(lambda f: f[:, 0:k * src.shape[2]].rearrange("p (c n) -> p c n", c=k), src)])

    def plan_up(key, w1, w3):
        ring.plan(("up",) + key, 2, [
            (lambda f: f[:, 0:UNIT], w1.rearrange("(p k) f -> p (k f)", k=8)),
            (lambda f: f[:, UNIT:2 * UNIT], w3.rearrange("(p k) f -> p (k f)", k=8))])

    def plan_down(key, w2):
        ring.plan(("down",) + key, 1, [(lambda f: f[:, 0:UNIT], w2.rearrange("(p j) n -> p (j n)", j=2))])

    for l in range(LAYERS):
        for j in range(6):
            plan_cols(("mod", l, j), I["w_mod"][l], j * D, D, 4)
        for b in range(4):
            plan_cols(("in", l, b), I["w_in"][l], b * D, D, 4)
        for b, n in enumerate(("w_proj_a", "w_proj_b", "w_proj_c")):
            plan_cols(("in", l, 4 + b), I["w_in"][l], (4 + b) * D, D, 4)
            plan_rows(("proj", l, b), I[n][l], 4, 2)
        plan_cols(("out", l), I["w_out"][l], 0, D, 4)
        plan_cols(("router", l), I["w_router"][l], 0, EXPERTS, 1)
        plan_up((l, EXPERTS), I["ws1"][l], I["ws3"][l])
        plan_down((l, EXPERTS), I["ws2"][l])
        for e in range(0, EXPERTS, 2):
            for u in (e, e + 1):
                plan_up((l, u), I["w1"][l, u], I["w3"][l, u])
            for u in (e, e + 1):
                plan_down((l, u), I["w2"][l, u])
    abw = I["ab_w_in_2"][0]
    for j in range(3):
        plan_cols(("mod2", 0, j), I["w_mod_2"][0], j * D, D, 4)
    plan_rows(("poolw",), I["ab_pool_w_2"][0].rearrange("g c d -> (g c) d"), 8, 1)
    for g in range(4):
        plan_cols(("pin", g), abw, 5 * D + g * 256, 256, 1)
        plan_cols(("pgate", g), abw, 6 * D + g * 256, 256, 1)
    plan_cols(("gates",), abw, 7 * D, 16, 1)
    for h in range(4):
        for n, b in (("q", 0), ("k", 1), ("v", 2), ("o", 3), ("z", 4)):
            plan_cols((n, h), abw, b * D + h * 256, 256, 1)
    for j in range(2):
        plan_rows(("about", j), I["ab_w_out_2"][0, j * D:(j + 1) * D, :], 8, 4)
    for j in range(3):
        plan_cols(("mod2", 1, j), I["w_mod_2"][1], j * D, D, 4)
    cw = I["c_w_in_2"][0]
    plan_cols(("cq",), cw, 0, D, 4)
    plan_cols(("ckv",), cw, D, 512, 2)
    plan_cols(("cz",), cw, D + 512, D, 4)
    plan_rows(("cout",), I["c_w_out_2"][0], 8, 4)

    npar = [0]

    def pdma(dst, src, slow=False):
        nc.scalar.dma_start(dst, src, allow_slow_non_contiguous=slow).then_inc(s_par, 16)
        npar[0] += 16

    def dcols(v):
        return v.rearrange("(p k) -> p k", k=8)

    pdma(cst[:, :], consts)
    xin = hT[:, 0:2048].rearrange("p (i d) -> p i d", i=2)
    cin = hT[:, 2048:4096].rearrange("p (i d) -> p i d", i=2)
    nc.scalar.dma_start(xin, I["x"][0].rearrange("(i p) d -> p i d", p=P)).then_inc(s_x, 16)
    nc.scalar.dma_start(cin, I["ctx_2"][0].rearrange("(i p) d -> p i d", p=P)).then_inc(s_x, 16)
    craw = pcol(24).rearrange("p (c k) -> p c k", c=3)
    pdma(craw[:, 0, :], dcols(I["c"][0]))
    pdma(craw[:, 1, :], dcols(I["c_ctx_2"]))
    pdma(craw[:, 2, :], dcols(I["c_2"][0]))
    bmod = [pcol(48).rearrange("p (j k) -> p j k", j=6) for _ in range(LAYERS)]
    gmix, gffn, bprb = [], [], []
    lamrow = carve(8, 64)
    brow = [pcol(64) for _ in range(LAYERS)]
    for l in range(LAYERS):
        pdma(bmod[l], I["b_mod"][l].rearrange("(j p k) -> p j k", j=6, k=8))
        for lst, n in ((gmix, "norm_mix_g"), (gffn, "norm_ffn_g"), (bprb, "b_proj_b")):
            lst.append(pcol(8))
            pdma(lst[l], dcols(I[n][l]))
        for q, n in enumerate(("lam_q1", "lam_k1", "lam_q2", "lam_k2")):
            pdma(lamrow[:, 4 * l + q, :], I[n][l].partition_broadcast(P))
        pdma(brow[l], I["b_router"][l].partition_broadcast(P))
    bmod2, gpre, gpost = [], [], []
    for l in range(2):
        bmod2.append(pcol(24).rearrange("p (j k) -> p j k", j=3))
        pdma(bmod2[l], I["b_mod_2"][l].rearrange("(j p k) -> p j k", j=3, k=8))
        for lst, n in ((gpre, "g_pre_2"), (gpost, "g_post_2")):
            lst.append(pcol(8))
            pdma(lst[l], dcols(I[n][l]))
    bgate = pcol(4)
    pdma(bgate[0:4, :], I["ab_b_gate_2"][0].rearrange("(t h) -> h t", t=4), True)
    sink = pcol(16)
    pdma(sink, I["c_sink_2"][0].partition_broadcast(P))
    posi = carve(256)
    pdma(posi.bitcast(I32), I["positions"][0].partition_broadcast(P))
    for l in range(LAYERS):
        pdma(rows[0:124, l, :], I["w_dw"][l].rearrange("k (c q) -> (k c) q", q=P))
    misc = []
    at = [0]

    def prow(key, src):
        n = src.shape[0]
        pdma(rows[at[0]:at[0] + n, 2, 0:src.shape[1]], src)
        misc.append((key, at[0], n))
        at[0] += n

    prow("conv", I["ab_conv_2"][0].rearrange("j (c q) -> (j c) q", q=P))
    for l in range(LAYERS):
        for n in ("b_dw", "conv_ln_g", "conv_ln_b"):
            prow((n, l), I[n][l].rearrange("(c q) -> c q", q=P))
        prow(("subln_g", l), I["subln_g"][l].rearrange("(c q) -> c q", q=P))
    prow("mnorm", I["ab_mnorm_2"][0].rearrange("(c q) -> c q", q=P))
    prow("pscale", I["ab_pool_scale_2"][0].rearrange("(c q) -> c q", q=P))
    for l in range(LAYERS):
        for n in ("qn_g", "kn_g"):
            r0 = at[0]
            pdma(rows[r0:r0 + 1, 2, 64:128], I[n][l].rearrange("(c q) -> c q", c=1))
            prow((n, l), I[n][l].rearrange("(c q) -> c q", c=1))
    NR = at[0]
    m_par = (s_par, npar[0], "par")
    m_x = (s_x, 32, "x")
    ring.pump()

    wdw = [sb(f"wdw{l}", [P, 124]) for l in range(LAYERS)]
    pmisc = sb("pmisc", [P, P])
    m_prm = []
    for l in range(LAYERS):
        b = banks.take()
        m = tr(b.t[:, 0:124], rows[0:124, l, :], ident[0:124, 0:124], [m_par] + b.w)
        m = V(ve.tensor_copy, [m], wdw[l][:, :], b.t[:, 0:124])
        b.free(m)
        m_prm.append(m)
    b = banks.take()
    m = tr(b.t[:, 0:NR], rows[0:NR, 2, :], ident[0:NR, 0:NR], [m_par] + b.w)
    m = V(ve.tensor_copy, [m], pmisc[:, 0:NR], b.t[:, 0:NR])
    b.free(m)
    m_prm.append(m)
    PM = {k: pmisc[:, o:o + n] for k, o, n in misc}
    for e in (A, V, G, T):
        e.wait([m_par] + m_prm)

    for src, c0 in ((cin, 0), (xin, 256)):
        for i in range(2):
            for k0 in (0, 4):
                b = banks.take()
                T.wait([m_x] + b.w)
                for k in range(k0, k0 + 4):
                    ins = te.transpose(b.t[:, (k - k0) * P:(k - k0 + 1) * P], src[:, i, k::8], ident)
                m = T.done(ins)
                m = A(ac.activation, [m], xT[:, k0:k0 + 4, c0 + i * P:c0 + (i + 1) * P],
                      b.t[:, :].rearrange("p (k t) -> p k t", k=4), ACT.Copy)
                b.free(m)
    cosT = sb("cosT", [P, 256])
    sinT = sb("sinT", [P, 256])
    posf, ang, rn, t0 = carve(256), carve(256), carve(256), carve(256)
    TWO_PI = 2.0 * math.pi
    C1 = 6.28125
    C2 = 0.00193500518798828125
    C3 = TWO_PI - C1 - C2
    MAGIC = 1.5 * 2.0 ** 23
    HALF = 3.1415925
    m = V(ve.tensor_copy, [], posf, posi.bitcast(I32))
    m = V(ve.tensor_scalar, [m], ang, posf, C("inv"), None, ALU.mult)
    m = V(ve.tensor_scalar, [m], rn, ang, 1.0 / TWO_PI, MAGIC, ALU.mult, ALU.add)
    m = V(ve.tensor_scalar, [m], rn, rn, MAGIC, None, ALU.subtract)
    for cc in (C1, C2, C3):
        m = V(ve.scalar_tensor_tensor, [m], ang, rn, -cc, ang, ALU.mult, ALU.add)
    m = V(ve.tensor_scalar, [m], ang, ang, HALF, -HALF, ALU.min, ALU.max)
    ms = A(ac.activation, [m], sinT[:, :], ang, ACT.Sin)
    m = V(ve.tensor_scalar, [m], rn, ang, math.pi / 2, None, ALU.add)
    m = V(ve.tensor_scalar, [m], t0, rn, math.pi, -TWO_PI, ALU.is_gt, ALU.mult)
    m = V(ve.tensor_tensor, [m], rn, rn, t0, ALU.add)
    m = V(ve.tensor_scalar, [m], rn, rn, HALF, -HALF, ALU.min, ALU.max)
    A(ac.activation, [m], cosT[:, :], rn, ACT.Sin)
    neglam = [pcol(1) for _ in range(LAYERS)]
    lams = pcol(4)
    for l in range(LAYERS):
        for q in range(2):
            m = V(ve.tensor_tensor, [], lamrow[:, 4 * l + 2 * q, :], lamrow[:, 4 * l + 2 * q, :],
                  lamrow[:, 4 * l + 2 * q + 1, :], ALU.mult)
            m = V(ve.tensor_reduce, [m], lams[:, 2 * l + q:2 * l + q + 1], lamrow[:, 4 * l + 2 * q, :], AX, ALU.add)
    lexp = pcol(4)
    m = A(ac.activation, [m], lexp, lams, ACT.Exp)
    lam_init = [0.8 - 0.6 * math.exp(-0.3 * l) for l in range(LAYERS)]
    sublnS = [pcol(1) for _ in range(LAYERS)]
    for l in range(LAYERS):
        m2 = V(ve.tensor_tensor, [m], neglam[l], lexp[:, 2 * l + 1:2 * l + 2], lexp[:, 2 * l:2 * l + 1], ALU.subtract)
        V(ve.tensor_scalar, [m2], neglam[l], neglam[l], -lam_init[l], None, ALU.add)
        V(ve.tensor_scalar, [], sublnS[l], PM[("subln_g", l)], 1.0 - lam_init[l], None, ALU.mult)
    cact = pcol(24).rearrange("p (c k) -> p c k", c=3)
    A(ac.activation, [], cact, craw, ACT.Silu)

    def rstd(src_ps, dst, n, waits):
        m = V(ve.tensor_scalar, waits, dst, src_ps, 1.0 / n, EPS, ALU.mult, ALU.add)
        m = V(ve.reciprocal, [m], dst, dst)
        return A(ac.activation, [m], dst, dst, ACT.Sqrt)

    def modulation(key, bias, ncol, cvec, dst):
        for j in range(bias.shape[1]):
            flat, ml = ring.get(key + (j,))
            w = flat.rearrange("p (k n) -> p k n", k=8)
            b = banks.take()
            for k in range(8):
                m = mm(b.t[:, k * ncol:(k + 1) * ncol], [(w[:, kk, k::8], cvec[kk]) for kk in range(8)],
                       [ml] + b.w)
            ring.release(key + (j,), m)
            for c in range(ncol):
                o = dst[:, c, j, :]
                src = b.t[:, 0:8 * ncol].rearrange("p (k c) -> p k c", c=ncol)[:, :, c]
                m2 = V(ve.tensor_tensor, [m], o, src, bias[:, j, :], ALU.add)
            b.free(m2)
        return m2

    def norm_modulate(cols, h, scale, shift, sq_t, r_t):
        c0, c1 = cols
        n = c1 - c0
        ms = A(ac.activation, [], sq_t, xT[:, :, c0:c1], ACT.Square)
        b = banks.take()
        m = mm(b.t[:, 0:n], [(ones, sq_t[:, k, :]) for k in range(8)], [ms] + b.w)
        mr = rstd(b.t[:, 0:n], r_t, D, [m])
        b.free(mr)
        for k in range(8):
            for s in range(n // 256):
                seg = slice(s * 256, (s + 1) * 256)
                m = V(ve.scalar_tensor_tensor, [mr], h[:, k, seg], xT[:, k, c0 + s * 256:c0 + (s + 1) * 256],
                      scale[s][:, k:k + 1], r_t[:, seg], ALU.mult, ALU.mult)
                mh = A(ac.activation, [m], h[:, k, seg], h[:, k, seg], ACT.Identity, bias=shift[s][:, k:k + 1])
        return mh

    XC = (256, 512)
    for l in range(LAYERS):
        first_layer(nc, locals(), l)
    second_block(nc, locals())


def first_layer(nc, S, l):
    V, A, T, G = S["V"], S["A"], S["T"], S["G"]
    te, ac, ve, gp = nc.tensor, nc.scalar, nc.vector, nc.gpsimd
    mm, tr, C, carve, reset, banks, ring, rstd = (S["mm"], S["tr"], S["C"], S["carve"], S["reset"], S["banks"],
                                                  S["ring"], S["rstd"])
    I, PM, hT, xT, ident, ones = S["I"], S["PM"], S["hT"], S["xT"], S["ident"], S["ones"]
    reset()
    h = hT[:, 0:2048].rearrange("p (k t) -> p k t", k=8)
    merged = hT[:, 2048:4096].rearrange("p (k t) -> p k t", k=8)
    mod = carve(1, 6, 8)
    m_mod = S["modulation"](("mod", l), S["bmod"][l], 1, [S["cact"][:, 0, kk:kk + 1] for kk in range(8)], mod)
    amix, affn = carve(8), carve(8)
    m1 = V(ve.scalar_tensor_tensor, [m_mod], amix, mod[:, 0, 1, :], 1.0, S["gmix"][l], ALU.add, ALU.mult)
    m2 = V(ve.scalar_tensor_tensor, [m_mod], affn, mod[:, 0, 4, :], 1.0, S["gffn"][l], ALU.add, ALU.mult)
    A.wait([m1, m2])
    V.wait([m1, m2])
    keep = S["top"][0]
    sq_t, r_t = carve(8, 256), carve(256)
    m_h = S["norm_modulate"](S["XC"], h, [amix], [mod[:, 0, 0, :]], sq_t, r_t)
    S["barrier"]()
    S["top"][0] = keep

    qR, kR = carve(4, 256), carve(4, 256)
    va, vc = carve(2, 512), carve(2, 512)
    hpad = carve(4, 286)
    acc = carve(4, 256)
    qc, kc = merged[:, 0:4, :], merged[:, 4:8, :]
    keep = S["top"][0]
    r_a, r_sq, r_t1, r_r = [Rot([carve(2, 256) for _ in range(2)]) for _ in range(4)]
    cosB = S["cosT"][:, :].unsqueeze(1).to_broadcast([P, 2, 256])
    sinB = S["sinT"][:, :].unsqueeze(1).to_broadcast([P, 2, 256])
    m_zero = G(gp.memset, [], hpad[:, :, 0:30], 0.0)

    flat, ml = ring.get(("in", l, 0))
    w = flat.rearrange("p (k n) -> p k n", k=8)
    m_rope = None
    for half, (dst, gname) in enumerate(((qR, "qn_g"), (kR, "kn_g"))):
        g = PM[(gname, l)]
        for pr in range(2):
            b = banks.take()
            for c in range(2):
                c0 = half * 512 + (2 * pr + c) * P
                m = mm(b.t[:, c * 256:(c + 1) * 256], [(w[:, kk, c0:c0 + P], h[:, kk, :]) for kk in range(8)],
                       [ml, m_h] + b.w)
            if half == 1 and pr == 1:
                ring.release(("in", l, 0), m)
            ps = b.t[:, :].rearrange("p (c t) -> p c t", c=2)
            qa, sq, t1, rr = r_a.take(), r_sq.take(), r_t1.take(), r_r.take()
            ma = A(ac.activation, [m] + qa.w, qa.t, ps, ACT.Copy, scale=g)
            mq = A(ac.activation, [m] + sq.w, sq.t, ps, ACT.Square)
            b.free(ma, mq)
            bs, bw = banks.take(), banks.take()
            m_ss = mm(bs.t[:, :], [(C("blk64"), sq.t)], [mq] + bs.w)
            sq.free(m_ss)
            m_sw = mm(bw.t[:, :], [(C("swap_half"), qa.t)], [ma] + bw.w)
            pss = bs.t[:, :].rearrange("p (c t) -> p c t", c=2)
            psw = bw.t[:, :].rearrange("p (c t) -> p c t", c=2)
            V.wait(rr.w)
            mr = rstd(pss, rr.t, 64, [m_ss])
            bs.free(mr)
            mt = V(ve.tensor_tensor, [m_sw] + t1.w, t1.t, psw, sinB, ALU.mult)
            bw.free(mt)
            mb = G(gp.tensor_tensor, [ma, m_sw], qa.t, qa.t, cosB, ALU.mult)
            mt = V(ve.tensor_tensor, [mt, mb], t1.t, t1.t, qa.t, ALU.add)
            qa.free(mt)
            m_rope = V(ve.tensor_tensor, [mt, mr], dst[:, 2 * pr:2 * pr + 2, :], t1.t, rr.t, ALU.mult)
            t1.free(m_rope)
            rr.free(m_rope)

    flat, ml = ring.get(("in", l, 1))
    w = flat.rearrange("p (k n) -> p k n", k=8)
    for i in range(2):
        b = banks.take()
        m = mm(b.t[:, :], [(h[:, kk, i * P:(i + 1) * P], w[:, kk, 0:512]) for kk in range(8)], [ml] + b.w)
        m_va = A(ac.activation, [m], va[:, i, :], b.t[:, :], ACT.Copy)
        b.free(m_va)
    for pr in range(2):
        b = banks.take()
        for c in range(2):
            c0 = 512 + (2 * pr + c) * P
            m = mm(b.t[:, c * 256:(c + 1) * 256], [(w[:, kk, c0:c0 + P], h[:, kk, :]) for kk in range(8)], b.w)
        m_ua = A(ac.activation, [m], hpad[:, 2 * pr:2 * pr + 2, 30:286],
                 b.t[:, :].rearrange("p (c t) -> p c t", c=2), ACT.Copy)
        b.free(m_ua)
    ring.release(("in", l, 1), m)
    flat, ml = ring.get(("in", l, 2))
    w = flat.rearrange("p (k n) -> p k n", k=8)
    m_glu = []
    for pr in range(2):
        b = banks.take()
        for c in range(2):
            c0 = (2 * pr + c) * P
            m = mm(b.t[:, c * 256:(c + 1) * 256], [(w[:, kk, c0:c0 + P], h[:, kk, :]) for kk in range(8)],
                   [ml] + b.w)
        sg = r_sq.take()
        ms = A(ac.activation, [m] + sg.w, sg.t, b.t[:, :].rearrange("p (c t) -> p c t", c=2), ACT.Sigmoid)
        b.free(ms)
        hp = hpad[:, 2 * pr:2 * pr + 2, 30:286]
        mg = V(ve.tensor_tensor, [ms, m_ua], hp, hp, sg.t, ALU.mult)
        sg.free(mg)
        m_glu.append(mg)
    for dst, blk, off in ((qc, 2, 512), (kc, 3, 0)):
        if blk == 3:
            ring.release(("in", l, 2), m)
            flat, ml = ring.get(("in", l, 3))
            w = flat.rearrange("p (k n) -> p k n", k=8)
        for pr in range(2):
            b = banks.take()
            for c in range(2):
                c0 = off + (2 * pr + c) * P
                m = mm(b.t[:, c * 256:(c + 1) * 256], [(w[:, kk, c0:c0 + P], h[:, kk, :]) for kk in range(8)],
                       [ml] + b.w)
            m_qk = A(ac.activation, [m], dst[:, 2 * pr:2 * pr + 2, :],
                     b.t[:, :].rearrange("p (c t) -> p c t", c=2), ACT.Copy)
            b.free(m_qk)
    for i in range(2):
        b = banks.take()
        m = mm(b.t[:, :], [(h[:, kk, i * P:(i + 1) * P], w[:, kk, 512:1024]) for kk in range(8)], [ml] + b.w)
        m_vc = A(ac.activation, [m], vc[:, i, :], b.t[:, :], ACT.Copy)
        b.free(m_vc)
    ring.release(("in", l, 3), m)

    wd = S["wdw"][l]
    mc = [None] * 4
    V.wait([m_zero] + m_glu)
    conv_steps = []
    for k in range(31):
        for c in range(4):
            conv_steps.append((k, c))

    def conv(n):
        for _ in range(min(n, len(conv_steps))):
            k, c = conv_steps.pop(0)
            tap = wd[:, k * 4 + c:k * 4 + c + 1]
            if k == 0:
                mc[c] = V(ve.tensor_scalar, [], acc[:, c, :], hpad[:, c, 0:256], tap, PM[("b_dw", l)][:, c:c + 1],
                          ALU.mult, ALU.add)
            else:
                mc[c] = V(ve.scalar_tensor_tensor, [mc[c]], acc[:, c, :], hpad[:, c, k:k + 256], tap, acc[:, c, :],
                          ALU.mult, ALU.add)

    S["barrier"]()
    S["top"][0] = keep
    oa, oc = carve(4, 256), carve(4, 256)
    f_s = Rot([carve(2, 256) for _ in range(2)])
    f_a = Rot([carve(1, 256) for _ in range(2)])
    f_st = Rot([carve(8) for _ in range(4)])
    f_at = Rot([carve(3, P) for _ in range(2)])
    f_o = Rot([carve(256) for _ in range(2)])
    f_r = Rot([carve(256) for _ in range(2)])
    mask = C("causal")

    def diff_head(hd):
        at = f_at.take()
        for i in range(2):
            K = (i + 1) * P
            s, st = f_s.take(), f_st.take()
            for mp in range(2):
                b = banks.take()
                m = mm(b.t[:, 0:K],
                       [(qR[mp * 64:mp * 64 + 64, hd, i * P:(i + 1) * P], kR[mp * 64:mp * 64 + 64, hd, 0:K])], b.w)
                m = V(ve.scalar_tensor_tensor, [m] + s.w, s.t[:, mp, 0:K], b.t[:, 0:K], 0.125, mask[:, 256 - K:256],
                      ALU.mult, ALU.add)
                b.free(m)
            m = V(ve.tensor_reduce, [m] + st.w, st.t[:, 0:2], s.t[:, :, 0:K], AX, ALU.max)
            m = V(ve.tensor_scalar, [m], st.t[:, 2:4], st.t[:, 0:2], -1.0, None, ALU.mult)
            for mp in range(2):
                me = A(ac.activation, [m], s.t[:, mp, 0:K], s.t[:, mp, 0:K], ACT.Exp, bias=st.t[:, 2 + mp:3 + mp],
                       accum_out=st.t[:, 4 + mp:5 + mp])
            m = V(ve.reciprocal, [me], st.t[:, 6:8], st.t[:, 4:6])
            a = f_a.take()
            m2 = V(ve.tensor_scalar, [m] + a.w, a.t[:, 0, 0:K], s.t[:, 0, 0:K], st.t[:, 6:7], None, ALU.mult)
            m1 = V(ve.tensor_tensor, [m], st.t[:, 7:8], st.t[:, 7:8], S["neglam"][l], ALU.mult)
            m = V(ve.scalar_tensor_tensor, [m1, m2], a.t[:, 0, 0:K], s.t[:, 1, 0:K], st.t[:, 7:8], a.t[:, 0, 0:K],
                  ALU.mult, ALU.add)
            s.free(m)
            st.free(m)
            b = banks.take()
            for kb in range(i + 1):
                mt = tr(b.t[:, kb * P:(kb + 1) * P], a.t[:, 0, kb * P:(kb + 1) * P], ident, [m] + b.w)
            a.free(mt)
            m_at = A(ac.activation, [mt] + at.w, at.t[:, i:2 * i + 1, :],
                     b.t[:, 0:K].rearrange("p (k t) -> p k t", k=i + 1), ACT.Copy)
            b.free(m_at)
        b = banks.take()
        vv = [va[:, kb, hd * P:(hd + 1) * P] for kb in range(2)]
        mm(b.t[:, 0:P], [(vv[0], at.t[:, 0, :])], [m_at] + b.w)
        m = mm(b.t[:, P:256], [(vv[0], at.t[:, 1, :]), (vv[1], at.t[:, 2, :])], [])
        at.free(m)
        o, r = f_o.take(), f_r.take()
        msq = A(ac.activation, [m] + o.w, o.t, b.t[:, 0:256], ACT.Square)
        b2 = banks.take()
        m2 = mm(b2.t[:, 0:256], [(ones, o.t)], [msq] + b2.w)
        o.free(m2)
        V.wait(r.w)
        mr = rstd(b2.t[:, 0:256], r.t, P, [m2])
        b2.free(mr)
        m = V(ve.scalar_tensor_tensor, [mr, m], oa[:, hd, :], b.t[:, 0:256], S["sublnS"][l], r.t, ALU.mult, ALU.mult)
        r.free(m)
        b.free(m, msq)
        return m

    f_z = Rot([carve(384) for _ in range(2)])
    f_e = Rot([carve(384) for _ in range(2)])
    bef = C("before")

    def stick_pair(c):
        bo = banks.take()
        wo = list(bo.w)
        for u in range(2):
            hd, base = 2 * c + u, u * 64
            b = banks.take()
            kk, qq = kc[base:base + 64, c, :], qc[base:base + 64, c, :]
            mm(b.t[:, 0:256], [(kk[:, 0:P], qq)], b.w)
            m = mm(b.t[:, 256:384], [(kk[:, P:256], qq[:, P:256])], [])
            z, e = f_z.take(), f_e.take()
            mz = V(ve.scalar_tensor_tensor, [m] + z.w, z.t, b.t[:, 0:384], 0.125, bef, ALU.mult, ALU.add)
            b.free(mz)
            m = A(ac.activation, [mz] + e.w, e.t, z.t, ACT.Abs)
            m = A(ac.activation, [m], e.t, e.t, ACT.Exp, scale=-1.0)
            m = A(ac.activation, [m], e.t, e.t, ACT.Ln, bias=ones[:, 0:1])
            m = V(ve.scalar_tensor_tensor, [m], e.t, z.t, 0.0, e.t, ALU.max, ALU.add)
            b = banks.take()
            mm(b.t[:, 256:384], [(C("from_s"), e.t[:, 256:384])], [m] + b.w)
            mm(b.t[:, 0:P], [(C("from_s"), e.t[:, 0:P])], [])
            ms = mm(b.t[:, P:256], [(C("from_s"), e.t[:, P:256]), (ones, e.t[:, 256:384])], [])
            m = V(ve.tensor_tensor, [ms], z.t, z.t, b.t[:, 0:384], ALU.subtract)
            b.free(m)
            m = A(ac.activation, [m], e.t, z.t, ACT.Exp)
            z.free(m)
            o = bo.t[base:base + 64, :]
            vv = [vc[:, j, hd * 64:(hd + 1) * 64] for j in range(2)]
            mm(o[:, 0:P], [(vv[0], e.t[:, 0:P])], [m] + wo)
            m = mm(o[:, P:256], [(vv[0], e.t[:, P:256]), (vv[1], e.t[:, 256:384])], [])
            e.free(m)
        m = A(ac.activation, [m], oc[:, c, :], bo.t[:, 0:256], ACT.Copy)
        bo.free(m)
        return m

    for c in range(4):
        m_oa = diff_head(c)
        conv(16)
        m_oc = stick_pair(c)
        conv(15)
    conv(999)
    lnm, lnr = f_o.take(), f_r.take()
    b = banks.take()
    m = mm(b.t[:, 0:256], [(ones, acc[:, c, :]) for c in range(4)], mc + b.w)
    m = A(ac.activation, [m] + lnm.w, lnm.t, b.t[:, 0:256], ACT.Copy, scale=1.0 / 512)
    b.free(m)
    m = V(ve.tensor_tensor, [m], acc, acc, lnm.t.unsqueeze(1).to_broadcast([P, 4, 256]), ALU.subtract)
    lnm.free(m)
    ob = hpad[:, :, 0:256]
    msq = A(ac.activation, [m], ob, acc, ACT.Square)
    b = banks.take()
    m2 = mm(b.t[:, 0:256], [(ones, ob[:, c, :]) for c in range(4)], [msq] + b.w)
    V.wait(lnr.w)
    mr = rstd(b.t[:, 0:256], lnr.t, 512, [m2])
    b.free(mr)
    m = V(ve.tensor_tensor, [mr], acc, acc, lnr.t.unsqueeze(1).to_broadcast([P, 4, 256]), ALU.mult)
    lnr.free(m)
    A.wait([m2])
    for c in range(4):
        m_ob = A(ac.activation, [m], ob[:, c, :], acc[:, c, :], ACT.Silu, bias=PM[("conv_ln_b", l)][:, c:c + 1],
                 scale=PM[("conv_ln_g", l)][:, c:c + 1])

    S["barrier"]()
    S["top"][0] = 64
    f_g = Rot([carve(256) for _ in range(3)])
    f_y = Rot([carve(256) for _ in range(3)])
    m_mrg = [None] * 8
    for br, (o, mo) in enumerate(((oa, m_oa), (ob, m_ob), (oc, m_oc))):
        flat, ml = ring.get(("in", l, 4 + br))
        w = flat.rearrange("p (k n) -> p k n", k=8)
        pflat, mp = ring.get(("proj", l, br))
        pw = pflat.rearrange("p (c n) -> p c n", c=4)
        for k in range(8):
            b = banks.take()
            mm(b.t[:, 0:256], [(w[:, kk, k::8], h[:, kk, :]) for kk in range(8)], [ml] + b.w)
            my = mm(b.t[:, 256:512], [(pw[:, c, k::8], o[:, c, :]) for c in range(4)], [mp, mo])
            sg = f_g.take()
            ms = A(ac.activation, [my] + sg.w, sg.t, b.t[:, 0:256], ACT.Sigmoid)
            if br == 0:
                m = V(ve.tensor_tensor, [ms, my], merged[:, k, :], sg.t, b.t[:, 256:512], ALU.mult)
                m_mrg[k] = m
            else:
                y = f_y.take()
                if br == 1:
                    m = V(ve.scalar_tensor_tensor, [ms, my] + y.w, y.t, b.t[:, 256:512], S["bprb"][l][:, k:k + 1],
                          sg.t, ALU.add, ALU.mult)
                else:
                    m = V(ve.tensor_tensor, [ms, my] + y.w, y.t, sg.t, b.t[:, 256:512], ALU.mult)
                m_mrg[k] = G(gp.tensor_tensor, [m, m_mrg[k]], merged[:, k, :], merged[:, k, :], y.t, ALU.add)
                y.free(m_mrg[k])
            sg.free(m)
            b.free(m, ms)
        ring.release(("in", l, 4 + br), my)
        ring.release(("proj", l, br), my)
    flat, ml = ring.get(("out", l))
    w = flat.rearrange("p (k n) -> p k n", k=8)
    for k in range(8):
        b = banks.take()
        m = mm(b.t[:, 0:256], [(w[:, kk, k::8], merged[:, kk, :]) for kk in range(8)], [ml] + m_mrg + b.w)
        mv = V(ve.scalar_tensor_tensor, [m], xT[:, k, 256:512], b.t[:, 0:256], mod[:, 0, 2, k:k + 1],
               xT[:, k, 256:512], ALU.mult, ALU.add)
        b.free(mv)
    ring.release(("out", l), m)

    S["barrier"]()
    S["top"][0] = 64
    sq_t, r_t = carve(8, 256), carve(256)
    m_h = S["norm_modulate"](S["XC"], h, [affn], [mod[:, 0, 3, :]], sq_t, r_t)
    moe(nc, S, l, h, m_h, mod)


def route(nc, S, l, h, m, b):
    V, A, T = S["V"], S["A"], S["T"]
    ac, ve = nc.scalar, nc.vector
    mm, C, carve = S["mm"], S["C"], S["carve"]
    ones, ident, iota = S["ones"], S["ident"], C("iota")
    mk, posm = carve(2, 64), carve(2, 64)
    e_x, t_x = carve(MORE), carve(MORE)
    e_int, n_int = S["pcol"](MORE).bitcast(I32), S["pcol"](1).bitcast(I32)
    keep = S["top"][0]
    sc, bi, rep = carve(2, 64), carve(2, 64), carve(2, 64)
    s8, gs, rank = carve(16, 8), carve(2, 8), carve(2, 8)
    cmp1, cmp2 = carve(2, 8, 8), carve(2, 8, 8)
    top8, den = carve(2, 8), carve(2)
    ms = A(ac.activation, [m], sc, b.t[:, 0:128].rearrange("p (i e) -> p i e", i=2), ACT.Sigmoid)
    b.free(ms)
    m = V(ve.tensor_tensor, [ms], bi, sc, S["brow"][l].unsqueeze(1).to_broadcast([P, 2, 64]), ALU.add)
    for q in range(16):
        m2 = V(ve.max, [m], s8[:, q, :], bi[:, q // 8, (q % 8) * 8:(q % 8) * 8 + 8])
    m = V(ve.tensor_tensor, [m2], gs.rearrange("p i g -> p (i g)"), s8[:, :, 0], s8[:, :, 1], ALU.add)
    tri8 = C("tri8").rearrange("p (a b) -> p a b", a=8)
    both = []
    for i in range(2):
        ga = gs[:, i, :].unsqueeze(2).to_broadcast([P, 8, 8])
        gb = gs[:, i, :].unsqueeze(1).to_broadcast([P, 8, 8])
        m1 = V(ve.tensor_tensor, [m], cmp1[:, i], gb, ga, ALU.is_gt)
        m2 = V(ve.tensor_tensor, [m], cmp2[:, i], gb, ga, ALU.is_equal)
        m2 = V(ve.tensor_tensor, [m2], cmp2[:, i], cmp2[:, i], tri8, ALU.mult)
        m2 = V(ve.tensor_tensor, [m1, m2], cmp1[:, i], cmp1[:, i], cmp2[:, i], ALU.add)
        m2 = V(ve.tensor_reduce, [m2], rank[:, i, :], cmp1[:, i], AX, ALU.add)
        m2 = V(ve.tensor_scalar, [m2], gs[:, i, :], rank[:, i, :], 3.5, None, ALU.is_lt)
        gm = gs[:, i, :].unsqueeze(2).to_broadcast([P, 8, 8])
        bv = bi[:, i, :].rearrange("p (g e) -> p g e", g=8)
        mv = mk[:, i, :].rearrange("p (g e) -> p g e", g=8)
        m1 = V(ve.tensor_tensor, [m2], mv, bv, gm, ALU.mult)
        m2 = V(ve.tensor_scalar, [m2], rank[:, i, :], gs[:, i, :], 1.0, 1.0e30, ALU.subtract, ALU.mult)
        m2 = V(ve.tensor_tensor, [m1, m2], mv, mv, rank[:, i, :].unsqueeze(2).to_broadcast([P, 8, 8]), ALU.add)
        m2 = V(ve.max, [m2], top8[:, i, :], mk[:, i, :])
        m2 = V(ve.match_replace, [m2], rep[:, i, :], top8[:, i, :], mk[:, i, :], -3.0e38)
        both.append(V(ve.tensor_tensor, [m2], rep[:, i, :], mk[:, i, :], rep[:, i, :], ALU.not_equal))
    m = both[1]
    m_sel = m
    m = V(ve.tensor_tensor, [m], mk, rep, sc, ALU.mult)
    m = V(ve.tensor_reduce, [m], den, mk, AX, ALU.add)
    m = V(ve.tensor_scalar, [m], den, den, 1e-20, None, ALU.add)
    m = V(ve.reciprocal, [m], den, den)
    for i in range(2):
        m_w = V(ve.tensor_scalar, [m], mk[:, i, :], mk[:, i, :], den[:, i:i + 1], 2.5, ALU.mult, ALU.mult)
    below = carve(P)
    m_b = V(ve.tensor_tensor, [], below, ones, C("from_s"), ALU.subtract)
    mm(b.t[:, 0:64], [(below, rep[:, 0, :])], [m_sel, m_b] + b.w)
    mm(b.t[:, 64:128], [(ones, rep[:, 0, :]), (below, rep[:, 1, :])], [])
    m = mm(b.t[0:64, 128:129], [(rep[:, i, :], ones[:, 0:1]) for i in range(2)], [])
    m1 = V(ve.scalar_tensor_tensor, [m], posm, b.t[:, 0:128].rearrange("p (i e) -> p i e", i=2), 1.0, rep,
           ALU.add, ALU.mult)
    m_p = V(ve.tensor_scalar, [m1], posm, posm, -1.0, None, ALU.add)
    nb, t1, upto = carve(1), carve(1), carve(64)
    m = V(ve.tensor_scalar, [m], nb[0:64, :], b.t[0:64, 128:129], SLOTS + 0.5, None, ALU.is_gt)
    for q in (2, 3):
        m1 = V(ve.tensor_scalar, [], t1[0:64, :], b.t[0:64, 128:129], q * SLOTS + 0.5, None, ALU.is_gt)
        m = V(ve.tensor_tensor, [m, m1], nb[0:64, :], nb[0:64, :], t1[0:64, :], ALU.add)
        V.wait([m])
    m1 = V(ve.tensor_tensor, [m_b], upto[0:64, :], below[0:64, 0:64], ident[0:64, 0:64], ALU.add)
    b.free(m)
    nrow = nb[0:64, 0:1].to_broadcast([64, P])
    mm(b.t[:, 0:64], [(nrow, below[0:64, 0:64])], [m, m1, m_p] + b.w)
    m = mm(b.t[:, 64:128], [(nrow, upto[0:64, :])], [])
    se = carve(2, 64)
    m = V(ve.tensor_copy, [m], se, b.t[:, 0:128].rearrange("p (a e) -> p a e", a=2))
    b.free(m)
    V.wait([m])
    nrow = carve(64)
    m_n = V(ve.tensor_tensor, [], nrow, se[:, 1, :], se[:, 0, :], ALU.subtract)
    over = carve(MORE, 64)
    m = V(ve.tensor_tensor, [], over, se[:, 1, :].unsqueeze(1).to_broadcast([P, MORE, 64]),
          iota[:, 0:MORE].unsqueeze(2).to_broadcast([P, MORE, 64]), ALU.is_le)
    m1 = V(ve.tensor_reduce, [m], e_x, over, AX, ALU.add)
    m = V(ve.tensor_tensor, [m, m1, m_n], over, over, nrow.unsqueeze(1).to_broadcast([P, MORE, 64]), ALU.mult)
    m = V(ve.tensor_reduce, [m], t_x, over, AX, ALU.add)
    m = V(ve.tensor_tensor, [m], t_x, iota[:, 0:MORE], t_x, ALU.subtract)
    m = V(ve.tensor_scalar, [m], t_x, t_x, 1.0, float(SLOTS), ALU.add, ALU.mult)
    m1 = V(ve.tensor_scalar, [m1], e_x, e_x, float(EXPERTS - 1), None, ALU.min)
    m1 = V(ve.tensor_copy, [m1], e_int, e_x)
    m2 = V(ve.tensor_copy, [], n_int, se[:, 1, 63:64])
    return mk, posm, e_x, t_x, e_int, n_int, [m_w, m_p], [m, m1, m2], keep


def moe(nc, S, l, h, m_h, mod):
    V, A, T, SP = S["V"], S["A"], S["T"], S["SP"]
    te, ac, ve = nc.tensor, nc.scalar, nc.vector
    mm, C, carve, banks, ring, xT, ident = S["mm"], S["C"], S["carve"], S["banks"], S["ring"], S["xT"], S["ident"]
    iota, I = C("iota"), S["I"]
    S["barrier"]()
    S["top"][0] = 64
    ps = banks.bufs
    yb = [b.t for b in ps[0:4]]
    gb, ub, ob = ps[4], ps[5], ps[6:8]
    for b in ps:
        b.free()

    flat, ml = ring.get(("router", l))
    w = flat[:, 0:512].rearrange("p (k e) -> p k e", k=8)
    rb = ob[1]
    for i in range(2):
        m = mm(rb.t[:, i * 64:(i + 1) * 64], [(h[:, kk, i * P:(i + 1) * P], w[:, kk, :]) for kk in range(8)],
               [ml, m_h])
    ring.release(("router", l), m)
    m_router = m
    flat, ml = ring.get(("up", l, EXPERTS))
    w1 = flat[:, 0:UNIT].rearrange("p (k f) -> p k f", k=8)
    w3 = flat[:, UNIT:2 * UNIT].rearrange("p (k f) -> p k f", k=8)
    hx = S["hT"][:, 2048:4096].rearrange("p (i d) -> p i d", i=2)
    gs, ss = [S["ar"][:, n:n + 512].rearrange("p (j t) -> p j t", j=2) for n in (AR_COLS - 1024, AR_COLS - 512)]
    mg = []
    for j, b in enumerate((gb, ub)):
        mm(b.t[:, 0:256], [(w1[:, kk, j::2], h[:, kk, :]) for kk in range(8)], [ml])
        m = mm(b.t[:, 256:512], [(w3[:, kk, j::2], h[:, kk, :]) for kk in range(8)], [])
        ms = A(ac.activation, [m], ss[:, j, :], b.t[:, 0:256], ACT.Silu)
        mg.append(V(ve.tensor_tensor, [ms], gs[:, j, :], ss[:, j, :], b.t[:, 256:512], ALU.mult))
        b.free(mg[j])
    ring.release(("up", l, EXPERTS), m)
    for i in range(2):
        for q in range(2):
            b = (ob[0], gb, ub)[(2 * i + q) % 3]
            T.wait(b.w)
            for k in range(4):
                ins = te.transpose(b.t[:, k * P:(k + 1) * P], h[:, 4 * q + k, i * P:(i + 1) * P], ident)
            m = T.done(ins)
            m_hx = A(ac.activation, [m], hx[:, i, q * 512:(q + 1) * 512], b.t[:, :], ACT.Copy)
            b.free(m_hx)
    flat, ml = ring.get(("down", l, EXPERTS))
    w2 = flat[:, 0:UNIT].rearrange("p (j n) -> p j n", j=2)
    T.wait([ml] + mg)
    for k in range(8):
        o = yb[k // 2][:, (k % 2) * 256:(k % 2) * 256 + 256]
        for j in range(2):
            ins = te.matmul(o, w2[:, j, k::8], gs[:, j, :], start=(j == 0 and k % 2 == 0), stop=False,
                            skip_group_check=True)
    m = T.done(ins)
    ring.release(("down", l, EXPERTS), m)
    mk, posm, e_x, t_x, e_int, n_int, m_r, m_more, keep = route(nc, S, l, h, m_router, rb)

    S["top"][0] = keep
    V.wait(m_more + [V.last(), m_hx])
    f_s = Rot([carve(2, P) for _ in range(2)])
    f_w = Rot([carve(2, P) for _ in range(2)])
    x_b, u_b, g_b, o_b, t_b = Buf(carve(8, P)), Buf(carve(256)), Buf(carve(256)), Buf(carve(1024)), Buf(carve(512))
    T.wait([T.last(), V.last()])
    wbuf = [[carve(2, 2048), carve(2048)], [carve(2, 2048), S["hT"][:, 0:2048]]]
    work = Rot(None, ps[4:8])
    both = (slice(0, SLOTS), slice(SLOTS, P))

    def load_more(x, sp, waits):
        sem = S["more"][l][3][x % 2]
        sp.wait(waits)
        e = nc.sync.value_load(e_int[0:1, x:x + 1], min_val=0, max_val=EXPERTS - 1)
        a, b = wbuf[x % 2]
        for dst, n, k in ((a[:, 0, :], "w1", 8), (a[:, 1, :], "w3", 8), (b, "w2", 2)):
            src = I[n][l][bass.ds(e, 1), :, :].rearrange("a (p k) f -> p (a k f)", k=k)
            nc.sync.dma_start(dst, src).then_inc(sem, 16)
        return (sem, 48 * (x // 2 + 1), f"more{l}{x % 2}")

    def select(p):
        s, w = f_s.take(), f_w.take()
        for u in range(2):
            e = 2 * p + u
            for i in range(2):
                at = posm[:, i, e:e + 1]
                ms = V(ve.tensor_scalar, m_r + s.w, s.t[:, i, both[u]], iota, at, None, ALU.is_equal)
                mw = V(ve.tensor_scalar, w.w, w.t[:, i, both[u]], iota, at, mk[:, i, e:e + 1], ALU.is_equal,
                       ALU.mult)
        return s, ms, w, mw

    def gather(s, ms):
        m_x = []
        for q in range(2):
            b = work.take()
            T.wait([ms] + b.w)
            for k in range(4):
                c = (4 * q + k) * P
                for i in range(2):
                    ins = te.matmul(b.t[:, k * P:(k + 1) * P], hx[:, i, c:c + P], s.t[:, i, :], start=(i == 0),
                                    stop=(i == 1))
            m = T.done(ins)
            src = b.t[:, :].rearrange("p (k s) -> p k s", k=4)
            if q == 0:
                m_x.append(A(ac.activation, [m] + x_b.w, x_b.t[:, 0:4, :], src, ACT.Copy))
            else:
                m_x.append(V(ve.tensor_copy, [m] + x_b.w, x_b.t[:, 4:8, :], src))
            b.free(m_x[q])
        s.free(m)
        return m_x

    def up(p, m_x):
        b = work.take()
        T.wait(m_x + b.w)
        w = []
        for u in range(2):
            flat, ml = ring.get(("up", l, 2 * p + u))
            T.wait([ml])
            w.append(flat[:, 0:2 * UNIT].rearrange("p (m k f) -> p m k f", m=2, k=8))
        for kk in range(8):
            for u in range(2):
                ins = te.matmul(b.t[both[u], :], x_b.t[:, kk, both[u]], w[u][:, :, kk, :], start=(kk == 0),
                                stop=(kk == 7))
        m = T.done(ins)
        x_b.free(m)
        for u in range(2):
            ring.release(("up", l, 2 * p + u), m)
        ms = A(ac.activation, [m] + u_b.w, u_b.t, b.t[:, 0:256], ACT.Silu)
        m = V(ve.tensor_tensor, [ms] + g_b.w, g_b.t, u_b.t, b.t[:, 256:512], ALU.mult)
        u_b.free(m)
        b.free(m)
        return m

    def turn(mg, w, mw):
        b = work.take()
        T.wait([mg, mw] + b.w)
        for j in range(2):
            te.transpose(b.t[:, j * P:(j + 1) * P], g_b.t[:, j::2], ident)
        for i in range(2):
            ins = te.transpose(b.t[:, 256 + i * P:256 + (i + 1) * P], w.t[:, i, :], ident)
        m = T.done(ins)
        g_b.free(m)
        w.free(m)
        m = V(ve.tensor_copy, [m] + t_b.w, t_b.t, b.t[:, :])
        b.free(m)
        return m

    def down(p, mt):
        w = []
        for u in range(2):
            flat, ml = ring.get(("down", l, 2 * p + u))
            T.wait([ml])
            w.append(flat[:, 0:UNIT].rearrange("p (j n) -> p j n", j=2))
        m_o = []
        for q in range(2):
            b = work.take()
            T.wait([mt] + b.w)
            for j in range(2):
                for u in range(2):
                    ins = te.matmul(b.t[both[u], :], t_b.t[:, j * P + u * SLOTS:j * P + (u + 1) * SLOTS],
                                    w[u][:, j, q * 512:(q + 1) * 512], start=(j == 0), stop=(j == 1))
            m = T.done(ins)
            if q == 0:
                m_o.append(A(ac.activation, [m] + o_b.w, o_b.t[:, 0:512], b.t[:, :], ACT.Copy))
            else:
                m_o.append(V(ve.tensor_copy, [m] + o_b.w, o_b.t[:, 512:1024], b.t[:, :]))
            b.free(m_o[q])
        for u in range(2):
            ring.release(("down", l, 2 * p + u), m)
        return m_o

    def scatter(m_o):
        T.wait(m_o)
        for k in range(8):
            ins = te.matmul(yb[k // 2][:, (k % 2) * 256:(k % 2) * 256 + 256], o_b.t[:, k::8], t_b.t[:, 256:512],
                            start=False, stop=False, skip_group_check=True)
        m = T.done(ins)
        o_b.free(m)
        t_b.free(m)

    pairs = EXPERTS // 2
    s, ms, w, mw = select(0)
    m_x, m_o = gather(s, ms), None
    for p in range(pairs):
        mg = up(p, m_x)
        if p + 1 < pairs:
            nxt = select(p + 1)
        if m_o:
            scatter(m_o)
        mt = turn(mg, w, mw)
        if p + 1 < pairs:
            s, ms, w, mw = nxt
            m_x = gather(s, ms)
        m_o = down(p, mt)
        if p == pairs // 2:
            m_wx = [load_more(x, SP, m_more) for x in range(2)]
    scatter(m_o)

    S["barrier"]()
    SP.wait([e.last() for e in (T, A, V)])
    count = nc.values_load(n_int[0:1, 0:1], min_val=0, max_val=MORE)
    tiles = (hx, posm, mk, e_x, t_x, wbuf, f_s.bufs[0].t, f_s.bufs[1].t, f_w.bufs[0].t, f_w.bufs[1].t, x_b.t, u_b.t,
             g_b.t, o_b.t, t_b.t, yb, [b.t for b in ps[4:8]])
    for x in range(MORE):
        with nc.If(count > x):
            beyond(nc, S, l, x, m_wx[x] if x < 2 else load_more(x, SP, []), tiles)
        with nc.Else():
            pass
    for e in (T, A, V, S["G"], SP):
        e.wait(m_wx)
    for k in range(8):
        o = yb[k // 2][:, (k % 2) * 256:(k % 2) * 256 + 256]
        V(ve.scalar_tensor_tensor, [], xT[:, k, 256:512], o, mod[:, 0, 5, k:k + 1], xT[:, k, 256:512],
          ALU.mult, ALU.add)
    S["barrier"]()
    for b in banks.bufs:
        b.free()


def beyond(nc, S, l, x, m_wt, tiles):
    T, A, V = S["more"][l][0:3]
    te, ac, ve = nc.tensor, nc.scalar, nc.vector
    ident, iota = S["ident"], S["C"]("iota")
    hx, posm, mk, e_x, t_x, wbuf, s, one, w, at, xs, u, g, o, t, yb, (g0, g1, ob0, ob1) = tiles
    one, at = one[:, 0, 0:64], at[:, 0, 0:4]
    pick = o[:, 0:256].rearrange("p (a i e) -> p a i e", a=2, i=2)
    L = slice(0, SLOTS)
    m = V(ve.tensor_scalar, [], one, iota, e_x[:, x:x + 1], None, ALU.is_equal)
    for a, src in enumerate((posm, mk)):
        m1 = V(ve.tensor_tensor, [m], pick[:, a], src, one.unsqueeze(1).to_broadcast([P, 2, 64]), ALU.mult)
        m1 = V(ve.tensor_reduce, [m1], at[:, 2 * a:2 * a + 2], pick[:, a], AX, ALU.add)
    m = V(ve.tensor_scalar, [m1], at[:, 0:2], at[:, 0:2], t_x[:, x:x + 1], None, ALU.subtract)
    for i in range(2):
        V(ve.tensor_scalar, [m], s[:, i, L], iota, at[:, i:i + 1], None, ALU.is_equal)
        ms = V(ve.tensor_scalar, [], w[:, i, L], iota, at[:, i:i + 1], at[:, 2 + i:3 + i], ALU.is_equal, ALU.mult)
    T.wait([ms])
    for k in range(8):
        for i in range(2):
            ins = te.matmul(g0[:, k * SLOTS:(k + 1) * SLOTS], hx[:, i, k * P:(k + 1) * P], s[:, i, L],
                            start=(i == 0), stop=(i == 1))
    m = T.done(ins)
    m = A(ac.activation, [m], xs[:, :, L], g0[:, :].rearrange("p (k s) -> p k s", k=8), ACT.Copy)
    T.wait([m, m_wt])
    w13 = wbuf[x % 2][0].rearrange("p m (k f) -> p m k f", k=8)
    for kk in range(8):
        ins = te.matmul(g1[L, :], xs[:, kk, L], w13[:, :, kk, :], start=(kk == 0), stop=(kk == 7))
    m = T.done(ins)
    m = A(ac.activation, [m], u[L, :], g1[L, 0:256], ACT.Silu)
    m = V(ve.tensor_tensor, [m], g[L, :], u[L, :], g1[L, 256:512], ALU.mult)
    T.wait([m])
    for j in range(2):
        te.transpose(g0[:, j * SLOTS:(j + 1) * SLOTS], g[L, j::2], ident[L, L])
    m = T.done(te.transpose(g0[L, 256:384], w[:, 0, L], ident))
    m1 = T.done(te.transpose(g0[L, 384:512], w[:, 1, L], ident))
    m = V(ve.tensor_copy, [m1], t[:, 0:P], g0[:, 0:P])
    mt = V(ve.tensor_copy, [], t[L, 256:512], g0[L, 256:512])
    T.wait([m])
    w2 = wbuf[x % 2][1].rearrange("p (j n) -> p j n", j=2)
    for q, b in enumerate((ob0, ob1)):
        for j in range(2):
            ins = te.matmul(b[L, :], t[:, j * SLOTS:(j + 1) * SLOTS], w2[:, j, q * 512:(q + 1) * 512],
                            start=(j == 0), stop=(j == 1))
        m = T.done(ins)
        if q == 0:
            m0 = A(ac.activation, [m, mt], o[L, 0:512], b[L, :], ACT.Copy)
        else:
            m1 = V(ve.tensor_copy, [m], o[L, 512:1024], b[L, :])
    T.wait([m0, m1, mt])
    for k in range(8):
        ins = te.matmul(yb[k // 2][:, (k % 2) * 256:(k % 2) * 256 + 256], o[L, k::8], t[L, 256:512], start=False,
                        stop=False, skip_group_check=True)
    T.done(ins)
    for e in (T, A, V):
        e.wait([T.last(), A.last(), V.last()])
    for e in (nc.gpsimd, nc.sync):
        for src in (T, A, V):
            e.wait_ge(src.sem, src.n)


def modulate2(nc, S, l):
    V, ve, carve = S["V"], nc.vector, S["carve"]
    cact = S["cact"]
    mod = carve(2, 3, 8)
    m = S["modulation"](("mod2", l), S["bmod2"][l], 2, [cact[:, 1:3, kk] for kk in range(8)], mod)
    sc, gt = carve(2, 8), carve(2, 8)
    for s in range(2):
        m1 = V(ve.scalar_tensor_tensor, [m], sc[:, s, :], mod[:, s, 1, :], 1.0, S["gpre"][l], ALU.add, ALU.mult)
        m2 = V(ve.tensor_tensor, [m], gt[:, s, :], mod[:, s, 2, :], S["gpost"][l], ALU.mult)
    for e in (S["V"], S["A"], S["G"]):
        e.wait([m, m1, m2])
    return mod, sc, gt


def second_block(nc, S):
    V, A, T, G = S["V"], S["A"], S["T"], S["G"]
    te, ac, ve, gp = nc.tensor, nc.scalar, nc.vector, nc.gpsimd
    mm, tr, C, carve, reset, banks, ring, rstd = (S["mm"], S["tr"], S["C"], S["carve"], S["reset"], S["banks"],
                                                  S["ring"], S["rstd"])
    I, PM, xT, ident, ones = S["I"], S["PM"], S["xT"], S["ident"], S["ones"]
    top, barrier = S["top"], S["barrier"]
    h = S["hT"][:, :].rearrange("p (k t) -> p k t", k=8)
    seg2 = lambda a: a.rearrange("p (s t) -> p s t", s=2)

    reset()
    mod, sc, gt = modulate2(nc, S, 0)
    keep = top[0]
    sq_t, r_t = carve(8, 512), carve(512)
    m_h = S["norm_modulate"]((0, 512), h, [sc[:, 0, :], sc[:, 1, :]], [mod[:, 0, 0, :], mod[:, 1, 0, :]], sq_t, r_t)
    barrier()
    top[0] = keep
    yp, ym = carve(8, 512), carve(8, 512)
    keep = top[0]
    pad = Rot([carve(2, 272) for _ in range(2)])
    lev = [Rot([carve(2, 272) for _ in range(1)]) for _ in range(2)]
    dif = Rot([carve(2, 512) for _ in range(2)])
    sgr = Rot([carve(512) for _ in range(2)])
    mz = None
    for b_ in pad.bufs:
        mz = G(gp.memset, [], b_.t, 0.0)
        b_.free(mz)
    pflat, mpw = ring.get(("poolw",))
    pw = pflat.rearrange("p (c n) -> p c n", c=8)
    for g in range(4):
        flat, ml = ring.get(("pin", g))
        w = flat.rearrange("p (k n) -> p k n", k=8)
        df = dif.take()
        for c in range(2):
            b = banks.take()
            m = mm(b.t[:, :], [(w[:, kk, c * P:(c + 1) * P], h[:, kk, :]) for kk in range(8)], [ml, m_h] + b.w)
            p = pad.take()
            m = A(ac.activation, [m] + p.w, p.t[:, :, 8:264], seg2(b.t[:, :]), ACT.Copy)
            b.free(m)
            src = p.t
            lo, hi = 1, 272
            for lv in range(g + 1):
                o = lev[lv % 2].bufs[0].t
                if lv == 0:
                    m = V(ve.tensor_tensor, [m, V.last()], o[:, :, 1:272], src[:, :, 0:271], src[:, :, 1:272], ALU.add)
                else:
                    d = 1 << (lv - 1)
                    lo, hi = lo + d, hi - d
                    m = V(ve.tensor_tensor, [m], o[:, :, lo:hi], src[:, :, lo - d:hi - d], src[:, :, lo + d:hi + d],
                          ALU.add)
                src = o
            rec = C("recip")[:, g * 256:(g + 1) * 256].unsqueeze(1).to_broadcast([P, 2, 256])
            o = lev[(g + 1) % 2].bufs[0].t
            m = V(ve.tensor_tensor, [m], o[:, :, 8:264], src[:, :, 8:264], rec, ALU.mult)
            m_d = V(ve.tensor_tensor, [m] + df.w, seg2(df.t[:, c, :]), o[:, :, 8:264], p.t[:, :, 8:264],
                    ALU.subtract)
            p.free(m_d)
        ring.release(("pin", g), T.last())
        flat, ml = ring.get(("pgate", g))
        w = flat.rearrange("p (k n) -> p k n", k=8)
        for c in range(2):
            b = banks.take()
            m = mm(b.t[:, :], [(w[:, kk, c * P:(c + 1) * P], h[:, kk, :]) for kk in range(8)], [ml] + b.w)
            s = sgr.take()
            ms = A(ac.activation, [m] + s.w, s.t, b.t[:, :], ACT.Silu)
            b.free(ms)
            b = banks.take()
            m = mm(b.t[:, :], [(pw[:, 2 * g + cc, c * P:(c + 1) * P], df.t[:, cc, :]) for cc in range(2)],
                   [mpw, m_d] + b.w)
            mv = V(ve.scalar_tensor_tensor, [m, ms], yp[:, 2 * g + c, :], b.t[:, :],
                   PM["pscale"][:, 2 * g + c:2 * g + c + 1], s.t, ALU.mult, ALU.mult)
            b.free(mv)
            s.free(mv)
        df.free(m)
        ring.release(("pgate", g), m)
    ring.release(("poolw",), m)
    m_yp = mv
    barrier()
    top[0] = keep
    spare = ym.rearrange("p k t -> p (k t)")
    g16 = spare[:, 0:512]
    gates = spare[:, 512:2560].rearrange("p (j t) -> p j t", j=4)
    tmp = spare[:, 2560:3584].rearrange("p (j t) -> p j t", j=2)
    aR = spare[:, 3584:4096]
    nM = [carve(512) for _ in range(2)]
    flat, ml = ring.get(("gates",))
    w = flat[:, 0:128].rearrange("p (k n) -> p k n", k=8)
    b = banks.take()
    m = mm(b.t[0:16, :], [(w[:, kk, :], h[:, kk, :]) for kk in range(8)], [ml] + b.w)
    ring.release(("gates",), m)
    mg = A(ac.activation, [m], g16[0:16, :], b.t[0:16, :], ACT.Copy)
    b.free(mg)
    for t in range(4):
        b = banks.take()
        m = mm(b.t[0:4, :], [(ident[0:16, 4 * t:4 * t + 4], g16[0:16, :])], [mg] + b.w)
        m = A(ac.activation, [m], gates[0:4, t, :], b.t[0:4, :], ACT.Identity, bias=S["bgate"][0:4, t:t + 1])
        b.free(m)
    m_gt = m
    acol, ecol = carve(4, 2, 4), carve(4, 2, 4)
    for d in range(2):
        li, lf = gates[0:4, 2 * d, :], gates[0:4, 2 * d + 1, :]
        e, B = tmp[0:4, 0, :], tmp[0:4, 1, :]
        m = A(ac.activation, [m_gt, V.last(), T.last()], e, lf, ACT.Abs)
        m = A(ac.activation, [m], e, e, ACT.Exp, scale=-1.0)
        m = A(ac.activation, [m], e, e, ACT.Ln, bias=ones[0:4, 0:1])
        m = V(ve.scalar_tensor_tensor, [m], lf, lf, 0.0, e, ALU.min, ALU.subtract)

        def scans(dst, src, op, init, m):
            if d == 0:
                return V(ve.tensor_tensor_scan, [m], dst, src, src, init, op, ALU.bypass)
            m = V(ve.tensor_tensor_scan, [m], seg2(dst)[:, 0, ::-1],
                  seg2(src)[:, 0, ::-1], seg2(src)[:, 0, ::-1], init, op, ALU.bypass)
            return V(ve.tensor_tensor_scan, [m], seg2(dst)[:, 1, ::-1], seg2(src)[:, 1, ::-1],
                     seg2(src)[:, 1, ::-1], dst[:, 0:1], op, ALU.bypass)

        m = scans(B, lf, ALU.add, 0.0, m)
        m = V(ve.tensor_tensor, [m, T.last()], aR[0:4, :], li, B, ALU.subtract)
        m = scans(nM[d][0:4, :], aR[0:4, :], ALU.max, 0.0, m)
        m = V(ve.tensor_scalar, [m], nM[d][0:4, :], nM[d][0:4, :], -1.0, None, ALU.mult)
        nMB = e
        m = V(ve.tensor_tensor, [m], nMB, nM[d][0:4, :], B, ALU.subtract)
        b = banks.take()
        for j in range(4):
            tr(b.t[:, j * 4:j * 4 + 4], aR[0:4, j * P:(j + 1) * P], ident[0:4, 0:4], [m] + b.w)
            mt = tr(b.t[:, 16 + j * 4:20 + j * 4], nMB[:, j * P:(j + 1) * P], ident[0:4, 0:4], [])
        m1 = A(ac.activation, [mt], acol[:, :, d, :], b.t[:, 0:16].rearrange("p (j h) -> p j h", j=4), ACT.Copy)
        m2 = A(ac.activation, [mt], ecol[:, :, d, :], b.t[:, 16:32].rearrange("p (j h) -> p j h", j=4), ACT.Exp)
        b.free(m2)
    m_cols = m2
    A.wait([m_cols])
    V.wait([m_cols])
    T.wait([V.last()])
    vaug = carve(4, 257)
    qT, kT = carve(2, 512), carve(2, 512)
    oh = kT.rearrange("p a t -> p (a t)").rearrange("p (j e) -> p j e", j=4)
    zT = qT
    hs = carve(4, 256)
    upad = Rot([carve(2, 258)])
    Cd = carve(4, 512)
    dm = ym[:, 7, :].rearrange("p (j t) -> p j t", j=4)
    stt = carve(4, 4)
    ss = carve(8)
    for b_ in upad.bufs:
        b_.free(G(gp.memset, [], b_.t, 0.0))
    mone = G(gp.memset, [], vaug[:, :, 256:257], 1.0)
    cv = PM["conv"]
    m_hs = None
    for hd in range(4):
        barrier()
        for n, dst in (("q", qT), ("k", kT)):
            flat, ml = ring.get((n, hd))
            w = flat.rearrange("p (k n) -> p k n", k=8)
            for c in range(2):
                b = banks.take()
                m = mm(b.t[:, :], [(w[:, kk, c * P:(c + 1) * P], h[:, kk, :]) for kk in range(8)], [ml] + b.w)
                u = upad.take()
                m = A(ac.activation, [m] + u.w, u.t[:, :, 1:257], seg2(b.t[:, :]), ACT.Copy)
                b.free(m)
                ch = (0 if n == "q" else 8) + hd * 2 + c
                o = seg2(dst[:, c, :])
                m = V(ve.tensor_scalar, [m], o, u.t[:, :, 0:256], cv[:, ch:ch + 1], None, ALU.mult)
                for j in (1, 2):
                    m = V(ve.scalar_tensor_tensor, [m], o, u.t[:, :, j:j + 256], cv[:, 16 * j + ch:16 * j + ch + 1], o,
                          ALU.mult, ALU.add)
                u.free(m)
            ring.release((n, hd), T.last())
        m_qk = m
        flat, ml = ring.get(("v", hd))
        w = flat.rearrange("p (k n) -> p k n", k=8)
        for j in range(4):
            b = banks.take()
            m = mm(b.t[:, 0:256], [(h[:, kk, j * P:(j + 1) * P], w[:, kk, :]) for kk in range(8)], [ml] + b.w)
            m_v = A(ac.activation, [m], vaug[:, j, 0:256], b.t[:, 0:256], ACT.Copy)
            b.free(m_v)
        ring.release(("v", hd), m)
        for d in range(2):
            b = banks.take()
            m_nm = mm(b.t[:, :], [(ident[0:4, hd:hd + 1].to_broadcast([4, P]), nM[d][0:4, :])], b.w)
            tri = C("tri_f" if d == 0 else "tri_b").unsqueeze(1).to_broadcast([P, 4, P])
            m = V(ve.tensor_tensor, [m_nm, T.last(), A.last()], dm, b.t[:, :].rearrange("p (j t) -> p j t", j=4),
                  tri, ALU.add)
            spans = []
            for i in range(4):
                bias = acol[:, i, d, hd:hd + 1]
                lo, hi = i * P, (i + 1) * P
                if d == 0:
                    rest = [(hi, 512)]
                elif i < 2:
                    rest = [(0, lo), (256, 512)]
                else:
                    rest = [(256, lo)]
                A(ac.activation, [m], Cd[:, i, lo:hi], dm[:, i, :], ACT.Exp, bias=bias)
                me = A.last()
                for r0, r1 in rest:
                    if r1 > r0:
                        me = A(ac.activation, [m_nm], Cd[:, i, r0:r1], b.t[:, r0:r1], ACT.Exp, bias=bias)
                sp = [(lo, hi)] + [r for r in rest if r[1] > r[0]]
                sp.sort()
                out_ = [sp[0]]
                for r in sp[1:]:
                    if r[0] == out_[-1][1]:
                        out_[-1] = (out_[-1][0], r[1])
                    else:
                        out_.append(r)
                spans.append((out_, me))
            b.free(me, m)
            for i in range(4):
                b = banks.take()
                t0 = 0 if i < 2 else 256
                m_s = m = mm(b.t[:, t0:512], [(kT[:, c, i * P:(i + 1) * P], qT[:, c, t0:512]) for c in range(2)],
                       [m_qk] + b.w)
                for r0, r1 in spans[i][0]:
                    mc = V(ve.scalar_tensor_tensor, [m, spans[i][1]], Cd[:, i, r0:r1], b.t[:, r0:r1], 0.0625,
                           Cd[:, i, r0:r1], ALU.mult, ALU.mult)
                b.free(mc)
            for j in range(4):
                if d == 0:
                    src = list(range(j + 1))
                elif j < 2:
                    src = list(range(j, 2))
                else:
                    src = [0, 1] + list(range(j, 4))
                b = banks.take()
                m = mm(b.t[:, 0:257], [(Cd[:, i, j * P:(j + 1) * P], vaug[:, i, :]) for i in src],
                       [mc, m_v, mone] + b.w)
                st = stt[:, j, 2 * d:2 * d + 1]
                m = A(ac.activation, [m], st, b.t[:, 256:257], ACT.Abs)
                m = V(ve.tensor_tensor, [m], st, st, ecol[:, j, d, hd:hd + 1], ALU.max)
                m = V(ve.reciprocal, [m], st, st)
                if d == 0:
                    m_hs = V(ve.tensor_scalar, [m], hs[:, j, :], b.t[:, 0:256], st, None, ALU.mult)
                else:
                    m_hs = V(ve.scalar_tensor_tensor, [m], hs[:, j, :], b.t[:, 0:256], st, hs[:, j, :], ALU.mult,
                             ALU.add)
                b.free(m_hs)
        flat, ml = ring.get(("o", hd))
        w = flat.rearrange("p (k n) -> p k n", k=8)
        for j in range(4):
            b = banks.take()
            m = mm(b.t[:, 0:256], [(h[:, kk, j * P:(j + 1) * P], w[:, kk, :]) for kk in range(8)], [ml] + b.w)
            m_o = A(ac.activation, [m, m_s], oh[:, j, :], b.t[:, 0:256], ACT.Sigmoid)
            b.free(m_o)
        ring.release(("o", hd), m)
        flat, ml = ring.get(("z", hd))
        w = flat.rearrange("p (k n) -> p k n", k=8)
        for c in range(2):
            b = banks.take()
            m = mm(b.t[:, :], [(w[:, kk, c * P:(c + 1) * P], h[:, kk, :]) for kk in range(8)], [ml] + b.w)
            m_z = A(ac.activation, [m, m_s], zT[:, c, :], b.t[:, :], ACT.Silu)
            b.free(m_z)
        ring.release(("z", hd), m)
        m = V(ve.tensor_tensor, [m_hs, m_o], hs, hs, oh, ALU.mult)
        for j in range(4):
            mq = A(ac.activation, [m], oh[:, j, :], hs[:, j, :], ACT.Square, accum_out=ss[:, j:j + 1])
        mr = V(ve.tensor_scalar, [mq], ss[:, 4:8], ss[:, 0:4], 1.0 / 256, EPS, ALU.mult, ALU.add)
        mr = V(ve.reciprocal, [mr], ss[:, 4:8], ss[:, 4:8])
        mr = A(ac.activation, [mr], ss[:, 4:8], ss[:, 4:8], ACT.Sqrt)
        for j in range(4):
            m = V(ve.tensor_scalar, [mr], hs[:, j, :], hs[:, j, :], ss[:, 4 + j:5 + j], None, ALU.mult)
        for c in range(2):
            b = banks.take()
            for j in range(4):
                mt = tr(b.t[:, j * P:(j + 1) * P], hs[:, j, c * P:(c + 1) * P], ident, [m] + b.w)
            mv = V(ve.scalar_tensor_tensor, [mt, m_z], ym[:, 2 * hd + c, :], b.t[:, :],
                   PM["mnorm"][:, 2 * hd + c:2 * hd + c + 1], zT[:, c, :], ALU.mult, ALU.mult)
            b.free(mv)
    m_ym = mv
    barrier()
    fa, ma = ring.get(("about", 0))
    fb, mb = ring.get(("about", 1))
    wa, wb = fa.rearrange("p (c n) -> p c n", c=8), fb.rearrange("p (c n) -> p c n", c=8)
    for k in range(8):
        b = banks.take()
        m = mm(b.t[:, :], [(wa[:, c, k::8], ym[:, c, :]) for c in range(8)]
               + [(wb[:, c, k::8], yp[:, c, :]) for c in range(8)], [ma, mb, m_ym, m_yp] + b.w)
        m_y = A(ac.activation, [m], h[:, k, :], b.t[:, :], ACT.Copy)
        b.free(m_y)
    ring.release(("about", 0), m)
    ring.release(("about", 1), m)
    barrier()
    top[0] = keep
    post_norm(nc, S, h, 512, [(0, gt[:, 0, :]), (1, gt[:, 1, :])], ym, carve(512))

    reset()
    mod, sc, gt = modulate2(nc, S, 1)
    keep = top[0]
    sq_t, r_t = carve(8, 512), carve(512)
    m_h = S["norm_modulate"]((0, 512), h, [sc[:, 0, :], sc[:, 1, :]], [mod[:, 0, 0, :], mod[:, 1, 0, :]], sq_t, r_t)
    barrier()
    top[0] = keep
    qT, zT, oT = carve(8, 256), carve(8, 256), carve(8, 256)
    kT, vv, kd = carve(2, 512), carve(4, 256), carve(4, 512)
    axc, axs = C("ax_cos"), C("ax_sin")
    t1r = Rot([carve(256) for _ in range(2)])
    hx = h[:, :, 256:512]

    def rope(dst, m):
        b = banks.take()
        m = mm(b.t[:, 0:256], [(C("swap_pair"), dst)], [m] + b.w)
        t1 = t1r.take()
        mt = V(ve.tensor_tensor, [m] + t1.w, t1.t, b.t[:, 0:256], axs, ALU.mult)
        b.free(mt)
        mg = G(gp.tensor_tensor, [m], dst, dst, axc, ALU.mult)
        m = V(ve.tensor_tensor, [mt, mg], dst, dst, t1.t, ALU.add)
        t1.free(m)
        return m

    flat, ml = ring.get(("cq",))
    w = flat.rearrange("p (k n) -> p k n", k=8)
    for a in range(2):
        for g in range(4):
            b = banks.take()
            m = mm(b.t[:, 0:256], [(w[:, kk, (4 * a + g) * P:(4 * a + g + 1) * P], hx[:, kk, :]) for kk in range(8)], [ml, m_h] + b.w)
            ma = A(ac.activation, [m], qT[:, 4 * a + g, :], b.t[:, 0:256], ACT.Copy)
            b.free(ma)
            m_q = rope(qT[:, 4 * a + g, :], ma)
    ring.release(("cq",), m)
    flat, ml = ring.get(("ckv",))
    w = flat.rearrange("p (k n) -> p k n", k=8)
    for a in range(2):
        b = banks.take()
        m = mm(b.t[:, :], [(w[:, kk, a * P:(a + 1) * P], h[:, kk, :]) for kk in range(8)], [ml] + b.w)
        ma = A(ac.activation, [m], kT[:, a, :], b.t[:, :], ACT.Copy)
        b.free(ma)
        mr = rope(kT[:, a, 256:512], ma)
        for u in range(2):
            for half in (0, 64):
                m_k = A(ac.activation, [mr, ma], kd[half:half + 64, 2 * a + u, :], kT[u * 64:u * 64 + 64, a, :], ACT.Copy)
    for j in range(4):
        b = banks.take()
        m = mm(b.t[:, 0:256], [(h[:, kk, j * P:(j + 1) * P], w[:, kk, 256:512]) for kk in range(8)], [ml] + b.w)
        m_v = A(ac.activation, [m], vv[:, j, :], b.t[:, 0:256], ACT.Copy)
        b.free(m_v)
    ring.release(("ckv",), m)
    flat, ml = ring.get(("cz",))
    w = flat.rearrange("p (k n) -> p k n", k=8)
    for a in range(2):
        for g in range(4):
            b = banks.take()
            m = mm(b.t[:, 0:256], [(w[:, kk, (4 * a + g) * P:(4 * a + g + 1) * P], hx[:, kk, :]) for kk in range(8)], [ml] + b.w)
            m_z = A(ac.activation, [m], zT[:, 4 * a + g, :], b.t[:, 0:256], ACT.Silu)
            b.free(m_z)
    ring.release(("cz",), m)
    f_s = Rot([carve(512) for _ in range(3)])
    f_p = Rot([carve(4, P) for _ in range(2)])
    f_st = Rot([carve(8) for _ in range(4)])
    band = C("band").rearrange("p (i t) -> p i t", i=2)
    work, outs = Rot(None, banks.bufs[0:6]), Rot(None, banks.bufs[6:8])
    A.wait([m_z])
    V.wait([m_z])
    for a in range(2):
        for g in range(4):
            ch = 4 * a + g
            bo = outs.take()
            wo = list(bo.w)
            for u in range(2):
                hd, kv, base = 2 * ch + u, ch // 2, u * 64
                for i in range(2):
                    b = work.take()
                    m = mm(b.t[:, :], [(qT[base:base + 64, ch, i * P:(i + 1) * P], kd[base:base + 64, kv, :])],
                           [m_q, m_k] + b.w)
                    s, st = f_s.take(), f_st.take()
                    m = V(ve.scalar_tensor_tensor, [m] + s.w, s.t, b.t[:, :], 0.125, band[:, i, :], ALU.mult, ALU.add)
                    b.free(m)
                    m = V(ve.tensor_reduce, [m] + st.w, st.t[:, 0:1], s.t, AX, ALU.max)
                    m = V(ve.tensor_scalar, [m], st.t[:, 1:2], st.t[:, 0:1], S["sink"][:, hd:hd + 1], -1.0,
                          ALU.max, ALU.mult)
                    me = A(ac.activation, [m], s.t, s.t, ACT.Exp, bias=st.t[:, 1:2], accum_out=st.t[:, 2:3])
                    mk = A(ac.activation, [m], st.t[:, 3:4], S["sink"][:, hd:hd + 1], ACT.Exp, bias=st.t[:, 1:2])
                    m = V(ve.tensor_tensor, [mk, me], st.t[:, 4:5], st.t[:, 2:3], st.t[:, 3:4], ALU.add)
                    m = V(ve.reciprocal, [m], st.t[:, 5:6], st.t[:, 4:5])
                    m = V(ve.tensor_scalar, [m], s.t, s.t, st.t[:, 5:6], None, ALU.mult)
                    st.free(m)
                    b = work.take()
                    for kb in range(4):
                        mt = tr(b.t[:, kb * P:(kb + 1) * P], s.t[:, kb * P:(kb + 1) * P], ident, [m] + b.w)
                    s.free(mt)
                    p = f_p.take()
                    m = A(ac.activation, [mt] + p.w, p.t, b.t[:, :].rearrange("p (k t) -> p k t", k=4), ACT.Copy)
                    b.free(m)
                    m_o = mm(bo.t[base:base + 64, i * P:(i + 1) * P],
                             [(vv[:, kb, kv * 64:(kv + 1) * 64], p.t[:, kb, :]) for kb in range(4)], [m, m_v] + wo)
                    p.free(m_o)
            m_oT = V(ve.tensor_tensor, [m_o], oT[:, ch, :], zT[:, ch, :], bo.t[:, 0:256], ALU.mult)
            bo.free(m_oT)
    flat, ml = ring.get(("cout",))
    w = flat.rearrange("p (c n) -> p c n", c=8)
    y = S["hT"][:, 0:2048].rearrange("p (k t) -> p k t", k=8)
    for k in range(8):
        b = banks.take()
        m = mm(b.t[:, 0:256], [(w[:, c, k::8], oT[:, c, :]) for c in range(8)], [ml, m_oT] + b.w)
        m_y = A(ac.activation, [m], y[:, k, :], b.t[:, 0:256], ACT.Copy)
        b.free(m_y)
    ring.release(("cout",), m)
    barrier()
    post_norm(nc, S, y, 256, [(1, gt[:, 1, :])], qT, carve(256))
    barrier()
    xo = S["hT"][:, 2048:4096].rearrange("p (i d) -> p i d", i=2)
    for i in range(2):
        for k0 in (0, 4):
            b = banks.take()
            for k in range(k0, k0 + 4):
                m = tr(b.t[:, (k - k0) * P:(k - k0 + 1) * P], xT[:, k, 256 + i * P:256 + (i + 1) * P], ident, b.w)
            dst = xo[:, i, :].rearrange("p (d k) -> p k d", k=8)[:, k0:k0 + 4, :]
            m = V(ve.tensor_copy, [m], dst, b.t[:, :].rearrange("p (k t) -> p k t", k=4))
            b.free(m)
        S["SP"].wait([m])
        nc.sync.dma_start(S["out"][0, i * P:(i + 1) * P, :], xo[:, i, :]).then_inc(S["s_out"], 16)
    nc.sync.wait_ge(S["s_out"], 32)


def post_norm(nc, S, y, n, parts, sq_t, r_t):
    V, A, banks, mm, xT, ve, ac = S["V"], S["A"], S["banks"], S["mm"], S["xT"], nc.vector, nc.scalar
    ms = A(ac.activation, [], sq_t, y, ACT.Square)
    b = banks.take()
    m = mm(b.t[:, 0:n], [(S["ones"], sq_t[:, k, :]) for k in range(8)], [ms] + b.w)
    mr = S["rstd"](b.t[:, 0:n], r_t, D, [m])
    b.free(mr)
    for k in range(8):
        for q, (s, g) in enumerate(parts):
            seg = slice(q * 256, (q + 1) * 256)
            m = V(ve.scalar_tensor_tensor, [mr], y[:, k, seg], y[:, k, seg], g[:, k:k + 1], r_t[:, seg], ALU.mult,
                  ALU.mult)
            xs = xT[:, k, s * 256:(s + 1) * 256]
            V(ve.tensor_tensor, [m], xs, xs, y[:, k, seg], ALU.add)


_INS = """x c positions w_mod b_mod norm_mix_g norm_ffn_g w_in qn_g kn_g lam_q1 lam_k1 lam_q2 lam_k2 subln_g
w_proj_a w_dw b_dw conv_ln_g conv_ln_b w_proj_b b_proj_b w_proj_c w_out w_router b_router w1 w3 w2 ws1 ws3 ws2
c_2 ctx_2 c_ctx_2 w_mod_2 b_mod_2 g_pre_2 g_post_2 ab_w_in_2 ab_b_gate_2 ab_conv_2 ab_mnorm_2 ab_pool_w_2
ab_pool_scale_2 ab_w_out_2 c_w_in_2 c_sink_2 c_w_out_2""".split()


def kernel(**inputs):
    import concourse.bacc as _bacc
    from concourse.bass_utils import run_bass_kernel_spmd as _run

    nc = _bacc.Bacc("TRN2", target_bir_lowering=False, num_devices=1)
    arrays, aps = {}, {}
    for name in _INS:
        a = np.ascontiguousarray(inputs[name])
        arrays[f"in_{name}"] = a
        aps[name] = nc.dram_tensor(f"in_{name}", a.shape, mybir.dt.from_np(a.dtype), kind="ExternalInput").ap()
    table = make_consts()
    arrays["in_table"] = table
    consts = nc.dram_tensor("in_table", table.shape, F32, kind="ExternalInput").ap()
    out = nc.dram_tensor("out_0", (1, 256, D), F32, kind="ExternalOutput").ap()
    build(nc, aps, consts, out)
    r = _run(nc, [arrays], core_ids=[0])
    return r.results[0]["out_0"]
```

```python
import math
from contextlib import ExitStack

import numpy as np
import concourse.bass as bass
from concourse import mybir

F32 = mybir.dt.float32
I32 = mybir.dt.int32
ALU = mybir.AluOpType
ACT = mybir.ActivationFunctionType
AX = mybir.AxisListType.X

P = 128
D = 1024
NEG = -1.0e30
EPS = 1e-6
UNIT = 2048
UNITS = 11
LAYERS = 2
EXPERTS = 64
SLOTS = 64
MORE = 32
LN_EXP = "natural_log_exp_and_others"
AR_COLS = 15976

CONST_COLS = {}


def make_consts():
    p = np.arange(P)
    cols = []
    at = [0]

    def add(name, a):
        a = np.asarray(a, np.float32).reshape(P, -1)
        CONST_COLS[name] = (at[0], a.shape[1])
        at[0] += a.shape[1]
        cols.append(a)

    add("ident", np.eye(P))
    add("ones", np.ones((P, P)))
    add("blk64", (p[:, None] // 64) == (p[None, :] // 64))
    half = np.zeros((P, P))
    pair = np.zeros((P, P))
    for m in range(P):
        if m % 64 < 32:
            half[m + 32, m] = -1.0
        else:
            half[m - 32, m] = 1.0
        if m % 2 == 0:
            pair[m + 1, m] = -1.0
        else:
            pair[m - 1, m] = 1.0
    add("swap_half", half)
    add("swap_pair", pair)
    add("from_s", p[:, None] >= p[None, :])
    causal = np.where(p[None, :] <= p[:, None], 0.0, NEG)
    add("causal", np.concatenate([np.zeros((P, P)), causal], 1))
    before = np.where(p[:, None] < p[None, :], 0.0, NEG)
    add("before", np.concatenate([before, np.zeros((P, P)), before], 1))
    add("tri_f", np.where(p[:, None] <= p[None, :], 0.0, NEG))
    add("tri_b", np.where(p[:, None] >= p[None, :], 0.0, NEG))
    inv = (np.float32(10000.0) ** (-np.arange(0, 64, 2, dtype=np.float32) / np.float32(64))).astype(np.float32)
    add("inv", inv[p % 32][:, None])
    add("iota", np.broadcast_to(np.arange(64)[None, :], (P, 64)))
    add("eps", np.full((P, 1), EPS))
    a8 = np.arange(8)
    add("tri8", np.broadcast_to((a8[None, :] < a8[:, None]).astype(np.float32).reshape(1, 64), (P, 64)))
    t = np.arange(256)
    band = []
    for i in range(2):
        q = i * P + p
        ok = np.abs(q[:, None] - t[None, :]) <= 128
        band.append(np.concatenate([np.zeros((P, 256)), np.where(ok, 0.0, NEG)], 1))
    add("band", np.concatenate(band, 1))
    rec = []
    for w in (2, 4, 8, 16):
        n = np.clip(t + w // 2, 0, 256) - np.clip(t - w // 2, 0, 256)
        rec.append((np.float32(1.0) / n.astype(np.float32)))
    add("recip", np.broadcast_to(np.concatenate(rec)[None, :], (P, 1024)))
    f = (np.float32(10000.0) ** (-np.arange(16, dtype=np.float32) / np.float32(16))).astype(np.float32)
    ang = np.concatenate([(t // 64).astype(np.float32)[:, None] * f, (t % 64).astype(np.float32)[:, None] * f], 1)
    i32 = (p % 64) // 2
    add("ax_cos", np.cos(ang.astype(np.float64))[:, i32].T)
    add("ax_sin", np.sin(ang.astype(np.float64))[:, i32].T)
    return np.ascontiguousarray(np.concatenate(cols, 1))


class Eng:

    def __init__(self, eng, sem, name):
        self.eng, self.sem, self.name, self.n, self.seen = eng, sem, name, 0, {}

    def wait(self, marks):
        for m in marks:
            if m is None:
                continue
            if isinstance(m, list):
                self.wait(m)
                continue
            sem, value, key = m
            if self.seen.get(key, 0) < value:
                self.eng.wait_ge(sem, value)
                self.seen[key] = value

    def __call__(self, fn, waits, *args, **kw):
        self.wait(waits)
        ins = fn(*args, **kw)
        return self.done(ins)

    def done(self, ins):
        self.n += 1
        ins.then_inc(self.sem, 1)
        return (self.sem, self.n, self.name)

    def last(self):
        return (self.sem, self.n, self.name)


class Buf:

    def __init__(self, t):
        self.t, self.w = t, []

    def free(self, *marks):
        self.w = list(marks)


class Rot:

    def __init__(self, tiles, bufs=None):
        self.bufs, self.i = bufs or [Buf(t) for t in tiles], 0

    def take(self):
        b = self.bufs[self.i % len(self.bufs)]
        self.i += 1
        return b


class Ring:

    def __init__(self, tile, sp, sems):
        self.tile, self.sp, self.sems = tile, sp, sems
        self.items, self.nxt, self.pos, self.live = [], 0, 0, []
        self.count = [0] * len(sems)
        self.where, self.gone = {}, {}

    def plan(self, key, units, parts):
        self.items.append((key, units, parts))

    def pump(self):
        while self.nxt < len(self.items):
            key, units, parts = self.items[self.nxt]
            pos = self.pos if self.pos + units <= UNITS else 0
            over = [x for x in self.live if x[0] < pos + units and pos < x[1]]
            if any(x[2] not in self.gone for x in over):
                return
            for x in over:
                self.sp.wait([self.gone[x[2]]])
            self.live = [x for x in self.live if x not in over]
            flat = self.tile[:, pos * UNIT:(pos + units) * UNIT]
            k = self.nxt % len(self.sems)
            for dst, src in parts:
                self.sp.eng.dma_start(dst(flat), src).then_inc(self.sems[k], 16)
                self.count[k] += 16
            self.where[key] = (flat, (self.sems[k], self.count[k], f"ring{k}"))
            self.live.append((pos, pos + units, key))
            self.pos = pos + units
            self.nxt += 1

    def get(self, key):
        return self.where[key]

    def release(self, key, *marks):
        self.gone[key] = list(marks)
        self.pump()


def build(nc, I, consts, out):
    ctx = ExitStack()
    with ctx:
        program(nc, ctx, I, consts, out)


def program(nc, ctx, I, consts, out):
    def sb(name, shape, dt=F32):
        return ctx.enter_context(nc.sbuf_tensor(name, shape, dt))

    def sem(name):
        return ctx.enter_context(nc.semaphore(name))

    T = Eng(nc.tensor, sem("s_pe"), "pe")
    A = Eng(nc.scalar, sem("s_act"), "act")
    V = Eng(nc.vector, sem("s_dve"), "dve")
    G = Eng(nc.gpsimd, sem("s_pool"), "pool")
    SP = Eng(nc.sync, sem("s_sp"), "sp")
    engines = [T, A, V, G]
    te, ac, ve, gp = nc.tensor, nc.scalar, nc.vector, nc.gpsimd

    def barrier():
        marks = [e.last() for e in engines if e.n]
        for e in engines:
            e.wait([m for m in marks if m[2] != e.name] + ([e.last()] if e.n and e is not T else []))

    def settle():
        A.wait([V.last()])
        for e in (V, G):
            e.wait([V.last(), A.last()])

    NCOL = consts.shape[1]
    cst = sb("cst", [P, NCOL])
    ring_t = sb("ring", [P, UNITS * UNIT])
    xT = sb("xT", [P, 8, 512])
    hT = sb("hT", [P, 4096])
    par = sb("par", [P, 928])
    ar = sb("ar", [P, AR_COLS])
    banks = Rot([ctx.enter_context(nc.psum_tensor(f"ps{i}", [P, 512], F32)) for i in range(8)])
    ring = Ring(ring_t, SP, [sem(f"s_ring{i}") for i in range(UNITS + 1)])
    s_par = sem("s_par")
    s_x = sem("s_x")
    s_out = sem("s_out")
    more = []
    for l in range(LAYERS):
        more.append([Eng(e, sem(f"s_more_{n}{l}"), f"more_{n}{l}")
                     for e, n in ((nc.tensor, "pe"), (nc.scalar, "act"), (nc.vector, "dve"))]
                    + [[sem(f"s_more_w{l}{i}") for i in range(2)]])

    top = [0]

    def reset():
        barrier()
        top[0] = 0

    def carve(*shape):
        n = int(np.prod(shape))
        a = ar[:, top[0]:top[0] + n]
        top[0] += n
        assert top[0] <= AR_COLS, top[0]
        if len(shape) == 2:
            a = a.rearrange("p (a b) -> p a b", a=shape[0])
        if len(shape) == 3:
            a = a.rearrange("p (a b c) -> p a b c", a=shape[0], b=shape[1])
        return a

    rows = carve(3, P)

    def C(name):
        o, n = CONST_COLS[name]
        return cst[:, o:o + n]

    ptop = [0]

    def pcol(n):
        a = par[:, ptop[0]:ptop[0] + n]
        ptop[0] += n
        assert ptop[0] <= 928
        return a

    def mm(o, pairs, waits, first=True, last=True, lax=False, each=None):
        T.wait(waits)
        n = len(pairs)
        for i, (l, r) in enumerate(pairs):
            if each is not None:
                T.wait([each[i]])
            ins = te.matmul(o, l, r, start=(first and i == 0), stop=(last and i == n - 1), skip_group_check=lax)
        return T.done(ins)

    def tr(o, i, ident, waits):
        T.wait(waits)
        return T.done(te.transpose(o, i, ident))

    ident, ones = C("ident"), C("ones")

    def plan_cols(key, w, c0, n, units):
        src = w.rearrange("(p k) n -> p k n", k=8)[:, :, c0:c0 + n]
        ring.plan(key, units, [(lambda f: f[:, 0:8 * n].rearrange("p (k n) -> p k n", k=8), src)])

    def plan_half(key, w, q):
        src = w.rearrange("(p k) n -> p k n", k=8)[:, 4 * q:4 * q + 4, :]
        ring.plan(key, 2, [(lambda f: f[:, 0:2 * UNIT].rearrange("p (k n) -> p k n", k=4), src)])

    def plan_rows(key, w, k, units):
        src = w.rearrange("(c p) n -> p c n", c=k)
        ring.plan(key, units, [(lambda f: f[:, 0:k * src.shape[2]].rearrange("p (c n) -> p c n", c=k), src)])

    def plan_up(key, w1, w3):
        ring.plan(("up",) + key, 2, [
            (lambda f: f[:, 0:UNIT], w1.rearrange("(p k) f -> p (k f)", k=8)),
            (lambda f: f[:, UNIT:2 * UNIT], w3.rearrange("(p k) f -> p (k f)", k=8))])

    def plan_down(key, w2):
        ring.plan(("down",) + key, 1, [(lambda f: f[:, 0:UNIT], w2.rearrange("(p j) n -> p (j n)", j=2))])

    def plan_mod(name, l):
        w = I["w_mod" if name == "mod" else "w_mod_2"][l]
        for j in range(w.shape[1] // D):
            plan_cols((name, l, j), w, j * D, D, 4)

    for l in range(LAYERS):
        if l == 0:
            plan_mod("mod", 0)
        for b in (1, 2, 0, 3):
            plan_cols(("in", l, b), I["w_in"][l], b * D, D, 4)
        if l == 0:
            plan_mod("mod", 1)
        else:
            plan_mod("mod2", 0)
            plan_mod("mod2", 1)
        for b, n in enumerate(("w_proj_a", "w_proj_b", "w_proj_c")):
            plan_cols(("in", l, 4 + b), I["w_in"][l], (4 + b) * D, D, 4)
            plan_rows(("proj", l, b), I[n][l], 4, 2)
        for q in range(2):
            plan_half(("out", l, q), I["w_out"][l], q)
        plan_cols(("router", l), I["w_router"][l], 0, EXPERTS, 1)
        plan_up((l, EXPERTS), I["ws1"][l], I["ws3"][l])
        plan_down((l, EXPERTS), I["ws2"][l])
        for e in range(0, EXPERTS, 2):
            for u in (e, e + 1):
                plan_up((l, u), I["w1"][l, u], I["w3"][l, u])
            for u in (e, e + 1):
                plan_down((l, u), I["w2"][l, u])
    abw = I["ab_w_in_2"][0]
    plan_cols(("gates",), abw, 7 * D, 16, 1)
    plan_rows(("poolw",), I["ab_pool_w_2"][0].rearrange("g c d -> (g c) d"), 8, 1)
    for g in range(4):
        plan_cols(("pin", g), abw, 5 * D + g * 256, 256, 1)
        plan_cols(("pgate", g), abw, 6 * D + g * 256, 256, 1)
    for h in range(4):
        for n, b in (("q", 0), ("k", 1), ("v", 2), ("o", 3), ("z", 4)):
            plan_cols((n, h), abw, b * D + h * 256, 256, 1)
    for j in range(2):
        plan_rows(("about", j), I["ab_w_out_2"][0, j * D:(j + 1) * D, :], 8, 4)
    cw = I["c_w_in_2"][0]
    plan_cols(("cq",), cw, 0, D, 4)
    plan_cols(("ckv",), cw, D, 512, 2)
    plan_cols(("cz",), cw, D + 512, D, 4)
    plan_rows(("cout",), I["c_w_out_2"][0], 8, 4)

    npar = [0]

    def pdma(dst, src, slow=False):
        nc.scalar.dma_start(dst, src, allow_slow_non_contiguous=slow).then_inc(s_par, 16)
        npar[0] += 16

    def dcols(v):
        return v.rearrange("(p k) -> p k", k=8)

    s_c = sem("s_c")
    craw = pcol(24).rearrange("p (c k) -> p c k", c=3)
    for q, v in enumerate((I["c"][0], I["c_ctx_2"], I["c_2"][0])):
        nc.scalar.dma_start(craw[:, q, :], dcols(v)).then_inc(s_c, 16)
    nc.scalar.dma_start(cst[:, 0:P], consts[:, 0:P]).then_inc(s_c, 16)
    m_c = (s_c, 64, "c")
    xin = hT[:, 0:2048].rearrange("p (i d) -> p i d", i=2)
    cin = hT[:, 2048:4096].rearrange("p (i d) -> p i d", i=2)
    nc.scalar.dma_start(xin, I["x"][0].rearrange("(i p) d -> p i d", p=P)).then_inc(s_x, 16)
    nc.scalar.dma_start(cin, I["ctx_2"][0].rearrange("(i p) d -> p i d", p=P)).then_inc(s_x, 16)
    pdma(cst[:, P:], consts[:, P:])
    bmod = [pcol(48).rearrange("p (j k) -> p j k", j=6) for _ in range(LAYERS)]
    gmix, gffn, bprb = [], [], []
    lamrow = carve(8, 64)
    brow = [pcol(64) for _ in range(LAYERS)]
    for l in range(LAYERS):
        pdma(bmod[l], I["b_mod"][l].rearrange("(j p k) -> p j k", j=6, k=8))
        for lst, n in ((gmix, "norm_mix_g"), (gffn, "norm_ffn_g"), (bprb, "b_proj_b")):
            lst.append(pcol(8))
            pdma(lst[l], dcols(I[n][l]))
        for q, n in enumerate(("lam_q1", "lam_k1", "lam_q2", "lam_k2")):
            pdma(lamrow[:, 4 * l + q, :], I[n][l].partition_broadcast(P))
        pdma(brow[l], I["b_router"][l].partition_broadcast(P))
    bmod2, gpre, gpost = [], [], []
    for l in range(2):
        bmod2.append(pcol(24).rearrange("p (j k) -> p j k", j=3))
        pdma(bmod2[l], I["b_mod_2"][l].rearrange("(j p k) -> p j k", j=3, k=8))
        for lst, n in ((gpre, "g_pre_2"), (gpost, "g_post_2")):
            lst.append(pcol(8))
            pdma(lst[l], dcols(I[n][l]))
    bgate = pcol(4)
    pdma(bgate[0:4, :], I["ab_b_gate_2"][0].rearrange("(t h) -> h t", t=4), True)
    sink = pcol(16)
    pdma(sink, I["c_sink_2"][0].partition_broadcast(P))
    posi = carve(256)
    pdma(posi.bitcast(I32), I["positions"][0].partition_broadcast(P))
    for l in range(LAYERS):
        pdma(rows[0:124, l, :], I["w_dw"][l].rearrange("k (c q) -> (k c) q", q=P))
    misc = []
    at = [0]

    def prow(key, src):
        n = src.shape[0]
        pdma(rows[at[0]:at[0] + n, 2, 0:src.shape[1]], src)
        misc.append((key, at[0], n))
        at[0] += n

    prow("conv", I["ab_conv_2"][0].rearrange("j (c q) -> (j c) q", q=P))
    for l in range(LAYERS):
        for n in ("b_dw", "conv_ln_g", "conv_ln_b"):
            prow((n, l), I[n][l].rearrange("(c q) -> c q", q=P))
        prow(("subln_g", l), I["subln_g"][l].rearrange("(c q) -> c q", q=P))
    prow("mnorm", I["ab_mnorm_2"][0].rearrange("(c q) -> c q", q=P))
    prow("pscale", I["ab_pool_scale_2"][0].rearrange("(c q) -> c q", q=P))
    for l in range(LAYERS):
        for n in ("qn_g", "kn_g"):
            r0 = at[0]
            pdma(rows[r0:r0 + 1, 2, 64:128], I[n][l].rearrange("(c q) -> c q", c=1))
            prow((n, l), I[n][l].rearrange("(c q) -> c q", c=1))
    NR = at[0]
    m_par = (s_par, npar[0], "par")
    m_x = (s_x, 32, "x")
    ring.pump()

    cact = pcol(24).rearrange("p (c k) -> p c k", c=3)
    m_cact = A(ac.activation, [m_c], cact, craw, ACT.Silu)
    T.wait([m_c, m_cact])
    mods = [pcol(48).rearrange("p (c j k) -> p c j k", c=1, j=6) for _ in range(LAYERS)]
    mods2 = [pcol(48).rearrange("p (c j k) -> p c j k", c=2, j=3) for _ in range(2)]

    def modulation(key, bias, conds, dst, rt, take, param):
        nc_ = len(conds)
        for j in range(bias.shape[1]):
            flat, ml = ring.get(key + (j,))
            w = flat.rearrange("p (k n) -> p k n", k=8)
            for q in range(2):
                b = take()
                T.wait([ml] + b.w)
                for s in range(2 * nc_):
                    for t in range(4):
                        kk = (t % (4 // nc_)) * 2 * nc_ + s
                        ins = te.matmul(b.t[32 * t:32 * t + 32, :],
                                        cact[:, conds[t * nc_ // 4], kk:kk + 1].to_broadcast([P, 32]),
                                        w[:, kk, q * 512:(q + 1) * 512], start=(s == 0), stop=(s == 2 * nc_ - 1))
                m = T.done(ins)
                mr = A(ac.activation, [m] + rt.w, rt.t[:, q * 512:(q + 1) * 512], b.t[:, :], ACT.Copy)
                b.free(mr)
                if q == 1:
                    ring.release(key + (j,), m)
                yield
            b = take()
            T.wait([mr] + b.w)
            for k in range(8):
                ins = te.matmul(b.t[:, 4 * k:4 * k + 4], rt.t[:, k::8], ident[:, 0::32], start=True, stop=True)
            m = T.done(ins)
            rt.free(m)
            src = b.t[:, 0:32].rearrange("p (k c g) -> p c k g", c=nc_, g=4 // nc_)
            for c in range(nc_):
                m1 = V(ve.tensor_reduce, [m, param], dst[:, c, j, :], src[:, c], AX, ALU.add)
                m2 = V(ve.tensor_tensor, [m1], dst[:, c, j, :], dst[:, c, j, :], bias[:, j, :], ALU.add)
            b.free(m1)
            V.wait([m2])
            yield

    mod_gen = modulation(("mod", 0), bmod[0], [0], mods[0], Buf(carve(1024)), banks.take, m_par)
    for _ in range(3):
        next(mod_gen)
    for src, c0 in ((cin, 0), (xin, 256)):
        for i in range(2):
            for k0 in (0, 4):
                b = banks.take()
                T.wait([m_x] + b.w)
                for k in range(k0, k0 + 4):
                    ins = te.transpose(b.t[:, (k - k0) * P:(k - k0 + 1) * P], src[:, i, k::8], ident)
                m = T.done(ins)
                m = A(ac.activation, [m], xT[:, k0:k0 + 4, c0 + i * P:c0 + (i + 1) * P],
                      b.t[:, :].rearrange("p (k t) -> p k t", k=4), ACT.Copy)
                b.free(m)
    wdw = [sb(f"wdw{l}", [P, 124]) for l in range(LAYERS)]
    pmisc = sb("pmisc", [P, P])
    m_prm = []
    for l in range(LAYERS):
        b = banks.take()
        m = tr(b.t[:, 0:124], rows[0:124, l, :], ident[0:124, 0:124], [m_par] + b.w)
        m = V(ve.tensor_copy, [m], wdw[l][:, :], b.t[:, 0:124])
        b.free(m)
        m_prm.append(m)
    b = banks.take()
    m = tr(b.t[:, 0:NR], rows[0:NR, 2, :], ident[0:NR, 0:NR], [m_par] + b.w)
    m = V(ve.tensor_copy, [m], pmisc[:, 0:NR], b.t[:, 0:NR])
    b.free(m)
    m_prm.append(m)
    PM = {k: pmisc[:, o:o + n] for k, o, n in misc}
    for e in (A, V, G, T):
        e.wait([m_par] + m_prm)

    cosT = sb("cosT", [P, 256])
    sinT = sb("sinT", [P, 256])
    posf, ang, rn, t0 = carve(256), carve(256), carve(256), carve(256)
    TWO_PI = 2.0 * math.pi
    C1 = 6.28125
    C2 = 0.00193500518798828125
    C3 = TWO_PI - C1 - C2
    MAGIC = 1.5 * 2.0 ** 23
    HALF = 3.1415925
    m = V(ve.tensor_copy, [], posf, posi.bitcast(I32))
    m = V(ve.tensor_scalar, [m], ang, posf, C("inv"), None, ALU.mult)
    m = V(ve.tensor_scalar, [m], rn, ang, 1.0 / TWO_PI, MAGIC, ALU.mult, ALU.add)
    m = V(ve.tensor_scalar, [m], rn, rn, MAGIC, None, ALU.subtract)
    for cc in (C1, C2, C3):
        m = V(ve.scalar_tensor_tensor, [m], ang, rn, -cc, ang, ALU.mult, ALU.add)
    m = V(ve.tensor_scalar, [m], ang, ang, HALF, -HALF, ALU.min, ALU.max)
    ms = A(ac.activation, [m], sinT[:, :], ang, ACT.Sin)
    m = V(ve.tensor_scalar, [m], rn, ang, math.pi / 2, None, ALU.add)
    m = V(ve.tensor_scalar, [m], t0, rn, math.pi, -TWO_PI, ALU.is_gt, ALU.mult)
    m = V(ve.tensor_tensor, [m], rn, rn, t0, ALU.add)
    m = V(ve.tensor_scalar, [m], rn, rn, HALF, -HALF, ALU.min, ALU.max)
    A(ac.activation, [m], cosT[:, :], rn, ACT.Sin)
    neglam = [pcol(1) for _ in range(LAYERS)]
    lams = pcol(4)
    for l in range(LAYERS):
        for q in range(2):
            m = V(ve.tensor_tensor, [], lamrow[:, 4 * l + 2 * q, :], lamrow[:, 4 * l + 2 * q, :],
                  lamrow[:, 4 * l + 2 * q + 1, :], ALU.mult)
            m = V(ve.tensor_reduce, [m], lams[:, 2 * l + q:2 * l + q + 1], lamrow[:, 4 * l + 2 * q, :], AX, ALU.add)
    lexp = pcol(4)
    m = A(ac.activation, [m], lexp, lams, ACT.Exp)
    lam_init = [0.8 - 0.6 * math.exp(-0.3 * l) for l in range(LAYERS)]
    sublnS = [pcol(1) for _ in range(LAYERS)]
    for l in range(LAYERS):
        m2 = V(ve.tensor_tensor, [m], neglam[l], lexp[:, 2 * l + 1:2 * l + 2], lexp[:, 2 * l:2 * l + 1], ALU.subtract)
        V(ve.tensor_scalar, [m2], neglam[l], neglam[l], -lam_init[l], None, ALU.add)
        V(ve.tensor_scalar, [], sublnS[l], PM[("subln_g", l)], 1.0 - lam_init[l], None, ALU.mult)
    def scales(l):
        out = []
        for part, gain in ((1, gmix[l]), (4, gffn[l])):
            a = pcol(8)
            m = V(ve.scalar_tensor_tensor, [], a, mods[l][:, 0, part, :], 1.0, gain, ALU.add, ALU.mult)
            out.append(a)
        A.wait([m])
        V.wait([m])
        return out

    def scales2(l):
        sc, gt = pcol(16).rearrange("p (s k) -> p s k", s=2), pcol(16).rearrange("p (s k) -> p s k", s=2)
        for q in range(2):
            V(ve.scalar_tensor_tensor, [], sc[:, q, :], mods2[l][:, q, 1, :], 1.0, gpre[l], ALU.add, ALU.mult)
            m = V(ve.tensor_tensor, [], gt[:, q, :], mods2[l][:, q, 2, :], gpost[l], ALU.mult)
        A.wait([m])
        V.wait([m])
        return sc, gt

    for _ in mod_gen:
        pass

    def rstd(src_ps, dst, n, waits):
        m = A(ac.activation, waits, dst, src_ps, ACT.Ln, bias=C("eps"), scale=1.0 / n)
        return A(ac.activation, [m], dst, dst, ACT.Exp, scale=-0.5)

    def rstd_sqrt(src_ps, dst, n, waits):
        m = V(ve.tensor_scalar, waits, dst, src_ps, 1.0 / n, EPS, ALU.mult, ALU.add)
        m = V(ve.reciprocal, [m], dst, dst)
        return A(ac.activation, [m], dst, dst, ACT.Sqrt)

    def norm_modulate(cols, h, scale, shift, sq_t, r_t, marks=()):
        c0, c1 = cols
        n = c1 - c0
        b = banks.take()
        T.wait(b.w)
        for k in range(0, 8, 2):
            ms = A(ac.activation, list(marks[k:k + 2]), sq_t[:, k:k + 2, :], xT[:, k:k + 2, c0:c1], ACT.Square)
            T.wait([ms])
            for kk in (k, k + 1):
                ins = te.matmul(b.t[:, 0:n], ones, sq_t[:, kk, :], start=(kk == 0), stop=(kk == 7))
        m = T.done(ins)
        mr = rstd(b.t[:, 0:n], r_t, D, [m])
        b.free(mr)
        mh = []
        V.wait(list(marks))
        for k in range(8):
            for s in range(n // 256):
                seg = slice(s * 256, (s + 1) * 256)
                m = V(ve.scalar_tensor_tensor, [mr], h[:, k, seg], xT[:, k, c0 + s * 256:c0 + (s + 1) * 256],
                      scale[s][:, k:k + 1], r_t[:, seg], ALU.mult, ALU.mult)
                m = A(ac.activation, [m], h[:, k, seg], h[:, k, seg], ACT.Identity, bias=shift[s][:, k:k + 1])
            mh.append(m)
        return mh

    XC = (256, 512)
    reset()
    marks = ()
    for l in range(LAYERS):
        marks = first_layer(nc, locals(), l, marks)
    second_block(nc, locals(), marks)


def first_layer(nc, S, l, marks):
    V, A, T, G = S["V"], S["A"], S["T"], S["G"]
    te, ac, ve, gp = nc.tensor, nc.scalar, nc.vector, nc.gpsimd
    mm, tr, C, carve, reset, banks, ring, rstd = (S["mm"], S["tr"], S["C"], S["carve"], S["reset"], S["banks"],
                                                  S["ring"], S["rstd"])
    I, PM, hT, xT, ident, ones = S["I"], S["PM"], S["hT"], S["xT"], S["ident"], S["ones"]
    S["top"][0] = 0
    h = hT[:, 0:2048].rearrange("p (k t) -> p k t", k=8)
    merged = hT[:, 2048:4096].rearrange("p (k t) -> p k t", k=8)
    mod = S["mods"][l]
    amix, affn = S["scales"](l)
    keep = S["top"][0]
    sq_t, r_t = carve(8, 256), carve(256)
    m_h = S["norm_modulate"](S["XC"], h, [amix], [mod[:, 0, 0, :]], sq_t, r_t, marks)
    S["settle"]()
    S["top"][0] = keep

    qR, kR = carve(4, 256), carve(4, 256)
    va, vc = carve(2, 512), carve(2, 512)
    hpad = carve(4, 286)
    acc = carve(4, 256)
    qc, kc = merged[:, 0:4, :], merged[:, 4:8, :]
    keep = S["top"][0]
    r_a, r_sq, r_t1, r_r = [Rot([carve(2, 256) for _ in range(2)]) for _ in range(4)]
    cosB = S["cosT"][:, :].unsqueeze(1).to_broadcast([P, 2, 256])
    sinB = S["sinT"][:, :].unsqueeze(1).to_broadcast([P, 2, 256])
    m_zero = G(gp.memset, [], hpad[:, :, 0:30], 0.0)

    flat, ml = ring.get(("in", l, 1))
    w = flat.rearrange("p (k n) -> p k n", k=8)
    for i in range(2):
        b = banks.take()
        m = mm(b.t[:, :], [(h[:, kk, i * P:(i + 1) * P], w[:, kk, 0:512]) for kk in range(8)], [ml] + b.w, each=m_h)
        m_va = A(ac.activation, [m], va[:, i, :], b.t[:, :], ACT.Copy)
        b.free(m_va)
    for pr in range(2):
        b = banks.take()
        for c in range(2):
            c0 = 512 + (2 * pr + c) * P
            m = mm(b.t[:, c * 256:(c + 1) * 256], [(w[:, kk, c0:c0 + P], h[:, kk, :]) for kk in range(8)], b.w)
        m_ua = A(ac.activation, [m], hpad[:, 2 * pr:2 * pr + 2, 30:286],
                 b.t[:, :].rearrange("p (c t) -> p c t", c=2), ACT.Copy)
        b.free(m_ua)
    ring.release(("in", l, 1), m)
    flat, ml = ring.get(("in", l, 2))
    w = flat.rearrange("p (k n) -> p k n", k=8)
    m_glu = []
    for pr in range(2):
        b = banks.take()
        for c in range(2):
            c0 = (2 * pr + c) * P
            m = mm(b.t[:, c * 256:(c + 1) * 256], [(w[:, kk, c0:c0 + P], h[:, kk, :]) for kk in range(8)],
                   [ml] + b.w)
        sg = r_sq.take()
        ms = A(ac.activation, [m] + sg.w, sg.t, b.t[:, :].rearrange("p (c t) -> p c t", c=2), ACT.Sigmoid)
        b.free(ms)
        hp = hpad[:, 2 * pr:2 * pr + 2, 30:286]
        mg = V(ve.tensor_tensor, [ms, m_ua], hp, hp, sg.t, ALU.mult)
        sg.free(mg)
        m_glu.append(mg)
    wd = S["wdw"][l]
    mc = [None] * 4
    conv_steps = []
    for k in range(31):
        for c in range(4):
            conv_steps.append((k, c))

    def conv(n):
        for _ in range(min(n, len(conv_steps))):
            k, c = conv_steps.pop(0)
            tap = wd[:, k * 4 + c:k * 4 + c + 1]
            if k == 0:
                mc[c] = V(ve.tensor_scalar, [], acc[:, c, :], hpad[:, c, 0:256], tap, PM[("b_dw", l)][:, c:c + 1],
                          ALU.mult, ALU.add)
            else:
                mc[c] = V(ve.scalar_tensor_tensor, [mc[c]], acc[:, c, :], hpad[:, c, k:k + 256], tap, acc[:, c, :],
                          ALU.mult, ALU.add)

    V.wait([m_zero] + m_glu)
    for dst, blk, off in ((qc, 2, 512), (kc, 3, 0)):
        if blk == 3:
            ring.release(("in", l, 2), m)
            flat, ml = ring.get(("in", l, 0))
            w = flat.rearrange("p (k n) -> p k n", k=8)
            m_rope = None
            for half, (turned, gname) in enumerate(((qR, "qn_g"), (kR, "kn_g"))):
                g = PM[(gname, l)]
                for pr in range(2):
                    b = banks.take()
                    for c in range(2):
                        c0 = half * 512 + (2 * pr + c) * P
                        m = mm(b.t[:, c * 256:(c + 1) * 256], [(w[:, kk, c0:c0 + P], h[:, kk, :]) for kk in range(8)],
                               [ml] + b.w)
                    if half == 1 and pr == 1:
                        ring.release(("in", l, 0), m)
                    ps = b.t[:, :].rearrange("p (c t) -> p c t", c=2)
                    qa, sq, t1, rr = r_a.take(), r_sq.take(), r_t1.take(), r_r.take()
                    ma = A(ac.activation, [m] + qa.w, qa.t, ps, ACT.Copy, scale=g)
                    mq = A(ac.activation, [m] + sq.w, sq.t, ps, ACT.Square)
                    b.free(ma, mq)
                    bs, bw = banks.take(), banks.take()
                    m_ss = mm(bs.t[:, :], [(C("blk64"), sq.t)], [mq] + bs.w)
                    sq.free(m_ss)
                    m_sw = mm(bw.t[:, :], [(C("swap_half"), qa.t)], [ma] + bw.w)
                    pss = bs.t[:, :].rearrange("p (c t) -> p c t", c=2)
                    psw = bw.t[:, :].rearrange("p (c t) -> p c t", c=2)
                    V.wait(rr.w)
                    mr = S["rstd_sqrt"](pss, rr.t, 64, [m_ss])
                    bs.free(mr)
                    mt = V(ve.tensor_tensor, [m_sw] + t1.w, t1.t, psw, sinB, ALU.mult)
                    bw.free(mt)
                    mb = G(gp.tensor_tensor, [ma, m_sw], qa.t, qa.t, cosB, ALU.mult)
                    mt = V(ve.tensor_tensor, [mt, mb], t1.t, t1.t, qa.t, ALU.add)
                    qa.free(mt)
                    m_rope = V(ve.tensor_tensor, [mt, mr], turned[:, 2 * pr:2 * pr + 2, :], t1.t, rr.t, ALU.mult)
                    t1.free(m_rope)
                    rr.free(m_rope)
                    conv(9)

            flat, ml = ring.get(("in", l, 3))
            w = flat.rearrange("p (k n) -> p k n", k=8)
        for pr in range(2):
            b = banks.take()
            for c in range(2):
                c0 = off + (2 * pr + c) * P
                m = mm(b.t[:, c * 256:(c + 1) * 256], [(w[:, kk, c0:c0 + P], h[:, kk, :]) for kk in range(8)],
                       [ml] + b.w)
            m_qk = A(ac.activation, [m], dst[:, 2 * pr:2 * pr + 2, :],
                     b.t[:, :].rearrange("p (c t) -> p c t", c=2), ACT.Copy)
            b.free(m_qk)
            conv(14)
    for i in range(2):
        b = banks.take()
        m = mm(b.t[:, :], [(h[:, kk, i * P:(i + 1) * P], w[:, kk, 512:1024]) for kk in range(8)], [ml] + b.w)
        m_vc = A(ac.activation, [m], vc[:, i, :], b.t[:, :], ACT.Copy)
        b.free(m_vc)
    ring.release(("in", l, 3), m)

    S["top"][0] = keep
    for e in (T, A, V):
        e.wait([m_rope])
    ac.preload_act_table_set(LN_EXP)
    oa, oc = carve(4, 256), carve(4, 256)
    mask, bef = C("causal"), C("before")
    m_oa, m_oc, m_ob = [], [], []

    def diff_stream(heads, bk):
        s, a, st, at, o, r = carve(2, 256), carve(256), carve(8), carve(3, P), carve(256), carve(256)
        w_at, w_r, m = [], [], None
        for hd in heads:
            for i in range(2):
                K = (i + 1) * P
                both = []
                for mp in range(2):
                    b = bk.take()
                    both.append((b, mm(b.t[:, 0:K], [(qR[mp * 64:mp * 64 + 64, hd, i * P:(i + 1) * P],
                                                      kR[mp * 64:mp * 64 + 64, hd, 0:K])], b.w)))
                yield
                for mp, (b, mq) in enumerate(both):
                    m = V(ve.scalar_tensor_tensor, [mq, m], s[:, mp, 0:K], b.t[:, 0:K], 0.125, mask[:, 256 - K:256],
                          ALU.mult, ALU.add)
                    b.free(m)
                m = V(ve.tensor_reduce, [m], st[:, 0:2], s[:, :, 0:K], AX, ALU.max)
                m = V(ve.tensor_scalar, [m], st[:, 2:4], st[:, 0:2], -1.0, None, ALU.mult)
                yield
                for mp in range(2):
                    me = A(ac.activation, [m], s[:, mp, 0:K], s[:, mp, 0:K], ACT.Exp, bias=st[:, 2 + mp:3 + mp],
                           accum_out=st[:, 4 + mp:5 + mp])
                yield
                m = V(ve.reciprocal, [me], st[:, 6:8], st[:, 4:6])
                m2 = V(ve.tensor_scalar, [m, w_at], a[:, 0:K], s[:, 0, 0:K], st[:, 6:7], None, ALU.mult)
                m1 = V(ve.tensor_tensor, [m], st[:, 7:8], st[:, 7:8], S["neglam"][l], ALU.mult)
                m = V(ve.scalar_tensor_tensor, [m1, m2], a[:, 0:K], s[:, 1, 0:K], st[:, 7:8], a[:, 0:K],
                      ALU.mult, ALU.add)
                yield
                b = bk.take()
                for kb in range(i + 1):
                    mt = tr(b.t[:, kb * P:(kb + 1) * P], a[:, kb * P:(kb + 1) * P], ident, [m] + b.w)
                w_at = [mt]
                yield
                m_at = A(ac.activation, [mt], at[:, i:2 * i + 1, :],
                         b.t[:, 0:K].rearrange("p (k t) -> p k t", k=i + 1), ACT.Copy)
                b.free(m_at)
                yield
            b, b2 = bk.take(), bk.take()
            vv = [va[:, kb, hd * P:(hd + 1) * P] for kb in range(2)]
            mm(b.t[:, 0:P], [(vv[0], at[:, 0, :])], [m_at, m_va] + b.w)
            m_v = mm(b.t[:, P:256], [(vv[0], at[:, 1, :]), (vv[1], at[:, 2, :])], [])
            yield
            msq = A(ac.activation, [m_v], o, b.t[:, 0:256], ACT.Square)
            yield
            m2 = mm(b2.t[:, 0:256], [(ones, o)], [msq] + b2.w)
            yield
            mr = rstd(b2.t[:, 0:256], r, P, [m2] + w_r)
            b2.free(mr)
            yield
            m = V(ve.scalar_tensor_tensor, [mr, m_v], oa[:, hd, :], b.t[:, 0:256], S["sublnS"][l], r, ALU.mult,
                  ALU.mult)
            b.free(m, msq)
            w_r = [m]
            m_oa.append(m)

    def stick_stream(pairs, bo, bz):
        z, e = [carve(384) for _ in range(2)], [carve(384) for _ in range(2)]
        wz, we = [None, None], [None, None]
        for c in pairs:
            w_bo = list(bo.w)
            m = [None, None]
            for u in range(2):
                base = u * 64
                kk, qq = kc[base:base + 64, c, :], qc[base:base + 64, c, :]
                mm(bz[u].t[:, 0:256], [(kk[:, 0:P], qq)], [m_qk] + bz[u].w)
                m[u] = mm(bz[u].t[:, 256:384], [(kk[:, P:256], qq[:, P:256])], [])
            yield
            for u in range(2):
                m[u] = V(ve.scalar_tensor_tensor, [m[u], wz[u]], z[u], bz[u].t[:, 0:384], 0.125, bef, ALU.mult, ALU.add)
                bz[u].free(m[u])
            yield
            for fn, src, kw in ((ACT.Abs, z, {}), (ACT.Exp, e, {"scale": -1.0}), (ACT.Ln, e, {"bias": ones[:, 0:1]})):
                for u in range(2):
                    m[u] = A(ac.activation, [m[u], we[u]], e[u], src[u], fn, **kw)
            yield
            for u in range(2):
                m[u] = V(ve.scalar_tensor_tensor, [m[u]], e[u], z[u], 0.0, e[u], ALU.max, ALU.add)
            yield
            for u in range(2):
                b = bz[u]
                mm(b.t[:, 256:384], [(C("from_s"), e[u][:, 256:384])], [m[u]] + b.w)
                mm(b.t[:, 0:P], [(C("from_s"), e[u][:, 0:P])], [])
                m[u] = mm(b.t[:, P:256], [(C("from_s"), e[u][:, P:256]), (ones, e[u][:, 256:384])], [])
            yield
            for u in range(2):
                m[u] = V(ve.tensor_tensor, [m[u]], z[u], z[u], bz[u].t[:, 0:384], ALU.subtract)
                bz[u].free(m[u])
            yield
            for u in range(2):
                m[u] = wz[u] = A(ac.activation, [m[u]], e[u], z[u], ACT.Exp)
            yield
            for u in range(2):
                hd, o = 2 * c + u, bo.t[u * 64:u * 64 + 64, :]
                vv = [vc[:, j, hd * 64:(hd + 1) * 64] for j in range(2)]
                mm(o[:, 0:P], [(vv[0], e[u][:, 0:P])], [m[u], m_vc] + w_bo)
                m[u] = we[u] = mm(o[:, P:256], [(vv[0], e[u][:, P:256]), (vv[1], e[u][:, 256:384])], [])
            yield
            m = A(ac.activation, [m[1]], oc[:, c, :], bo.t[:, 0:256], ACT.Copy)
            bo.free(m)
            m_oc.append(m)

    def conv_stream(b):
        lnm, lnr = carve(256), carve(256)
        conv(999)
        m = mm(b.t[:, 0:256], [(ones, acc[:, c, :]) for c in range(4)], mc + b.w)
        yield
        m = A(ac.activation, [m], lnm, b.t[:, 0:256], ACT.Copy, scale=1.0 / 512)
        b.free(m)
        yield
        m = V(ve.tensor_tensor, [m], acc, acc, lnm.unsqueeze(1).to_broadcast([P, 4, 256]), ALU.subtract)
        yield
        msq = A(ac.activation, [m], ob, acc, ACT.Square)
        yield
        m2 = mm(b.t[:, 0:256], [(ones, ob[:, c, :]) for c in range(4)], [msq] + b.w)
        yield
        mr = rstd(b.t[:, 0:256], lnr, 512, [m2])
        b.free(mr)
        yield
        m = V(ve.tensor_tensor, [mr], acc, acc, lnr.unsqueeze(1).to_broadcast([P, 4, 256]), ALU.mult)
        yield
        A.wait([m2])
        for c in range(4):
            m = A(ac.activation, [m], ob[:, c, :], acc[:, c, :], ACT.Silu, bias=PM[("conv_ln_b", l)][:, c:c + 1],
                  scale=PM[("conv_ln_g", l)][:, c:c + 1])
        m_ob.append(m)
        ac.preload_act_table_set(LN_EXP)

    def mod_stream(b):
        rt = Buf(carve(1024))
        if l == 0:
            yield from S["modulation"](("mod", 1), S["bmod"][1], [0], S["mods"][1], rt, lambda: b, None)
        else:
            for q in range(2):
                yield from S["modulation"](("mod2", q), S["bmod2"][q], [1, 2], S["mods2"][q], rt, lambda: b, None)

    ob = hpad[:, :, 0:256]
    bk = banks.bufs
    A.wait([V.last()])
    streams = [diff_stream((0, 2), Rot(None, bk[0:2])), diff_stream((1, 3), Rot(None, bk[2:4])),
               stick_stream((0, 1, 2, 3), bk[4], bk[5:7])]
    one = conv_stream(bk[7])
    later = mod_stream(bk[7])
    for q in (0, 0, 0, 2):
        next(streams[q])
    while streams:
        for f in list(streams):
            if next(f, 0) == 0:
                streams.remove(f)
        if one is not None:
            if next(one, 0) == 0:
                one = None
        else:
            next(later, None)
    for _ in later:
        pass
    m_oa, m_ob, m_oc = m_oa[-2:], m_ob[-1], m_oc[-1]

    before = [e.last() for e in (T, V, A, G)]
    A.wait(before)
    V.wait(before)
    S["top"][0] = 0
    f_y = Rot([carve(256) for _ in range(3)])
    sg = carve(8, 256)
    m_mrg, m_sg = [None] * 8, [None] * 8
    for br, (o, mo) in enumerate(((oa, m_oa), (ob, m_ob), (oc, m_oc))):
        flat, ml = ring.get(("in", l, 4 + br))
        w = flat.rearrange("p (k n) -> p k n", k=8)
        for k in range(8):
            b = banks.take()
            m = mm(b.t[:, 0:256], [(w[:, kk, k::8], h[:, kk, :]) for kk in range(8)], [ml] + b.w)
            m_sg[k] = A(ac.activation, [m, m_mrg[k]], sg[:, k, :], b.t[:, 0:256], ACT.Sigmoid)
            b.free(m_sg[k])
        ring.release(("in", l, 4 + br), m)
        pflat, mp = ring.get(("proj", l, br))
        pw = pflat.rearrange("p (c n) -> p c n", c=4)
        for k in range(8):
            b = banks.take()
            m = mp_ = mm(b.t[:, 0:256], [(pw[:, c, k::8], o[:, c, :]) for c in range(4)], [mp, mo] + b.w)
            if br == 0:
                m_mrg[k] = V(ve.tensor_tensor, [m, m_sg[k]], merged[:, k, :], sg[:, k, :], b.t[:, 0:256], ALU.mult)
                b.free(m_mrg[k])
                continue
            y = f_y.take()
            if br == 1:
                m = V(ve.scalar_tensor_tensor, [m, m_sg[k]] + y.w, y.t, b.t[:, 0:256], S["bprb"][l][:, k:k + 1],
                      sg[:, k, :], ALU.add, ALU.mult)
            else:
                m = V(ve.tensor_tensor, [m, m_sg[k]] + y.w, y.t, sg[:, k, :], b.t[:, 0:256], ALU.mult)
            b.free(m)
            m_mrg[k] = V(ve.tensor_tensor, [m, m_mrg[k]], merged[:, k, :], merged[:, k, :], y.t, ALU.add)
            y.free(m_mrg[k])
        ring.release(("proj", l, br), mp_)
    marks = []
    halves = [ring.get(("out", l, q)) for q in range(2)]
    w = [f.rearrange("p (k n) -> p k n", k=4) for f, _ in halves]
    for k in range(8):
        b = banks.take()
        m = mm(b.t[:, 0:256], [(w[kk // 4][:, kk % 4, k::8], merged[:, kk, :]) for kk in range(8)],
               [x for _, x in halves] + b.w, each=m_mrg)
        mv = V(ve.scalar_tensor_tensor, [m], xT[:, k, 256:512], b.t[:, 0:256], mod[:, 0, 2, k:k + 1],
               xT[:, k, 256:512], ALU.mult, ALU.add)
        b.free(mv)
        marks.append(mv)
    for q in range(2):
        ring.release(("out", l, q), m)

    S["top"][0] = 0
    sq_t, r_t = carve(8, 256), carve(256)
    m_h = S["norm_modulate"](S["XC"], h, [affn], [mod[:, 0, 3, :]], sq_t, r_t, marks)
    return moe(nc, S, l, h, m_h, mod)


def route(nc, S, l, h, m, b):
    V, A, T = S["V"], S["A"], S["T"]
    ac, ve = nc.scalar, nc.vector
    mm, C, carve = S["mm"], S["C"], S["carve"]
    ones, ident, iota = S["ones"], S["ident"], C("iota")
    mk, posm = carve(2, 64), carve(2, 64)
    count, below = carve(1), carve(P)
    keep = S["top"][0]
    sc, bi, rep = carve(2, 64), carve(2, 64), carve(2, 64)
    s8, gs, rank = carve(16, 8), carve(2, 8), carve(2, 8)
    cmp1, cmp2 = carve(2, 8, 8), carve(2, 8, 8)
    top8, den = carve(2, 8), carve(2)
    ms = A(ac.activation, [m], sc, b.t[:, 0:128].rearrange("p (i e) -> p i e", i=2), ACT.Sigmoid)
    b.free(ms)
    m = V(ve.tensor_tensor, [ms], bi, sc, S["brow"][l].unsqueeze(1).to_broadcast([P, 2, 64]), ALU.add)
    for q in range(16):
        m2 = V(ve.max, [m], s8[:, q, :], bi[:, q // 8, (q % 8) * 8:(q % 8) * 8 + 8])
    m = V(ve.tensor_tensor, [m2], gs.rearrange("p i g -> p (i g)"), s8[:, :, 0], s8[:, :, 1], ALU.add)
    tri8 = C("tri8").rearrange("p (a b) -> p a b", a=8)
    both = []
    for i in range(2):
        ga = gs[:, i, :].unsqueeze(2).to_broadcast([P, 8, 8])
        gb = gs[:, i, :].unsqueeze(1).to_broadcast([P, 8, 8])
        m1 = V(ve.tensor_tensor, [m], cmp1[:, i], gb, ga, ALU.is_gt)
        m2 = V(ve.tensor_tensor, [m], cmp2[:, i], gb, ga, ALU.is_equal)
        m2 = V(ve.tensor_tensor, [m2], cmp2[:, i], cmp2[:, i], tri8, ALU.mult)
        m2 = V(ve.tensor_tensor, [m1, m2], cmp1[:, i], cmp1[:, i], cmp2[:, i], ALU.add)
        m2 = V(ve.tensor_reduce, [m2], rank[:, i, :], cmp1[:, i], AX, ALU.add)
        m2 = V(ve.tensor_scalar, [m2], gs[:, i, :], rank[:, i, :], 3.5, None, ALU.is_lt)
        gm = gs[:, i, :].unsqueeze(2).to_broadcast([P, 8, 8])
        bv = bi[:, i, :].rearrange("p (g e) -> p g e", g=8)
        mv = mk[:, i, :].rearrange("p (g e) -> p g e", g=8)
        m1 = V(ve.tensor_tensor, [m2], mv, bv, gm, ALU.mult)
        m2 = V(ve.tensor_scalar, [m2], rank[:, i, :], gs[:, i, :], 1.0, 1.0e30, ALU.subtract, ALU.mult)
        m2 = V(ve.tensor_tensor, [m1, m2], mv, mv, rank[:, i, :].unsqueeze(2).to_broadcast([P, 8, 8]), ALU.add)
        m2 = V(ve.max, [m2], top8[:, i, :], mk[:, i, :])
        m2 = V(ve.match_replace, [m2], rep[:, i, :], top8[:, i, :], mk[:, i, :], -3.0e38)
        both.append(V(ve.tensor_tensor, [m2], rep[:, i, :], mk[:, i, :], rep[:, i, :], ALU.not_equal))
    m = both[1]
    m_sel = m
    m = V(ve.tensor_tensor, [m], mk, rep, sc, ALU.mult)
    m = V(ve.tensor_reduce, [m], den, mk, AX, ALU.add)
    m = V(ve.tensor_scalar, [m], den, den, 1e-20, None, ALU.add)
    m = V(ve.reciprocal, [m], den, den)
    for i in range(2):
        m_w = V(ve.tensor_scalar, [m], mk[:, i, :], mk[:, i, :], den[:, i:i + 1], 2.5, ALU.mult, ALU.mult)
    yield
    m_b = V(ve.tensor_tensor, [], below, ones, C("from_s"), ALU.subtract)
    mm(b.t[:, 0:64], [(below, rep[:, 0, :])], [m_sel, m_b] + b.w)
    mm(b.t[:, 64:128], [(ones, rep[:, 0, :]), (below, rep[:, 1, :])], [])
    m = mm(b.t[0:64, 128:129], [(rep[:, i, :], ones[:, 0:1]) for i in range(2)], [])
    m1 = V(ve.scalar_tensor_tensor, [m], posm, b.t[:, 0:128].rearrange("p (i e) -> p i e", i=2), 1.0, rep,
           ALU.add, ALU.mult)
    m_p = V(ve.tensor_scalar, [m1], posm, posm, -1.0, None, ALU.add)
    m = V(ve.tensor_copy, [m], count[0:64, :], b.t[0:64, 128:129])
    b.free(m, m_p)
    yield mk, posm, count, below, [m_w, m_p], keep


def blocks_beyond(nc, S, l, count, below, b, room):
    V = S["V"]
    ve = nc.vector
    mm, C, ident, iota = S["mm"], S["C"], S["ident"], S["C"]("iota")
    at = [0]

    def take(n):
        at[0] += n
        return room[:, at[0] - n:at[0]]

    e_x, t_x = S["pcol"](MORE), S["pcol"](MORE)
    e_int, n_int = S["pcol"](MORE).bitcast(I32), S["pcol"](1).bitcast(I32)
    nb, t1, upto, none = take(1), take(1), take(64), take(MORE)
    se, nrow = take(P).rearrange("p (a e) -> p a e", a=2), take(64)
    over = take(MORE * 64).rearrange("p (x e) -> p x e", x=MORE)
    m = V(ve.tensor_scalar, [], nb[0:64, :], count[0:64, :], SLOTS + 0.5, None, ALU.is_gt)
    for q in (2, 3):
        m1 = V(ve.tensor_scalar, [m], t1[0:64, :], count[0:64, :], q * SLOTS + 0.5, None, ALU.is_gt)
        m = V(ve.tensor_tensor, [m, m1], nb[0:64, :], nb[0:64, :], t1[0:64, :], ALU.add)
    m1 = V(ve.tensor_tensor, [], upto[0:64, :], below[0:64, 0:64], ident[0:64, 0:64], ALU.add)
    by_e = nb[0:64, 0:1].to_broadcast([64, P])
    mm(b.t[:, 0:64], [(by_e, below[0:64, 0:64])], [m, m1] + b.w)
    m = mm(b.t[:, 64:128], [(by_e, upto[0:64, :])], [])
    m = V(ve.tensor_copy, [m], se, b.t[:, 0:128].rearrange("p (a e) -> p a e", a=2))
    b.free(m)
    yield
    m_n = V(ve.tensor_tensor, [m], nrow, se[:, 1, :], se[:, 0, :], ALU.subtract)
    m1 = V(ve.tensor_copy, [m], n_int, se[:, 1, 63:64])
    m2 = V(ve.tensor_scalar, [m], none, iota[:, 0:MORE], se[:, 1, 63:64], 1.0e6, ALU.is_ge, ALU.mult)
    yield
    m = V(ve.tensor_tensor, [m], over, se[:, 1, :].unsqueeze(1).to_broadcast([P, MORE, 64]),
          iota[:, 0:MORE].unsqueeze(2).to_broadcast([P, MORE, 64]), ALU.is_le)
    yield
    m3 = V(ve.tensor_reduce, [m], e_x, over, AX, ALU.add)
    yield
    m = V(ve.tensor_tensor, [m, m3, m_n], over, over, nrow.unsqueeze(1).to_broadcast([P, MORE, 64]), ALU.mult)
    yield
    m = V(ve.tensor_reduce, [m], t_x, over, AX, ALU.add)
    m = V(ve.tensor_tensor, [m], t_x, iota[:, 0:MORE], t_x, ALU.subtract)
    m = V(ve.tensor_scalar, [m], t_x, t_x, 1.0, float(SLOTS), ALU.add, ALU.mult)
    m = V(ve.tensor_tensor, [m, m2], t_x, t_x, none, ALU.add)
    m3 = V(ve.tensor_scalar, [m3], e_x, e_x, float(EXPERTS - 1), None, ALU.min)
    m3 = V(ve.tensor_copy, [m3], e_int, e_x)
    V.wait([m, m3])
    yield e_x, t_x, e_int, n_int, [m, m1, m3]


def moe(nc, S, l, h, m_h, mod):
    V, A, T, SP = S["V"], S["A"], S["T"], S["SP"]
    te, ac, ve = nc.tensor, nc.scalar, nc.vector
    mm, C, carve, banks, ring, xT, ident = S["mm"], S["C"], S["carve"], S["banks"], S["ring"], S["xT"], S["ident"]
    iota, I = C("iota"), S["I"]
    S["settle"]()
    S["top"][0] = 0
    ps = banks.bufs
    yb = [b.t for b in ps[0:4]]
    gb, ub, ob = ps[4], ps[5], ps[6:8]
    for b in ps:
        b.free()

    flat, ml = ring.get(("router", l))
    w = flat[:, 0:512].rearrange("p (k e) -> p k e", k=8)
    rb = ob[1]
    for i in range(2):
        m = mm(rb.t[:, i * 64:(i + 1) * 64], [(h[:, kk, i * P:(i + 1) * P], w[:, kk, :]) for kk in range(8)], [ml],
               each=m_h)
    ring.release(("router", l), m)
    choice = route(nc, S, l, h, m, rb)
    next(choice)
    flat, ml = ring.get(("up", l, EXPERTS))
    w1 = flat[:, 0:UNIT].rearrange("p (k f) -> p k f", k=8)
    w3 = flat[:, UNIT:2 * UNIT].rearrange("p (k f) -> p k f", k=8)
    hx = S["hT"][:, 2048:4096].rearrange("p (i d) -> p i d", i=2)
    gs, ss = [S["ar"][:, n:n + 512].rearrange("p (j t) -> p j t", j=2) for n in (AR_COLS - 1024, AR_COLS - 512)]
    mg = []
    for j, b in enumerate((gb, ub)):
        mm(b.t[:, 0:256], [(w1[:, kk, j::2], h[:, kk, :]) for kk in range(8)], [ml])
        m = mm(b.t[:, 256:512], [(w3[:, kk, j::2], h[:, kk, :]) for kk in range(8)], [])
        ms = A(ac.activation, [m], ss[:, j, :], b.t[:, 0:256], ACT.Silu)
        mg.append(V(ve.tensor_tensor, [ms], gs[:, j, :], ss[:, j, :], b.t[:, 256:512], ALU.mult))
        b.free(mg[j])
    ring.release(("up", l, EXPERTS), m)
    for i in range(2):
        for q in range(2):
            b = (ob[0], gb, ub)[(2 * i + q) % 3]
            T.wait(b.w)
            for k in range(4):
                ins = te.transpose(b.t[:, k * P:(k + 1) * P], h[:, 4 * q + k, i * P:(i + 1) * P], ident)
            m = T.done(ins)
            m_hx = A(ac.activation, [m], hx[:, i, q * 512:(q + 1) * 512], b.t[:, :], ACT.Copy)
            b.free(m_hx)
    mk, posm, count, below, m_r, keep = next(choice)
    flat, ml = ring.get(("down", l, EXPERTS))
    w2 = flat[:, 0:UNIT].rearrange("p (j n) -> p j n", j=2)
    T.wait([ml] + mg)
    for k in range(8):
        o = yb[k // 2][:, (k % 2) * 256:(k % 2) * 256 + 256]
        for j in range(2):
            ins = te.matmul(o, w2[:, j, k::8], gs[:, j, :], start=(j == 0 and k % 2 == 0), stop=False,
                            skip_group_check=True)
    m = T.done(ins)
    ring.release(("down", l, EXPERTS), m)

    S["top"][0] = keep
    V.wait([V.last(), m_hx])
    f_s = Rot([carve(2, P) for _ in range(2)])
    f_w = Rot([carve(2, P) for _ in range(2)])
    x_b, u_b, g_b, o_b, t_b = Buf(carve(8, P)), Buf(carve(256)), Buf(carve(256)), Buf(carve(1024)), Buf(carve(512))
    T.wait([T.last(), V.last()])
    more_one, more_pick, more_at = carve(2, 64), carve(2, 2, 2 * 64), carve(2, 4)
    wbuf = [[carve(2, 2048), carve(2048)], [carve(2, 2048), S["hT"][:, 0:2048]]]
    work = Rot(None, ps[4:8])
    both = (slice(0, SLOTS), slice(SLOTS, P))

    def load_more(x, sp, waits):
        sem = S["more"][l][3][x % 2]
        sp.wait(waits)
        e = nc.sync.value_load(e_int[0:1, x:x + 1], min_val=0, max_val=EXPERTS - 1)
        a, b = wbuf[x % 2]
        for dst, n, k in ((a[:, 0, :], "w1", 8), (a[:, 1, :], "w3", 8), (b, "w2", 2)):
            src = I[n][l][bass.ds(e, 1), :, :].rearrange("a (p k) f -> p (a k f)", k=k)
            nc.sync.dma_start(dst, src).then_inc(sem, 16)
        return (sem, 48 * (x // 2 + 1), f"more{l}{x % 2}")

    def select(p):
        s, w = f_s.take(), f_w.take()
        for u in range(2):
            e = 2 * p + u
            for i in range(2):
                at = posm[:, i, e:e + 1]
                ms = V(ve.tensor_scalar, m_r + s.w, s.t[:, i, both[u]], iota, at, None, ALU.is_equal)
                mw = V(ve.tensor_scalar, w.w, w.t[:, i, both[u]], iota, at, mk[:, i, e:e + 1], ALU.is_equal,
                       ALU.mult)
        return s, ms, w, mw

    def select_more():
        s, w = f_s.take(), f_w.take()
        pick = more_pick.rearrange("p b a (i e) -> p b a i e", i=2)
        V.wait(s.w + w.w)
        ms = choose(V, nc, iota, (posm, mk, e_x, t_x), 0, s.t, w.t, more_one, pick, more_at)
        return s, ms, w, ms

    def gather(s, ms):
        m_x = []
        for q in range(2):
            b = work.take()
            T.wait([ms] + b.w)
            for k in range(4):
                c = (4 * q + k) * P
                for i in range(2):
                    ins = te.matmul(b.t[:, k * P:(k + 1) * P], hx[:, i, c:c + P], s.t[:, i, :], start=(i == 0),
                                    stop=(i == 1))
            m = T.done(ins)
            src = b.t[:, :].rearrange("p (k s) -> p k s", k=4)
            if q == 0:
                m_x.append(A(ac.activation, [m] + x_b.w, x_b.t[:, 0:4, :], src, ACT.Copy))
            else:
                m_x.append(V(ve.tensor_copy, [m] + x_b.w, x_b.t[:, 4:8, :], src))
            b.free(m_x[q])
        s.free(m)
        return m_x

    def up(p, m_x):
        b = work.take()
        T.wait(m_x + b.w)
        w = []
        for u in range(2):
            flat, ml = ring.get(("up", l, 2 * p + u)) if p < pairs else (wbuf[u][0].rearrange("p m n -> p (m n)"),
                                                                         m_wx[u])
            T.wait([ml])
            w.append(flat[:, 0:2 * UNIT].rearrange("p (m k f) -> p m k f", m=2, k=8))
        for kk in range(8):
            for u in range(2):
                ins = te.matmul(b.t[both[u], :], x_b.t[:, kk, both[u]], w[u][:, :, kk, :], start=(kk == 0),
                                stop=(kk == 7))
        m = T.done(ins)
        x_b.free(m)
        for u in range(2):
            if p < pairs:
                ring.release(("up", l, 2 * p + u), m)
        ms = A(ac.activation, [m] + u_b.w, u_b.t, b.t[:, 0:256], ACT.Silu)
        m = V(ve.tensor_tensor, [ms] + g_b.w, g_b.t, u_b.t, b.t[:, 256:512], ALU.mult)
        u_b.free(m)
        b.free(m)
        return m

    def turn(mg, w, mw):
        b = work.take()
        T.wait([mg, mw] + b.w)
        for j in range(2):
            te.transpose(b.t[:, j * P:(j + 1) * P], g_b.t[:, j::2], ident)
        for i in range(2):
            ins = te.transpose(b.t[:, 256 + i * P:256 + (i + 1) * P], w.t[:, i, :], ident)
        m = T.done(ins)
        g_b.free(m)
        w.free(m)
        m = V(ve.tensor_copy, [m] + t_b.w, t_b.t, b.t[:, :])
        b.free(m)
        return m

    def down(p, mt):
        w = []
        for u in range(2):
            flat, ml = ring.get(("down", l, 2 * p + u)) if p < pairs else (wbuf[u][1], m_wx[u])
            T.wait([ml])
            w.append(flat[:, 0:UNIT].rearrange("p (j n) -> p j n", j=2))
        m_o = []
        for q in range(2):
            b = work.take()
            T.wait([mt] + b.w)
            for j in range(2):
                for u in range(2):
                    ins = te.matmul(b.t[both[u], :], t_b.t[:, j * P + u * SLOTS:j * P + (u + 1) * SLOTS],
                                    w[u][:, j, q * 512:(q + 1) * 512], start=(j == 0), stop=(j == 1))
            m = T.done(ins)
            if q == 0:
                m_o.append(A(ac.activation, [m] + o_b.w, o_b.t[:, 0:512], b.t[:, :], ACT.Copy))
            else:
                m_o.append(V(ve.tensor_copy, [m] + o_b.w, o_b.t[:, 512:1024], b.t[:, :]))
            b.free(m_o[q])
        for u in range(2):
            if p < pairs:
                ring.release(("down", l, 2 * p + u), m)
        return m_o

    def scatter(m_o):
        T.wait(m_o)
        for k in range(8):
            ins = te.matmul(yb[k // 2][:, (k % 2) * 256:(k % 2) * 256 + 256], o_b.t[:, k::8], t_b.t[:, 256:512],
                            start=False, stop=False, skip_group_check=True)
        m = T.done(ins)
        o_b.free(m)
        t_b.free(m)

    pairs = EXPERTS // 2
    listing = blocks_beyond(nc, S, l, count, below, work.bufs[0], wbuf[0][0].rearrange("p a n -> p (a n)"))
    listed = None
    s, ms, w, mw = select(0)
    m_x, m_o = gather(s, ms), None
    for p in range(pairs + 1):
        mg = up(p, m_x)
        if p < pairs:
            nxt = select(p + 1) if p + 1 < pairs else select_more()
        if m_o:
            scatter(m_o)
        mt = turn(mg, w, mw)
        if p == 4 or p > 4 and listed is None:
            listed = next(listing)
        if p < pairs:
            s, ms, w, mw = nxt
            m_x = gather(s, ms)
        m_o = down(p, mt)
        if p == pairs // 2:
            e_x, t_x, e_int, n_int, m_more = listed
            m_wx = [load_more(x, SP, m_more) for x in range(2)]
    scatter(m_o)

    S["barrier"]()
    SP.wait([e.last() for e in (T, A, V)])
    total = nc.values_load(n_int[0:1, 0:1], min_val=0, max_val=MORE)
    tiles = (hx, posm, mk, e_x, t_x, wbuf, f_s.bufs[0].t, f_s.bufs[1].t, f_w.bufs[0].t, f_w.bufs[1].t, x_b.t, u_b.t,
             g_b.t, o_b.t, t_b.t, yb, [b.t for b in ps[4:8]])

    def chain(q):
        with nc.If(total > 2 * q):
            m_w = [load_more(x, SP, []) for x in (2 * q, 2 * q + 1)]
            beyond(nc, S, l, 2 * q, m_w, tiles)
            if 2 * q + 2 < MORE:
                chain(q + 1)
        with nc.Else():
            pass

    chain(1)
    for e in (T, A, V, S["G"], SP):
        e.wait(m_wx)
    marks = []
    for k in range(8):
        o = yb[k // 2][:, (k % 2) * 256:(k % 2) * 256 + 256]
        marks.append(V(ve.scalar_tensor_tensor, [], xT[:, k, 256:512], o, mod[:, 0, 5, k:k + 1], xT[:, k, 256:512],
                       ALU.mult, ALU.add))
    for b in banks.bufs:
        b.free(marks[-1])
    return marks


def choose(V, nc, iota, lists, x0, s, w, one, pick, at):
    ve = nc.vector
    posm, mk, e_x, t_x = lists
    for b in range(2):
        x, n = x0 + b, slice(b * SLOTS, (b + 1) * SLOTS)
        m = V(ve.tensor_scalar, [], one[:, b], iota, e_x[:, x:x + 1], None, ALU.is_equal)
        for a, src in enumerate((posm, mk)):
            m1 = V(ve.tensor_tensor, [m], pick[:, b, a], src, one[:, b].unsqueeze(1).to_broadcast([P, 2, 64]),
                   ALU.mult)
            m1 = V(ve.tensor_reduce, [m1], at[:, b, 2 * a:2 * a + 2], pick[:, b, a], AX, ALU.add)
        m = V(ve.tensor_scalar, [m1], at[:, b, 0:2], at[:, b, 0:2], t_x[:, x:x + 1], None, ALU.subtract)
        for i in range(2):
            V(ve.tensor_scalar, [m], s[:, i, n], iota, at[:, b, i:i + 1], None, ALU.is_equal)
            ms = V(ve.tensor_scalar, [], w[:, i, n], iota, at[:, b, i:i + 1], at[:, b, 2 + i:3 + i], ALU.is_equal,
                   ALU.mult)
    return ms


def beyond(nc, S, l, x0, m_wt, tiles):
    T, A, V = S["more"][l][0:3]
    te, ac, ve = nc.tensor, nc.scalar, nc.vector
    ident, iota = S["ident"], S["C"]("iota")
    hx, posm, mk, e_x, t_x, wbuf, s, one, w, at, xs, u, g, o, t, yb, (g0, g1, ob0, ob1) = tiles
    both = (slice(0, SLOTS), slice(SLOTS, P))
    pick = o[:, 0:512].rearrange("p (b a i e) -> p b a i e", b=2, a=2, i=2)
    at = at[:, 0, 0:8].rearrange("p (b n) -> p b n", b=2)
    ms = choose(V, nc, iota, (posm, mk, e_x, t_x), x0, s, w, one.rearrange("p i n -> p (i n)")[:, 0:P].rearrange("p (b n) -> p b n", b=2), pick, at)
    T.wait([ms])
    m_x = []
    for q, b in enumerate((g0, ob0)):
        for k in range(4):
            c = (4 * q + k) * P
            for i in range(2):
                ins = te.matmul(b[:, k * P:(k + 1) * P], hx[:, i, c:c + P], s[:, i, :], start=(i == 0), stop=(i == 1))
        m = T.done(ins)
        src, dst = b[:, :].rearrange("p (k s) -> p k s", k=4), xs[:, 4 * q:4 * q + 4, :]
        m_x.append(A(ac.activation, [m], dst, src, ACT.Copy) if q == 0 else V(ve.tensor_copy, [m], dst, src))
    T.wait(m_x + m_wt)
    wts = [wbuf[b] for b in range(2)]
    for kk in range(8):
        for b in range(2):
            w13 = wts[b][0].rearrange("p m (k f) -> p m k f", k=8)
            ins = te.matmul(g1[both[b], :], xs[:, kk, both[b]], w13[:, :, kk, :], start=(kk == 0), stop=(kk == 7))
    m = T.done(ins)
    m = A(ac.activation, [m], u, g1[:, 0:256], ACT.Silu)
    m = V(ve.tensor_tensor, [m], g, u, g1[:, 256:512], ALU.mult)
    T.wait([m])
    for j in range(2):
        te.transpose(g0[:, j * P:(j + 1) * P], g[:, j::2], ident)
    for i in range(2):
        ins = te.transpose(g0[:, 256 + i * P:256 + (i + 1) * P], w[:, i, :], ident)
    m = T.done(ins)
    mt = V(ve.tensor_copy, [m], t, g0[:, :])
    T.wait([mt])
    m_o = []
    for q, bank in enumerate((ob0, ob1)):
        for j in range(2):
            for b in range(2):
                w2 = wts[b][1].rearrange("p (j n) -> p j n", j=2)
                ins = te.matmul(bank[both[b], :], t[:, j * P + b * SLOTS:j * P + (b + 1) * SLOTS],
                                w2[:, j, q * 512:(q + 1) * 512], start=(j == 0), stop=(j == 1))
        m = T.done(ins)
        if q == 0:
            m_o.append(A(ac.activation, [m, ms], o[:, 0:512], bank[:, :], ACT.Copy))
        else:
            m_o.append(V(ve.tensor_copy, [m], o[:, 512:1024], bank[:, :]))
    T.wait(m_o)
    for k in range(8):
        ins = te.matmul(yb[k // 2][:, (k % 2) * 256:(k % 2) * 256 + 256], o[:, k::8], t[:, 256:512], start=False,
                        stop=False, skip_group_check=True)
    T.done(ins)
    for e in (T, A, V):
        e.wait([T.last(), A.last(), V.last()])
    for e in (nc.gpsimd, nc.sync):
        for src in (T, A, V):
            e.wait_ge(src.sem, src.n)


def second_block(nc, S, marks):
    V, A, T, G = S["V"], S["A"], S["T"], S["G"]
    te, ac, ve, gp = nc.tensor, nc.scalar, nc.vector, nc.gpsimd
    mm, tr, C, carve, reset, banks, ring, rstd = (S["mm"], S["tr"], S["C"], S["carve"], S["reset"], S["banks"],
                                                  S["ring"], S["rstd"])
    I, PM, xT, ident, ones = S["I"], S["PM"], S["xT"], S["ident"], S["ones"]
    top, barrier = S["top"], S["barrier"]
    h = S["hT"][:, :].rearrange("p (k t) -> p k t", k=8)
    seg2 = lambda a: a.rearrange("p (s t) -> p s t", s=2)

    top[0] = 0
    mod = S["mods2"][0]
    sc, gt = S["scales2"](0)
    keep = top[0]
    sq_t, r_t = carve(8, 512), carve(512)
    m_h = S["norm_modulate"]((0, 512), h, [sc[:, 0, :], sc[:, 1, :]], [mod[:, 0, 0, :], mod[:, 1, 0, :]], sq_t, r_t, marks)
    S["settle"]()
    top[0] = keep
    yp, ym = carve(8, 512), carve(8, 512)
    keep = top[0]
    spare = ym.rearrange("p k t -> p (k t)")
    g16 = spare[:, 0:512]
    gates = spare[:, 512:2560].rearrange("p (j t) -> p j t", j=4)
    tmp = spare[:, 2560:3584].rearrange("p (j t) -> p j t", j=2)
    aR = spare[:, 3584:4096]
    nM = [carve(512) for _ in range(2)]
    acol, ecol = carve(4, 2, 4), carve(4, 2, 4)
    keep = top[0]

    def scan_stream():
        flat, ml = ring.get(("gates",))
        w = flat[:, 0:128].rearrange("p (k n) -> p k n", k=8)
        b = banks.take()
        m = mm(b.t[0:16, :], [(w[:, kk, :], h[:, kk, :]) for kk in range(8)], [ml] + b.w)
        ring.release(("gates",), m)
        yield
        mg = A(ac.activation, [m], g16[0:16, :], b.t[0:16, :], ACT.Copy)
        b.free(mg)
        yield
        for t in range(4):
            b = banks.take()
            m = mm(b.t[0:4, :], [(ident[0:16, 4 * t:4 * t + 4], g16[0:16, :])], [mg] + b.w)
            m = A(ac.activation, [m], gates[0:4, t, :], b.t[0:4, :], ACT.Identity, bias=S["bgate"][0:4, t:t + 1])
            b.free(m)
            yield
        m_gt = m
        for d in range(2):
            li, lf = gates[0:4, 2 * d, :], gates[0:4, 2 * d + 1, :]
            e, B = tmp[0:4, 0, :], tmp[0:4, 1, :]
            m = A(ac.activation, [m_gt, V.last(), T.last()], e, lf, ACT.Abs)
            m = A(ac.activation, [m], e, e, ACT.Exp, scale=-1.0)
            yield
            m = A(ac.activation, [m], e, e, ACT.Ln, bias=ones[0:4, 0:1])
            m = V(ve.scalar_tensor_tensor, [m], lf, lf, 0.0, e, ALU.min, ALU.subtract)

            def scans(dst, src, op, init, m):
                if d == 0:
                    return V(ve.tensor_tensor_scan, [m], dst, src, src, init, op, ALU.bypass)
                m = V(ve.tensor_tensor_scan, [m], seg2(dst)[:, 0, ::-1],
                      seg2(src)[:, 0, ::-1], seg2(src)[:, 0, ::-1], init, op, ALU.bypass)
                return V(ve.tensor_tensor_scan, [m], seg2(dst)[:, 1, ::-1], seg2(src)[:, 1, ::-1],
                         seg2(src)[:, 1, ::-1], dst[:, 0:1], op, ALU.bypass)

            yield
            m = scans(B, lf, ALU.add, 0.0, m)
            yield
            m = V(ve.tensor_tensor, [m, T.last()], aR[0:4, :], li, B, ALU.subtract)
            yield
            m = scans(nM[d][0:4, :], aR[0:4, :], ALU.max, 0.0, m)
            m = V(ve.tensor_scalar, [m], nM[d][0:4, :], nM[d][0:4, :], -1.0, None, ALU.mult)
            nMB = e
            m = V(ve.tensor_tensor, [m], nMB, nM[d][0:4, :], B, ALU.subtract)
            yield
            b = banks.take()
            for j in range(4):
                tr(b.t[:, j * 4:j * 4 + 4], aR[0:4, j * P:(j + 1) * P], ident[0:4, 0:4], [m] + b.w)
                mt = tr(b.t[:, 16 + j * 4:20 + j * 4], nMB[:, j * P:(j + 1) * P], ident[0:4, 0:4], [])
            m1 = A(ac.activation, [mt], acol[:, :, d, :], b.t[:, 0:16].rearrange("p (j h) -> p j h", j=4), ACT.Copy)
            m2 = A(ac.activation, [mt], ecol[:, :, d, :], b.t[:, 16:32].rearrange("p (j h) -> p j h", j=4), ACT.Exp)
            b.free(m2)
            yield

    scan_steps = scan_stream()
    pad = Rot([carve(2, 272) for _ in range(2)])
    lev = [Rot([carve(2, 272) for _ in range(1)]) for _ in range(2)]
    dif = Rot([carve(2, 512) for _ in range(2)])
    sgr = Rot([carve(512) for _ in range(2)])
    mz = None
    for b_ in pad.bufs:
        mz = G(gp.memset, [], b_.t, 0.0)
        b_.free(mz)
    pflat, mpw = ring.get(("poolw",))
    pw = pflat.rearrange("p (c n) -> p c n", c=8)
    for g in range(4):
        flat, ml = ring.get(("pin", g))
        w = flat.rearrange("p (k n) -> p k n", k=8)
        df = dif.take()
        for c in range(2):
            b = banks.take()
            m = mm(b.t[:, :], [(w[:, kk, c * P:(c + 1) * P], h[:, kk, :]) for kk in range(8)], [ml] + b.w, each=m_h)
            p = pad.take()
            m = A(ac.activation, [m] + p.w, p.t[:, :, 8:264], seg2(b.t[:, :]), ACT.Copy)
            b.free(m)
            src = p.t
            lo, hi = 1, 272
            for lv in range(g + 1):
                o = lev[lv % 2].bufs[0].t
                if lv == 0:
                    m = V(ve.tensor_tensor, [m, V.last()], o[:, :, 1:272], src[:, :, 0:271], src[:, :, 1:272], ALU.add)
                else:
                    d = 1 << (lv - 1)
                    lo, hi = lo + d, hi - d
                    m = V(ve.tensor_tensor, [m], o[:, :, lo:hi], src[:, :, lo - d:hi - d], src[:, :, lo + d:hi + d],
                          ALU.add)
                src = o
            rec = C("recip")[:, g * 256:(g + 1) * 256].unsqueeze(1).to_broadcast([P, 2, 256])
            o = lev[(g + 1) % 2].bufs[0].t
            m = V(ve.tensor_tensor, [m], o[:, :, 8:264], src[:, :, 8:264], rec, ALU.mult)
            m_d = V(ve.tensor_tensor, [m] + df.w, seg2(df.t[:, c, :]), o[:, :, 8:264], p.t[:, :, 8:264],
                    ALU.subtract)
            p.free(m_d)
            next(scan_steps, None)
            next(scan_steps, None)
        ring.release(("pin", g), T.last())
        flat, ml = ring.get(("pgate", g))
        w = flat.rearrange("p (k n) -> p k n", k=8)
        for c in range(2):
            b = banks.take()
            m = mm(b.t[:, :], [(w[:, kk, c * P:(c + 1) * P], h[:, kk, :]) for kk in range(8)], [ml] + b.w)
            s = sgr.take()
            ms = A(ac.activation, [m] + s.w, s.t, b.t[:, :], ACT.Silu)
            b.free(ms)
            b = banks.take()
            m = mm(b.t[:, :], [(pw[:, 2 * g + cc, c * P:(c + 1) * P], df.t[:, cc, :]) for cc in range(2)],
                   [mpw, m_d] + b.w)
            mv = V(ve.scalar_tensor_tensor, [m, ms], yp[:, 2 * g + c, :], b.t[:, :],
                   PM["pscale"][:, 2 * g + c:2 * g + c + 1], s.t, ALU.mult, ALU.mult)
            b.free(mv)
            s.free(mv)
            next(scan_steps, None)
        df.free(m)
        ring.release(("pgate", g), m)
    ring.release(("poolw",), m)
    m_yp = mv
    for _ in scan_steps:
        pass
    barrier()
    top[0] = keep
    vaug = carve(4, 257)
    qT, kT = carve(2, 512), carve(2, 512)
    oh = kT.rearrange("p a t -> p (a t)").rearrange("p (j e) -> p j e", j=4)
    zT = qT
    hs = carve(4, 256)
    upad = Rot([carve(2, 258)])
    Cd = carve(4, 512)
    dm = ym[:, 7, :].rearrange("p (j t) -> p j t", j=4)
    stt = carve(4, 4)
    ss = carve(8)
    for b_ in upad.bufs:
        b_.free(G(gp.memset, [], b_.t, 0.0))
    mone = G(gp.memset, [], vaug[:, :, 256:257], 1.0)
    cv = PM["conv"]
    m_hs = finish = None
    oz, every = banks.bufs[4:8], banks
    banks = Rot(None, every.bufs[0:4])
    for hd in range(4):
        def project(n, c):
            flat, ml = ring.get((n, hd))
            w = flat.rearrange("p (k n) -> p k n", k=8)
            b = banks.take()
            m = mm(b.t[:, :], [(w[:, kk, c * P:(c + 1) * P], h[:, kk, :]) for kk in range(8)], [ml] + b.w)
            if c == 1:
                ring.release((n, hd), m)
            return b, m

        def convolve(n, c, b, m):
            u = upad.take()
            m = A(ac.activation, [m] + u.w, u.t[:, :, 1:257], seg2(b.t[:, :]), ACT.Copy)
            b.free(m)
            ch = (0 if n == "q" else 8) + hd * 2 + c
            o = seg2((qT if n == "q" else kT)[:, c, :])
            m = V(ve.tensor_scalar, [m], o, u.t[:, :, 0:256], cv[:, ch:ch + 1], None, ALU.mult)
            for j in (1, 2):
                m = V(ve.scalar_tensor_tensor, [m], o, u.t[:, :, j:j + 256], cv[:, 16 * j + ch:16 * j + ch + 1], o,
                      ALU.mult, ALU.add)
            u.free(m)
            return m

        first = [project("q", 0), project("q", 1)]
        if finish is not None:
            finish()
        V.wait([e.last() for e in (T, A, V, G)])
        for c in range(2):
            convolve("q", c, *first[c])
        for c in range(2):
            m = convolve("k", c, *project("k", c))
        m_qk = m
        flat, ml = ring.get(("v", hd))
        w = flat.rearrange("p (k n) -> p k n", k=8)
        A.wait([V.last(), G.last(), T.last()])
        for j in range(4):
            b = banks.take()
            m = mm(b.t[:, 0:256], [(h[:, kk, j * P:(j + 1) * P], w[:, kk, :]) for kk in range(8)], [ml] + b.w)
            m_v = A(ac.activation, [m], vaug[:, j, 0:256], b.t[:, 0:256], ACT.Copy)
            b.free(m_v)
        ring.release(("v", hd), m)
        m_oz = []

        def outer_gates():
            flat, ml = ring.get(("o", hd))
            w = flat.rearrange("p (k n) -> p k n", k=8)
            for j in range(4):
                m_oz.append(mm(oz[j // 2].t[:, (j % 2) * 256:(j % 2) * 256 + 256],
                               [(h[:, kk, j * P:(j + 1) * P], w[:, kk, :]) for kk in range(8)], [ml] + oz[j // 2].w))
                yield
            ring.release(("o", hd), m_oz[-1])
            flat, ml = ring.get(("z", hd))
            w = flat.rearrange("p (k n) -> p k n", k=8)
            for c in range(2):
                for half in range(2):
                    cols = slice(half * 256, half * 256 + 256)
                    m_oz.append(mm(oz[2 + c].t[:, cols],
                                   [(w[:, kk, c * P:(c + 1) * P], h[:, kk, cols]) for kk in range(8)],
                                   [ml] + oz[2 + c].w))
                    yield
            ring.release(("z", hd), m_oz[-1])

        outer = outer_gates()
        for d in range(2):
            b = banks.take()
            m_nm = mm(b.t[:, :], [(ident[0:4, hd:hd + 1].to_broadcast([4, P]), nM[d][0:4, :])], b.w)
            tri = C("tri_f" if d == 0 else "tri_b").unsqueeze(1).to_broadcast([P, 4, P])
            m = V(ve.tensor_tensor, [m_nm, T.last(), A.last()], dm, b.t[:, :].rearrange("p (j t) -> p j t", j=4),
                  tri, ALU.add)
            next(outer, None)
            next(outer, None)
            spans = []
            for i in range(4):
                bias = acol[:, i, d, hd:hd + 1]
                lo, hi = i * P, (i + 1) * P
                if d == 0:
                    rest = [(hi, 512)]
                elif i < 2:
                    rest = [(0, lo), (256, 512)]
                else:
                    rest = [(256, lo)]
                A(ac.activation, [m], Cd[:, i, lo:hi], dm[:, i, :], ACT.Exp, bias=bias)
                me = A.last()
                for r0, r1 in rest:
                    if r1 > r0:
                        me = A(ac.activation, [m_nm], Cd[:, i, r0:r1], b.t[:, r0:r1], ACT.Exp, bias=bias)
                sp = [(lo, hi)] + [r for r in rest if r[1] > r[0]]
                sp.sort()
                out_ = [sp[0]]
                for r in sp[1:]:
                    if r[0] == out_[-1][1]:
                        out_[-1] = (out_[-1][0], r[1])
                    else:
                        out_.append(r)
                spans.append((out_, me))
            b.free(me, m)
            for i in range(4):
                b = banks.take()
                t0 = 0 if i < 2 else 256
                m_s = m = mm(b.t[:, t0:512], [(kT[:, c, i * P:(i + 1) * P], qT[:, c, t0:512]) for c in range(2)],
                       [m_qk] + b.w)
                for r0, r1 in spans[i][0]:
                    mc = V(ve.scalar_tensor_tensor, [m, spans[i][1]], Cd[:, i, r0:r1], b.t[:, r0:r1], 0.0625,
                           Cd[:, i, r0:r1], ALU.mult, ALU.mult)
                b.free(mc)
                if i % 2 == 1:
                    next(outer, None)
            for j in range(4):
                if d == 0:
                    src = list(range(j + 1))
                elif j < 2:
                    src = list(range(j, 2))
                else:
                    src = [0, 1] + list(range(j, 4))
                b = banks.take()
                m = mm(b.t[:, 0:257], [(Cd[:, i, j * P:(j + 1) * P], vaug[:, i, :]) for i in src],
                       [mc, m_v, mone] + b.w)
                st = stt[:, j, 2 * d:2 * d + 1]
                m = A(ac.activation, [m], st, b.t[:, 256:257], ACT.Abs)
                m = V(ve.tensor_tensor, [m], st, st, ecol[:, j, d, hd:hd + 1], ALU.max)
                m = V(ve.reciprocal, [m], st, st)
                if d == 0:
                    m_hs = V(ve.tensor_scalar, [m], hs[:, j, :], b.t[:, 0:256], st, None, ALU.mult)
                else:
                    m_hs = V(ve.scalar_tensor_tensor, [m], hs[:, j, :], b.t[:, 0:256], st, hs[:, j, :], ALU.mult,
                             ALU.add)
                b.free(m_hs)
        for _ in outer:
            pass
        for q in range(2):
            m_o = A(ac.activation, [m_oz[-1], m_s], oh[:, 2 * q:2 * q + 2, :],
                    oz[q].t[:, :].rearrange("p (j e) -> p j e", j=2), ACT.Sigmoid)
            oz[q].free(m_o)
            m_z = A(ac.activation, [m_s], zT[:, q, :], oz[2 + q].t[:, :], ACT.Silu)
            oz[2 + q].free(m_z)
        m = V(ve.tensor_tensor, [m_hs, m_o], hs, hs, oh, ALU.mult)
        for j in range(4):
            mq = A(ac.activation, [m], oh[:, j, :], hs[:, j, :], ACT.Square, accum_out=ss[:, j:j + 1])
        mr = S["rstd_sqrt"](ss[:, 0:4], ss[:, 4:8], 256, [mq])
        for j in range(4):
            m = V(ve.tensor_scalar, [mr], hs[:, j, :], hs[:, j, :], ss[:, 4 + j:5 + j], None, ALU.mult)
        def finish(hd=hd, m=m, m_z=m_z):
            for c in range(2):
                b = banks.take()
                for j in range(4):
                    mt = tr(b.t[:, j * P:(j + 1) * P], hs[:, j, c * P:(c + 1) * P], ident, [m] + b.w)
                mv = V(ve.scalar_tensor_tensor, [mt, m_z], ym[:, 2 * hd + c, :], b.t[:, :],
                       PM["mnorm"][:, 2 * hd + c:2 * hd + c + 1], zT[:, c, :], ALU.mult, ALU.mult)
                b.free(mv)
            return mv

    m_ym = finish()
    barrier()
    banks = every
    fa, ma = ring.get(("about", 0))
    fb, mb = ring.get(("about", 1))
    wa, wb = fa.rearrange("p (c n) -> p c n", c=8), fb.rearrange("p (c n) -> p c n", c=8)
    top[0] = keep

    def product(k, o, waits):
        return mm(o, [(wa[:, c, k::8], ym[:, c, :]) for c in range(8)] + [(wb[:, c, k::8], yp[:, c, :]) for c in range(8)],
                  [ma, mb, m_ym, m_yp] + waits)

    sc2, gt2 = S["scales2"](1)
    marks = project_norm(nc, S, 512, product, [(0, gt[:, 0, :]), (1, gt[:, 1, :])], h, Rot([carve(512) for _ in range(2)]),
                         carve(512))
    ring.release(("about", 0), T.last())
    ring.release(("about", 1), T.last())

    top[0] = keep = 0
    mod = S["mods2"][1]
    sc, gt = sc2, gt2
    sq_t, r_t = carve(8, 512), carve(512)
    m_h = S["norm_modulate"]((0, 512), h, [sc[:, 0, :], sc[:, 1, :]], [mod[:, 0, 0, :], mod[:, 1, 0, :]], sq_t, r_t, marks)
    S["settle"]()
    top[0] = keep
    qT, zT, oT = carve(8, 256), carve(8, 256), carve(8, 256)
    kT, vv, kd = carve(2, 512), carve(4, 256), carve(4, 512)
    axc, axs = C("ax_cos"), C("ax_sin")
    t1r = Rot([carve(256) for _ in range(2)])
    hx = h[:, :, 256:512]

    def rope(dst, m):
        b = banks.take()
        m = mm(b.t[:, 0:256], [(C("swap_pair"), dst)], [m] + b.w)
        t1 = t1r.take()
        mt = V(ve.tensor_tensor, [m] + t1.w, t1.t, b.t[:, 0:256], axs, ALU.mult)
        b.free(mt)
        mg = G(gp.tensor_tensor, [m], dst, dst, axc, ALU.mult)
        m = V(ve.tensor_tensor, [mt, mg], dst, dst, t1.t, ALU.add)
        t1.free(m)
        return m

    flat, ml = ring.get(("cq",))
    w = flat.rearrange("p (k n) -> p k n", k=8)
    for a in range(2):
        for g in range(4):
            b = banks.take()
            m = mm(b.t[:, 0:256], [(w[:, kk, (4 * a + g) * P:(4 * a + g + 1) * P], hx[:, kk, :]) for kk in range(8)],
                   [ml] + b.w, each=m_h)
            ma = A(ac.activation, [m], qT[:, 4 * a + g, :], b.t[:, 0:256], ACT.Copy)
            b.free(ma)
            m_q = rope(qT[:, 4 * a + g, :], ma)
    ring.release(("cq",), m)
    flat, ml = ring.get(("ckv",))
    w = flat.rearrange("p (k n) -> p k n", k=8)
    for a in range(2):
        b = banks.take()
        m = mm(b.t[:, :], [(w[:, kk, a * P:(a + 1) * P], h[:, kk, :]) for kk in range(8)], [ml] + b.w)
        ma = A(ac.activation, [m], kT[:, a, :], b.t[:, :], ACT.Copy)
        b.free(ma)
        mr = rope(kT[:, a, 256:512], ma)
        for u in range(2):
            for half in (0, 64):
                m_k = A(ac.activation, [mr, ma], kd[half:half + 64, 2 * a + u, :], kT[u * 64:u * 64 + 64, a, :], ACT.Copy)
    for j in range(4):
        b = banks.take()
        m = mm(b.t[:, 0:256], [(h[:, kk, j * P:(j + 1) * P], w[:, kk, 256:512]) for kk in range(8)], [ml] + b.w)
        m_v = A(ac.activation, [m], vv[:, j, :], b.t[:, 0:256], ACT.Copy)
        b.free(m_v)
    ring.release(("ckv",), m)
    band = C("band").rearrange("p (i t) -> p i t", i=2)
    zdone, m_oT = [], []

    def gate_stream(b):
        flat, ml = ring.get(("cz",))
        w = flat.rearrange("p (k n) -> p k n", k=8)
        for ch in range(8):
            m = mm(b.t[:, 0:256], [(w[:, kk, ch * P:(ch + 1) * P], hx[:, kk, :]) for kk in range(8)], [ml] + b.w)
            mz = A(ac.activation, [m], zT[:, ch, :], b.t[:, 0:256], ACT.Silu)
            b.free(mz)
            zdone.append(mz)
            if ch == 7:
                ring.release(("cz",), m)
            yield

    def head_stream(chs, bo, bk):
        s, p, st = carve(2, 512), carve(2, 4, P), carve(8, 2)
        w_s, w_p, w_st = [], [], []
        for ch in chs:
            w_bo = list(bo.w)
            for u in range(2):
                hd, kv, base = 2 * ch + u, ch // 2, u * 64
                sink = S["sink"][:, hd:hd + 1]
                both = [mm(bk[i].t[:, :], [(qT[base:base + 64, ch, i * P:(i + 1) * P], kd[base:base + 64, kv, :])],
                           [m_q, m_k] + bk[i].w) for i in range(2)]
                yield
                for i in range(2):
                    m = V(ve.scalar_tensor_tensor, [both[i]] + w_s, s[:, i, :], bk[i].t[:, :], 0.125, band[:, i, :],
                          ALU.mult, ALU.add)
                    bk[i].free(m)
                yield
                m = V(ve.tensor_reduce, [m] + w_st, st[:, 0, :], s, AX, ALU.max)
                m = V(ve.tensor_scalar, [m], st[:, 1, :], st[:, 0, :], sink, -1.0, ALU.max, ALU.mult)
                yield
                for i in range(2):
                    me = A(ac.activation, [m], s[:, i, :], s[:, i, :], ACT.Exp, bias=st[:, 1, i:i + 1],
                           accum_out=st[:, 2, i:i + 1])
                mk = A(ac.activation, [m], st[:, 3, :], st[:, 1, :], ACT.Exp, bias=sink)
                yield
                m = V(ve.tensor_tensor, [mk, me], st[:, 4, :], st[:, 2, :], st[:, 3, :], ALU.add)
                m = V(ve.reciprocal, [m], st[:, 5, :], st[:, 4, :])
                m1 = V(ve.tensor_scalar, [m], s[:, 0, :], s[:, 0, :], st[:, 5, 0:1], None, ALU.mult)
                m2 = A(ac.activation, [m], s[:, 1, :], s[:, 1, :], ACT.Copy, scale=st[:, 5, 1:2])
                w_st = [m1, m2]
                yield
                for i, mi in enumerate((m1, m2)):
                    T.wait([mi] + bk[i].w)
                    for kb in range(4):
                        ins = te.transpose(bk[i].t[:, kb * P:(kb + 1) * P], s[:, i, kb * P:(kb + 1) * P], ident)
                    both[i] = T.done(ins)
                w_s = [both[1]]
                yield
                for i in range(2):
                    both[i] = A(ac.activation, [both[i]] + w_p, p[:, i], bk[i].t[:, :].rearrange("p (k t) -> p k t", k=4),
                                ACT.Copy)
                    bk[i].free(both[i])
                yield
                for i in range(2):
                    m_o = mm(bo.t[base:base + 64, i * P:(i + 1) * P],
                             [(vv[:, kb, kv * 64:(kv + 1) * 64], p[:, i, kb, :]) for kb in range(4)],
                             [both[i], m_v] + w_bo)
                w_p = [m_o]
                yield
            while len(zdone) <= ch:
                next(gates)
            m = V(ve.tensor_tensor, [m_o, zdone[ch]], oT[:, ch, :], zT[:, ch, :], bo.t[:, 0:256], ALU.mult)
            bo.free(m)
            m_oT.append(m)

    bk = banks.bufs
    gates = gate_stream(bk[6])
    streams = [head_stream(range(q, 8, 2), bk[4 + q], bk[2 * q:2 * q + 2]) for q in range(2)]
    for _ in range(4):
        next(streams[0])
    rounds = 0
    while streams:
        for f in list(streams):
            if next(f, 0) == 0:
                streams.remove(f)
        rounds += 1
        if rounds % 4 == 1:
            next(gates, None)
    flat, ml = ring.get(("cout",))
    w = flat.rearrange("p (c n) -> p c n", c=8)
    y = S["hT"][:, 0:2048].rearrange("p (k t) -> p k t", k=8)
    marks = project_norm(nc, S, 256, lambda k, o, waits: mm(o, [(w[:, c, k::8], oT[:, c, :]) for c in range(8)],
                                                            [ml] + m_oT + waits),
                         [(1, gt[:, 1, :])], y, Rot([carve(256) for _ in range(2)]), carve(256))
    ring.release(("cout",), T.last())
    xo = S["hT"][:, 2048:4096].rearrange("p (i d) -> p i d", i=2)
    for i in range(2):
        for k0 in (0, 4):
            b = banks.take()
            for k in range(k0, k0 + 4):
                m = tr(b.t[:, (k - k0) * P:(k - k0 + 1) * P], xT[:, k, 256 + i * P:256 + (i + 1) * P], ident,
                       [marks[k]] + b.w)
            dst = xo[:, i, :].rearrange("p (d k) -> p k d", k=8)[:, k0:k0 + 4, :]
            m = V(ve.tensor_copy, [m], dst, b.t[:, :].rearrange("p (k t) -> p k t", k=4))
            b.free(m)
        S["SP"].wait([m])
        nc.sync.dma_start(S["out"][0, i * P:(i + 1) * P, :], xo[:, i, :]).then_inc(S["s_out"], 16)
    nc.sync.wait_ge(S["s_out"], 32)


def project_norm(nc, S, n, product, parts, y, sq, r_t):
    V, A, T, G, xT = S["V"], S["A"], S["T"], S["G"], S["xT"]
    te, ve, ac, gp = nc.tensor, nc.vector, nc.scalar, nc.gpsimd
    work, tot = Rot(None, S["banks"].bufs[0:7]), S["banks"].bufs[7]
    c0 = 256 * parts[0][0]

    def add(k, t, ms):
        T.wait([ms] + tot.w)
        m = T.done(te.matmul(tot.t[:, 0:n], S["ones"], t.t, start=(k == 0), stop=(k == 7), skip_group_check=True))
        t.free(m)
        return m

    last = None
    for k in range(8):
        b = work.take()
        m = product(k, b.t[:, 0:n], b.w)
        t = sq.take()
        ms = A(ac.activation, [m] + t.w, t.t, b.t[:, 0:n], ACT.Square)
        for q, (_, g) in enumerate(parts):
            seg = slice(q * 256, (q + 1) * 256)
            m = A(ac.activation, [m], y[:, k, seg], b.t[:, seg], ACT.Copy, scale=g[:, k:k + 1])
        b.free(m)
        if last:
            add(*last)
        last = (k, t, ms)
    m_t = add(*last)
    mr = S["rstd"](tot.t[:, 0:n], r_t, D, [m_t])
    tot.free(mr)
    marks = []
    for k in range(8):
        m = V(ve.tensor_tensor, [mr], y[:, k, :], y[:, k, :], r_t, ALU.mult)
        xs = xT[:, k, c0:c0 + n]
        marks.append(G(gp.tensor_tensor, [m], xs, xs, y[:, k, :], ALU.add))
    return marks


_INS = """x c positions w_mod b_mod norm_mix_g norm_ffn_g w_in qn_g kn_g lam_q1 lam_k1 lam_q2 lam_k2 subln_g
w_proj_a w_dw b_dw conv_ln_g conv_ln_b w_proj_b b_proj_b w_proj_c w_out w_router b_router w1 w3 w2 ws1 ws3 ws2
c_2 ctx_2 c_ctx_2 w_mod_2 b_mod_2 g_pre_2 g_post_2 ab_w_in_2 ab_b_gate_2 ab_conv_2 ab_mnorm_2 ab_pool_w_2
ab_pool_scale_2 ab_w_out_2 c_w_in_2 c_sink_2 c_w_out_2""".split()


def kernel(**inputs):
    import concourse.bacc as _bacc
    from concourse.bass_utils import run_bass_kernel_spmd as _run

    nc = _bacc.Bacc("TRN2", target_bir_lowering=False, num_devices=1)
    arrays, aps = {}, {}
    for name in _INS:
        a = np.ascontiguousarray(inputs[name])
        arrays[f"in_{name}"] = a
        aps[name] = nc.dram_tensor(f"in_{name}", a.shape, mybir.dt.from_np(a.dtype), kind="ExternalInput").ap()
    table = make_consts()
    arrays["in_table"] = table
    consts = nc.dram_tensor("in_table", table.shape, F32, kind="ExternalInput").ap()
    out = nc.dram_tensor("out_0", (1, 256, D), F32, kind="ExternalOutput").ap()
    build(nc, aps, consts, out)
    r = _run(nc, [arrays], core_ids=[0])
    return r.results[0]["out_0"]
```
